# Optimizing a Trainium2 kernel written in Bass

```python
import numpy as np
import jax, jax.numpy as jnp
from jax import lax

D_MODEL = 1024
BATCH = 1
SEQ = 512
DEPTH = 1
DEC_BATCH = 8
DEC_SEQ = 4
PAST_LEN = 4096
PAGE_SIZE = 128

ML_HEADS = 4
ML_DQK = 128
ML_DV = 256
ML_CHUNK = 128
GM_GROUPS = 4
GM_DG = 256
GM_CHUNK = 128
MOE_GROUPS = 4
MOE_PER_GROUP = 8
MOE_EXPERTS = MOE_GROUPS * MOE_PER_GROUP
MOE_TOPK = 2
MOE_HIDDEN = 256
EPS = 1e-6
SPLITS = (ML_HEADS * ML_DQK, ML_HEADS * ML_DQK, ML_HEADS * ML_DV, ML_HEADS * ML_DV, ML_HEADS, ML_HEADS, GM_GROUPS * GM_DG, GM_GROUPS * GM_DG, D_MODEL, D_MODEL)
IN_WIDTH = 2 * ML_HEADS * ML_DQK + 2 * ML_HEADS * ML_DV + 2 * ML_HEADS + 2 * GM_GROUPS * GM_DG + 2 * D_MODEL

kernel_name = 'hybrid_mlstm_gmlp_hmoe_step'

def rmsnorm(x, g):
    xf = x.astype(jnp.float32)
    y = xf * lax.rsqrt(jnp.mean(xf * xf, axis=-1, keepdims=True) + EPS)
    return (y * g.astype(jnp.float32)).astype(x.dtype)

def mlstm_chunk(carry, inp):
    c0, n0, m0 = carry
    q, k, v, logi, logf = inp
    L = q.shape[2]
    b = jnp.cumsum(logf, axis=-1)
    causal = jnp.tril(jnp.ones((L, L), dtype=bool))
    d = jnp.where(causal, b[..., :, None] - b[..., None, :] + logi[..., None, :], -jnp.inf)
    inter = b + m0[..., None]
    m = jnp.maximum(inter, jnp.max(d, axis=-1))
    w_intra = jnp.exp(d - m[..., None])
    w_inter = jnp.exp(inter - m)
    s = jnp.einsum('bhtd,bhsd->bhts', q, k) * w_intra
    num = jnp.einsum('bhts,bhsv->bhtv', s, v) + w_inter[..., None] * jnp.einsum('bhvd,bhtd->bhtv', c0, q)
    den = jnp.sum(s, axis=-1) + w_inter * jnp.einsum('bhd,bhtd->bht', n0, q)
    h = num / jnp.maximum(jnp.abs(den), jnp.exp(-m))[..., None]
    b_last = b[..., -1]
    w_end = b_last[..., None] - b + logi
    m_new = jnp.maximum(b_last + m0, jnp.max(w_end, axis=-1))
    decay = jnp.exp(b_last + m0 - m_new)
    w_end = jnp.exp(w_end - m_new[..., None])
    c_new = decay[..., None, None] * c0 + jnp.einsum('bhs,bhsv,bhsd->bhvd', w_end, v, k)
    n_new = decay[..., None] * n0 + jnp.einsum('bhs,bhsd->bhd', w_end, k)
    return (c_new, n_new, m_new), h

def mixer(h, w_in, b_i, b_f, ml_g, gm_g, gm_ws, gm_bs, p_a, p_b, w_out, ml_state, prompt):
    f32 = jnp.float32
    nb, t, _ = h.shape
    z = h @ w_in
    q, k, v, og, ig, fg, u, gv, ga, gb = jnp.split(z, np.cumsum(SPLITS)[:-1].tolist(), axis=-1)

    def heads(a, dh):
        return a.reshape(nb, t, ML_HEADS, dh).transpose(0, 2, 1, 3).astype(f32)
    q = heads(q, ML_DQK) * (ML_DQK ** -0.5)
    k = heads(k, ML_DQK)
    v = heads(v, ML_DV)
    logi = (ig + b_i).astype(f32).transpose(0, 2, 1)
    logf = jax.nn.log_sigmoid((fg + b_f).astype(f32)).transpose(0, 2, 1)
    state0 = (ml_state[0].astype(f32), ml_state[1].astype(f32), ml_state[2].astype(f32))
    if prompt:
        nc = t // ML_CHUNK
        def chunks(a):
            a = a.reshape(a.shape[:2] + (nc, ML_CHUNK) + a.shape[3:])
            return jnp.moveaxis(a, 2, 0)
        state, hs = lax.scan(mlstm_chunk, state0, (chunks(q), chunks(k), chunks(v), chunks(logi), chunks(logf)))
        h_ml = jnp.moveaxis(hs, 0, 2).reshape(nb, ML_HEADS, t, ML_DV)
    else:
        state, h_ml = mlstm_chunk(state0, (q, k, v, logi, logf))
    h_ml = rmsnorm(h_ml, ml_g[:, None, :]).transpose(0, 2, 1, 3).reshape(nb, t, ML_HEADS * ML_DV)
    h_ml = (jax.nn.sigmoid(og.astype(f32)) * h_ml).astype(h.dtype)

    u = jax.nn.gelu(u).reshape(nb, t, GM_GROUPS, GM_DG)
    gv = rmsnorm(jax.nn.gelu(gv).reshape(nb, t, GM_GROUPS, GM_DG), gm_g)
    ws = jnp.where(jnp.tril(jnp.ones((GM_CHUNK, GM_CHUNK), dtype=bool)), gm_ws, 0.0).astype(gv.dtype)
    if prompt:
        nc = t // GM_CHUNK
        mixed = jnp.einsum('gts,bcsgd->bctgd', ws, gv.reshape(nb, nc, GM_CHUNK, GM_GROUPS, GM_DG))
        mixed = (mixed + gm_bs.T[:, :, None]).reshape(nb, t, GM_GROUPS, GM_DG)
        v_rows = None
    else:
        mixed = jnp.einsum('gts,bsgd->btgd', ws[:, :t, :t], gv) + gm_bs[:, :t].T[:, :, None]
        v_rows = gv
    h_gm = (u * mixed).reshape(nb, t, GM_GROUPS * GM_DG)

    merged = jax.nn.sigmoid(ga) * (h_ml @ p_a) + jax.nn.sigmoid(gb) * (h_gm @ p_b)
    return merged @ w_out, state, v_rows

def hier_moe(x, rc_w, rc_b, rf_w, rf_b, e_wg, e_wu, e_wd):
    f32 = jnp.float32
    shape = x.shape
    xt = x.reshape(-1, shape[-1])
    coarse = jax.nn.softmax((xt @ rc_w).astype(f32) + rc_b.astype(f32), axis=-1)
    grp = jnp.argmax(coarse, axis=-1)
    p_grp = jnp.max(coarse, axis=-1)
    fine_all = jnp.einsum('nd,gde->nge', xt, rf_w).astype(f32) + rf_b.astype(f32)
    fine = fine_all[jnp.arange(xt.shape[0]), grp]
    top_v, top_i = lax.top_k(fine, MOE_TOPK)
    gate = jax.nn.softmax(top_v, axis=-1) * p_grp[:, None]
    eid = grp[:, None] * MOE_PER_GROUP + top_i
    combine = jnp.sum(jax.nn.one_hot(eid, MOE_EXPERTS, dtype=f32) * gate[..., None], axis=1)

    def expert(acc, ew):
        wg, wu, wd, c = ew
        hid = jax.nn.silu(xt @ wg) * (xt @ wu)
        return acc + c[:, None] * (hid @ wd).astype(f32), None

    out, _ = lax.scan(expert, jnp.zeros(xt.shape, f32), (e_wg, e_wu, e_wd, combine.T))
    return out.astype(x.dtype).reshape(shape)

def trunk(x, c, n, m, prompt, weights):
    (norm_mix_g, w_in, ml_b_i, ml_b_f, ml_norm_g, gm_norm_g, gm_ws, gm_bs, p_a, p_b, w_out,
     norm_ffn_g, rc_w, rc_b, rf_w, rf_b, e_wg, e_wu, e_wd, final_norm_g) = weights
    cs, ns, ms, vs = [], [], [], []
    for l in range(DEPTH):
        y, st, v_rows = mixer(rmsnorm(x, norm_mix_g[l]), w_in[l], ml_b_i[l], ml_b_f[l], ml_norm_g[l],
                              gm_norm_g[l], gm_ws[l], gm_bs[l], p_a[l], p_b[l], w_out[l],
                              (c[l], n[l], m[l]), prompt)
        x = x + y
        x = x + hier_moe(rmsnorm(x, norm_ffn_g[l]), rc_w[l], rc_b[l], rf_w[l], rf_b[l], e_wg[l], e_wu[l], e_wd[l])
        cs.append(st[0])
        ns.append(st[1])
        ms.append(st[2])
        vs.append(v_rows)
    v_out = None if prompt else jnp.stack(vs)
    return rmsnorm(x, final_norm_g), jnp.stack(cs), jnp.stack(ns), jnp.stack(ms), v_out

def setup_inputs(seed: int = 0) -> dict:
    key = jax.random.key(seed)
    ks = jax.random.split(key, 28)
    f32 = jnp.float32

    def nrm(k, shape, scale):
        return scale * jax.random.normal(k, shape, f32)

    mw = ML_HEADS * ML_DV
    gw = GM_GROUPS * GM_DG
    return {
        'x_prompt': nrm(ks[0], (BATCH, SEQ, D_MODEL), 1.0),
        'x_sample': nrm(ks[1], (DEC_BATCH, DEC_SEQ, D_MODEL), 1.0),
        'state_mlstm_C': nrm(ks[2], (DEPTH, DEC_BATCH, ML_HEADS, ML_DV, ML_DQK), 0.05),
        'state_mlstm_n': nrm(ks[3], (DEPTH, DEC_BATCH, ML_HEADS, ML_DQK), 0.5),
        'state_mlstm_m': nrm(ks[4], (DEPTH, DEC_BATCH, ML_HEADS), 1.0),
        'norm_mix_g': 1.0 + nrm(ks[5], (DEPTH, D_MODEL), 0.02),
        'w_in': nrm(ks[6], (DEPTH, D_MODEL, IN_WIDTH), D_MODEL ** -0.5),
        'ml_b_i': nrm(ks[7], (DEPTH, ML_HEADS), 0.5),
        'ml_b_f': 3.0 + nrm(ks[8], (DEPTH, ML_HEADS), 0.5),
        'ml_norm_g': 1.0 + nrm(ks[9], (DEPTH, ML_HEADS, ML_DV), 0.02),
        'gm_norm_g': 1.0 + nrm(ks[10], (DEPTH, GM_GROUPS, GM_DG), 0.02),
        'gm_ws': nrm(ks[11], (DEPTH, GM_GROUPS, GM_CHUNK, GM_CHUNK), 0.5 * GM_CHUNK ** -0.5),
        'gm_bs': 1.0 + nrm(ks[12], (DEPTH, GM_GROUPS, GM_CHUNK), 0.1),
        'p_a': nrm(ks[13], (DEPTH, mw, D_MODEL), mw ** -0.5),
        'p_b': nrm(ks[14], (DEPTH, gw, D_MODEL), gw ** -0.5),
        'w_out': nrm(ks[15], (DEPTH, D_MODEL, D_MODEL), D_MODEL ** -0.5),
        'norm_ffn_g': 1.0 + nrm(ks[16], (DEPTH, D_MODEL), 0.02),
        'rc_w': nrm(ks[17], (DEPTH, D_MODEL, MOE_GROUPS), D_MODEL ** -0.5),
        'rc_b': nrm(ks[18], (DEPTH, MOE_GROUPS), 0.01),
        'rf_w': nrm(ks[19], (DEPTH, MOE_GROUPS, D_MODEL, MOE_PER_GROUP), D_MODEL ** -0.5),
        'rf_b': nrm(ks[20], (DEPTH, MOE_GROUPS, MOE_PER_GROUP), 0.01),
        'e_wg': nrm(ks[21], (DEPTH, MOE_EXPERTS, D_MODEL, MOE_HIDDEN), D_MODEL ** -0.5),
        'e_wu': nrm(ks[22], (DEPTH, MOE_EXPERTS, D_MODEL, MOE_HIDDEN), D_MODEL ** -0.5),
        'e_wd': nrm(ks[23], (DEPTH, MOE_EXPERTS, MOE_HIDDEN, D_MODEL), MOE_HIDDEN ** -0.5),
        'final_norm_g': 1.0 + nrm(ks[24], (D_MODEL,), 0.02),
    }

def reference(x_prompt, x_sample, state_mlstm_C, state_mlstm_n, state_mlstm_m, norm_mix_g, w_in, ml_b_i,
              ml_b_f, ml_norm_g, gm_norm_g, gm_ws, gm_bs, p_a, p_b, w_out, norm_ffn_g, rc_w, rc_b, rf_w, rf_b,
              e_wg, e_wu, e_wd, final_norm_g):
    weights = (norm_mix_g, w_in, ml_b_i, ml_b_f, ml_norm_g, gm_norm_g, gm_ws, gm_bs, p_a, p_b, w_out,
               norm_ffn_g, rc_w, rc_b, rf_w, rf_b, e_wg, e_wu, e_wd, final_norm_g)
    f32 = jnp.float32
    nbp = x_prompt.shape[0]
    zc = jnp.zeros((DEPTH, nbp, ML_HEADS, ML_DV, ML_DQK), f32)
    zn = jnp.zeros((DEPTH, nbp, ML_HEADS, ML_DQK), f32)
    zm = jnp.zeros((DEPTH, nbp, ML_HEADS), f32)
    y_prompt, c_p, n_p, m_p, _ = trunk(x_prompt, zc, zn, zm, True, weights)
    y_sample, c_s, n_s, m_s, v_s = trunk(x_sample, state_mlstm_C, state_mlstm_n, state_mlstm_m, False, weights)
    return (y_prompt, y_sample, c_p, n_p, m_p, c_s, n_s, m_s, v_s)


_drawn_inputs = setup_inputs


def setup_inputs(seed=0):
    import zlib

    import numpy as np

    out = dict(_drawn_inputs(seed))
    spreads = {}
    factors = {'ml_norm_g': 9.662,
     'gm_norm_g': 8.609,
     'rc_b': 5.517,
     'rf_b': 4.31,
     'final_norm_g': 8.109,
     'norm_ffn_g': 2.756}
    for name, (base, spread) in spreads.items():
        noise = np.random.default_rng([zlib.crc32(name.encode()), seed]).standard_normal(out[name].shape)
        drawn = base * np.exp(spread * noise) if base else spread * noise
        out[name] = __import__('jax').numpy.asarray(drawn.astype(out[name].dtype))
    for name, factor in factors.items():
        out[name] = (out[name] * factor).astype(out[name].dtype)
    return out
```

```python
from contextlib import ExitStack

import numpy as np

import concourse.bass as bass
from concourse import mybir

ALU = mybir.AluOpType
ACT = mybir.ActivationFunctionType
F32 = mybir.dt.float32
F32R = mybir.dt.float32r
I32 = mybir.dt.int32
U32 = mybir.dt.uint32
AX = mybir.AxisListType.X

D = 1024
NP_TOK, NB, NL = 512, 8, 4
NS = NB * NL
T = NS + NP_TOK
HALF = T // 2
NCH = NP_TOK // 128
H, DQK, DV = 4, 128, 256
KC = D // 128
NE, NG, NPG, EH = 32, 4, 8, 256
EPS = 1e-6
CAP = 64
MAXK = T // CAP
NOV = (2 * T) // CAP
NBLK = NE + NOV
BIG = 1.0e30
COL = {"q": 0, "k": 512, "v": 1024, "og": 2048, "gates": 3072, "u": 3080, "gv": 4104, "ga": 5128, "gb": 6152}
NTILE = NCH + 1


UE = 2048
NU = 3 * NE
PAIRS = (NE - 2) // 2


def tok_cols(t):
    return NS + 128 * t if t < NCH else 0


def rows(t):
    return 128 if t < NCH else NS


BLOCKS = ([("q", j) for j in range(4)] + [("k", j) for j in range(4)] + [("gates", 0)]
          + [("v", j) for j in range(8)] + [("gv", j) for j in range(8)] + [("u", j) for j in range(8)]
          + [b for j in range(8) for b in (("gb", j), ("pb", j))] + [("og", j) for j in range(8)]
          + [b for j in range(8) for b in (("ga", j), ("pa", j))]
          + [("wo", i) for i in range(16)])
NBK = len(BLOCKS)
AT = {b: i for i, b in enumerate(BLOCKS)}
BY_ACT = ("q", "k", "v", "gv", "u", "gb", "og", "ga", "gates")
WO0 = AT[("wo", 0)]

SIDE = {i: [] for i in range(NBK)}


def _place_side_steps():
    for j in range(4):
        SIDE[AT[("k", j)] + 1].append(("tr", "k", j))
    SIDE[AT[("gates", 0)] + 1].append(("rows", 0, 0))
    for j in range(8):
        SIDE[AT[("v", j)] + 1].append(("tr", "v", j))
        SIDE[AT[("gv", j)] + 1].append(("tr", "gv", j))
        SIDE[AT[("gv", 7)] + 1 + j // 2].append(("mix", j, 0))
    SIDE[AT[("v", 7)] + 1].append(("s_pre", 0, 0))
    pieces = list(range(17))
    for i in range(6):
        SIDE[AT[("gv", 0)] + 2 + i].append(("s_c", pieces.pop(0), 0))
    for i in range(8):
        SIDE[AT[("u", 0)] + i].append(("s_c", pieces.pop(0), 0))
        if i >= 5:
            SIDE[AT[("u", 0)] + i].append(("s_c", pieces.pop(0), 0))
    assert not pieces
    k = AT[("gb", 0)]
    SIDE[k] += [("s_den", 0, 0), ("s_ss", 0, 0)]
    for c in range(NCH):
        for stage in ("ml1", "ml2", "ml3"):
            k += 1
            SIDE[k].append((stage, c, 0))
    for i in range(2):
        k += 1
        SIDE[k].append(("c_out", i, 0))
    assert k < AT[("og", 0)]


_place_side_steps()
STEPS = [s for i in range(NBK) for s in SIDE[i]]
SN = {s: n for n, s in enumerate(STEPS)}


def hands(step):
    kind, what, j = step
    if kind == "tr":
        return (1, 1) if what == "gv" and j % 2 else (0, 0)
    return {"rows": (3, 1), "mix": (0, 0), "s_pre": (2, 1), "s_c": (1, 0), "s_den": (1, 0), "s_ss": (0, 0),
            "ml1": (2, 1), "ml2": (1, 0), "ml3": (0, 0), "c_out": (0, 0)}[kind]


def evacs(kind, j):
    if kind == "pa" and j == 7:
        return 8, 3
    if kind == "wo":
        return 0, NTILE if j % 8 == 7 else 0
    return {"q": (1, 0), "k": (1, 0), "v": (1, 0), "gv": (1, 0), "gates": (1, 0), "u": (2, 2), "og": (2, 2),
            "gb": (1, 1), "ga": (1, 1), "pb": (0, 1), "pa": (0, 2)}[kind]


HA, HD, _a, _d = {}, {}, 0, 0
for _s in STEPS:
    HA[_s], HD[_s] = _a, _d
    _a, _d = _a + hands(_s)[0], _d + hands(_s)[1]
EA, ED, _a, _d = [], [], 0, 0
for _b in BLOCKS:
    EA.append(_a)
    ED.append(_d)
    _a, _d = _a + evacs(*_b)[0], _d + evacs(*_b)[1]
EA.append(_a)
ED.append(_d)


ROOTS = [s for s in STEPS if s[0] in ("s_ss", "ml3") or (s[0] == "tr" and hands(s)[0])]
RN = {s: NTILE + n for n, s in enumerate(ROOTS)}


def build(nc, x_prompt, x_sample, state_C, state_n, state_m, norm_mix_g, w_in, ml_b_i, ml_b_f, ml_norm_g,
          gm_norm_g, gm_ws, gm_bs, p_a, p_b, w_out, norm_ffn_g, rc_w, rc_b, rf_w, rf_b, e_wg, e_wu, e_wd,
          final_norm_g, y_p, y_s, C_p, n_p, m_p, C_s, n_s, m_s, v_s):
    place = {}
    cur = [(nc.sbuf_base + 63) // 64 * 64]

    def at(name, shape, dt, offset):
        return nc.alloc_sbuf_tensor_at(name, shape, dt, offset=offset)[:]

    def take(name, shape, dt=F32):
        place[name] = cur[0]
        cur[0] += (4 * int(np.prod(shape[1:])) + 31) // 32 * 32
        return at(name, shape, dt, place[name])

    ident = take("ident", [128, 128])
    ones = take("ones", [128, 128])
    epsc = take("epsc", [128, 1])
    stat = take("stat", [128, 24])
    xtok = take("xtok", [128, NTILE, D])
    mixer0 = cur[0]
    tri = take("tri", [128, 128])
    btri = take("btri", [NS, NS])
    selb = take("selb", [NS, NB])
    selh = take("selh", [H, H, 128])
    mlg = take("mlg", [128, H, 2])
    gbias = take("gbias", [H, 2])
    CT = take("CT", [128, H, DV])
    nT = take("nT", [128, H])
    wsT = take("wsT", [128, NG, 128])
    wsS = take("wsS", [NS, NG, NS])
    gst = take("gst", [128, NTILE])
    sm = take("sm", [128, 160])
    m0s = take("m0s", [H, NB])
    n0s = take("n0s", [NB, H * DQK])
    Xh = take("Xh", [128, KC, T], F32R)
    Xl = take("Xl", [128, KC, T], F32R)
    Hh = take("Hh", [128, KC, T], F32R)
    Hl = take("Hl", [128, KC, T], F32R)
    wraw = take("wraw", [128, 3, KC * 128])
    wh = take("wh", [128, 2, KC * 128], F32R)
    wl = take("wl", [128, 2, KC * 128], F32R)
    ev = take("ev", [128, 2, T])
    rws = take("rws", [H, 5, T])
    E = take("E", [128, 8, 512])
    qT = take("qT", [128, H, T])
    kT = take("kT", [128, H, T])
    ktok = take("ktok", [128, NTILE, 512])
    vtok = take("vtok", [128, NTILE, D])
    assert cur[0] <= nc.sbuf_usable_end, (cur[0], nc.sbuf_usable_end)
    sumT = at("sumT", [128, KC, T], F32, place["xtok"])
    xres = at("xres", [128, NTILE, D], F32, place["qT"])
    mixT = at("mixT", [128, KC, T], F32, place["Hl"])
    junk = at("junk", [128, D], F32, place["Hl"])
    gB = at("gB", [128, D], F32, place["Hl"] + 4 * D)
    gmB = at("gmB", [128, D], F32, place["Hh"] + 6 * 4 * T)
    bsB = at("bsB", [128, NG, 128], F32, place["Hh"] + 5 * 4 * T)
    gjunk = at("gjunk", [128, 256], F32, place["Hh"] + 4 * 4 * T)
    wsraw = at("wsraw", [128, NG, 128], F32, place["Hh"])

    xn_dram = nc.dram_tensor("xn_rows", (T, D), F32).ap()
    slot_dram = nc.dram_tensor("slot_rows", (NBLK * CAP, D), F32).ap()
    zone = {"A": [mixer0, place["Xh"]], "C": [place["Hh"], place["wraw"]], "B": [place["Xh"], place["Hh"]],
            "D": [place["wraw"], place["ev"]], "F": [place["ev"], place["qT"]],
            "G": [place["qT"] + 4 * NTILE * D, place["vtok"]], "I": [place["vtok"], cur[0]]}

    def put(zone_name, name, shape, dt=F32):
        z = zone[zone_name]
        o = (z[0] + 31) // 32 * 32
        z[0] = o + 4 * int(np.prod(shape[1:]))
        assert z[0] <= z[1], (name, zone_name)
        return at(name, shape, dt, o)

    eraw = [put("C", f"eraw{i}", [128, UE]) for i in range(4)] + [put("I", f"eraw{4 + i}", [128, UE]) for i in range(2)]
    xn = at("xn", [128, NTILE, D], F32, place["xtok"])
    yg = at("yg", [128, 2 * NTILE, D], F32, place["Xh"])
    sq = put("D", "sq", [128, D])
    xnT = [put("D", f"xnT{i}", [128, KC, 128]) for i in range(2)]
    xT = [put("F", f"xT{i}", [128, KC, CAP]) for i in range(2)]
    xg = [put("F", f"xg{i}", [CAP, D]) for i in range(2)]
    gffn = put("F", "gffn", [128, D])
    yout = [put("F", f"yout{i}", [CAP, D]) for i in range(2)]
    sil = [put("A", f"sil{i}", [128, 2 * CAP]) for i in range(2)]
    hT = [put("A", f"hT{i}", [128, 2, CAP]) for i in range(2)]
    gfin = put("G", "gfin", [128, D])
    rw = put("G", "rw", [128, KC, NG + NE])
    rb = put("G", "rb", [128, NG + NE])
    io64 = put("G", "io64", [128, CAP])
    w8 = put("G", "w8", [128, NPG])
    tok1 = put("G", "tok1", [128, NTILE])
    ctl = put("G", "ctl", [1, 32], I32)
    octl = put("G", "octl", [1, 1], I32)
    idx1 = [put("G", f"idx1_{i}", [CAP, 1], I32) for i in range(3)]
    idx = put("G", "idx", [CAP, NBLK], I32)
    slots = put("G", "slots", [128, 2 * NTILE], I32)
    GT = put("G", "GT", [128, 2, NTILE])
    nst = put("G", "nst", [128, 2, NTILE])
    triS = put("A", "triS", [128, 128])
    OH = put("A", "OH", [128, 2, NTILE, NE])
    RK = put("A", "RK", [128, NTILE + 1, NE])
    Lg = put("B", "Lg", [128, NTILE, NG + NE])
    W1 = put("B", "W1", [128, NTILE, NE])
    CW = put("B", "CW", [128, NCH, NE])
    OT = put("B", "OT", [128, 2, NTILE, NE])
    F4 = put("B", "F4", [128, NTILE, NG, NPG])
    rt = put("B", "rt", [128, 512])
    Aoh = put("B", "Aoh", [128, 2 * NTILE, CAP])
    Boh = put("B", "Boh", [128, 2 * NTILE, NBLK])
    VI = put("B", "VI", [CAP, NBLK])
    CO = put("B", "CO", [1, NOV, NE])

    ctx = ExitStack()
    with ctx:
        Z = ctx.enter_context(nc.psum_tensor("Z", [128, 2, 2, 512], F32))[:]
        M = ctx.enter_context(nc.psum_tensor("M", [128, 4, 512], F32))[:]

        def sem(name):
            return ctx.enter_context(nc.semaphore(name))

        x_in = sem("x_in")
        misc_in = sem("misc_in")
        consts = sem("consts")
        pool_step = sem("pool_step")
        g_in = sem("g_in")
        x_ss = sem("x_ss")
        x_sc = sem("x_sc")
        x_tr = sem("x_tr")
        x_hi = sem("x_hi")
        x_lo = sem("x_lo")
        raw_in = [sem(f"raw_in{i}") for i in range(3)]
        w_hi = sem("w_hi")
        w_lo = sem("w_lo")
        z_done = sem("z_done")
        ev_act = sem("ev_act")
        ev_dve = sem("ev_dve")
        side_mm = sem("side_mm")
        side_act = sem("side_act")
        side_dve = sem("side_dve")
        side_end = sem("side_end")
        a_step = sem("a_step")
        v_step = sem("v_step")
        c_in = [sem(f"c_in{i}") for i in range(3)]
        c_st = [sem(f"c_st{i}") for i in range(3)]
        c_free = sem("c_free")
        out_st = sem("out_st")
        root_in = sem("root_in")
        root_out = sem("root_out")
        xr_in = sem("xr_in")
        moe_consts = sem("moe_consts")
        zeroed = sem("zeroed")
        moe_made = sem("moe_made")
        n_ss = sem("n_ss")
        n_mean = sem("n_mean")
        n_root = sem("n_root")
        n_xn = sem("n_xn")
        n_tr = sem("n_tr")
        n_ev = sem("n_ev")
        n_log = sem("n_log")
        xn_st = sem("xn_st")
        r_exp_in = sem("r_exp_in")
        r_exp_out = sem("r_exp_out")
        r_oh = sem("r_oh")
        r_rank = sem("r_rank")
        r_ab = sem("r_ab")
        r_idx = sem("r_idx")
        routed = sem("routed")
        wg_in = [sem(f"wg_in{i}") for i in range(2)]
        wu_in = [sem(f"wu_in{i}") for i in range(2)]
        wd_in = [sem(f"wd_in{i}") for i in range(2)]
        rows_in = [sem(f"rows_in{i}") for i in range(2)]
        xt_done = sem("xt_done")
        xt_ready = sem("xt_ready")
        up_done = sem("up_done")
        sil_ready = sem("sil_ready")
        h_ready = sem("h_ready")
        down_done = sem("down_done")
        y_copied = sem("y_copied")
        y_st = [sem(f"y_st{i}") for i in range(2)]
        o_w = sem("o_w")
        o_rows = sem("o_rows")
        o_st = sem("o_st")
        idx_step = sem("idx_step")
        moe_over = sem("moe_over")
        yg_in = [sem(f"yg_in{i}") for i in range(NTILE)]
        f_sum = sem("f_sum")
        f_ss = sem("f_ss")
        f_mean = sem("f_mean")
        f_root = sem("f_root")
        f_out = sem("f_out")
        out_y = sem("out_y")

        N_MOE = 1 + NG + 4
        N_MISC = 7 + NB * NG + 1

        def cpiece(ap, i):
            h, vh, bh = i // 4, i // 2 % 2, i % 2
            return ap[0, 4 * bh:4 * bh + 4, h, 128 * vh:128 * vh + 128, :].rearrange("b v d -> v b d")

        CIN = [E[:, 3, :], E[:, 4, :], E[:, 6, :]]
        CTS = [E[:, 7, :], E[:, 2, :]]
        KWM = E[0:NS, 1, :]
        KWS = E[0:NS, 5, :]

        def zz(t):
            return Z[:, t % 2, :, 0:HALF]

        def two(ap):
            return ap.rearrange("p (a b) -> p a b", a=2)

        def weight_src(i):
            kind, j = BLOCKS[i]
            if kind == "wo":
                half, q = j // 8, j % 8
                return w_out[0, 128 * q:128 * q + 128, 512 * half:512 * half + 512]
            if kind in ("pa", "pb"):
                w = p_a if kind == "pa" else p_b
                return w[0].rearrange("(c p) n -> p c n", p=128)[:, :, 128 * j:128 * j + 128]
            c0 = COL[kind] + 128 * j
            return w_in[0].rearrange("(c p) n -> p c n", p=128)[:, :, c0:c0 + 128]

        def bank_up(k):
            return Z[:, k, 0, 0:4 * CAP]

        def bank_xt():
            return Z[:, 0, 1, :]

        def bank_out(k):
            return M[0:CAP, 2 * k:2 * k + 2, :]

        def each_block(eng, body):
            for b in (0, 1):
                body(b, b)
            with eng.Fori(1, NE // 2 - 1) as i:
                for k in range(2):
                    body(i * 2 + k, k)
            for b in (NE - 2, NE - 1):
                body(b, b % 2)

        def one(ap, e):
            return ap[e] if isinstance(e, int) else ap[bass.ds(e, 1)].rearrange("o a b -> (o a) b")

        def up_rows(w, e):
            return one(w[0], e).rearrange("(p c) n -> p (c n)", c=KC)

        def down_rows(w, e):
            return one(w[0], e).rearrange("(j p) n -> p j n", p=128)

        def slot_rows(b):
            return slot_dram[bass.ds(b * CAP, CAP), :]

        def wsize(i):
            return 512 if BLOCKS[i][0] == "wo" else KC * 128

        block = ctx.enter_context(nc.Block())

        @block.sync
        def _(sp):
            sp.dma_start(xtok[:, 0:NCH, :], x_prompt[0].rearrange("(t p) d -> p t d", p=128)).then_inc(x_in, 16)
            sp.dma_start(xtok[0:NS, NCH, :], x_sample.rearrange("b t d -> (b t) d")).then_inc(x_in, 16)
            for i in range(NBK):
                if i >= 3:
                    sp.wait_ge(w_lo, i - 2)
                n = wsize(i)
                dst = wraw[:, i % 3, 0:n]
                if n != 512:
                    dst = dst.rearrange("p (c n) -> p c n", c=KC)
                sp.dma_start(dst, weight_src(i)).then_inc(raw_in[i % 3], 16)
            sp.wait_ge(z_done, AT[("pa", 7)] + 1)
            sp.wait_ge(ev_dve, ED[AT[("og", 7)] + 1])
            sp.wait_ge(side_end, len(STEPS))
            def load_expert(b, k):
                if not (isinstance(b, int) and b < 2):
                    sp.wait_ge(up_done, b - 1)
                sp.dma_start(eraw[3 * k], up_rows(e_wg, b)).then_inc(wg_in[k], 16)
                sp.dma_start(eraw[3 * k + 1], up_rows(e_wu, b)).then_inc(wu_in[k], 16)
                if not (isinstance(b, int) and b < 2):
                    sp.wait_ge(down_done, b - 1)
                sp.dma_start(eraw[3 * k + 2].rearrange("p (j n) -> p j n", j=2), down_rows(e_wd, b)) \
                    .then_inc(wd_in[k], 16)

            each_block(sp, load_expert)
            sp.wait_ge(routed, 1)
            sp.wait_ge(down_done, NE)
            n_ov = sp.value_load(ctl[0:1, NOV:NOV + 1], min_val=0, max_val=NOV)
            with sp.If(n_ov > 0):
                with sp.Fori(0, n_ov) as o:
                    e = sp.value_load(ctl[0:1, bass.ds(o, 1)], min_val=0, max_val=NE - 1)
                    sp.wait_ge(down_done, o + NE)
                    sp.dma_start(eraw[0], up_rows(e_wg, e)).then_inc(o_w, 16)
                    sp.dma_start(eraw[1], up_rows(e_wu, e)).then_inc(o_w, 16)
                    sp.dma_start(eraw[2].rearrange("p (j n) -> p j n", j=2), down_rows(e_wd, e)).then_inc(o_w, 16)
            for t in range(NTILE):
                sp.wait_ge(f_out, t + 1)
                dst = y_p[0, 128 * t:128 * t + 128, :] if t < NCH else y_s.rearrange("b t d -> (b t) d")
                sp.dma_start(dst, yg[0:rows(t), t, :]).then_inc(out_y, 16)
            sp.wait_ge(out_y, 16 * NTILE)

        @block.gpsimd
        def _(pool):
            n = [0]

            def step(ins):
                ins.then_inc(pool_step, 1)
                n[0] += 1
                pool.wait_ge(pool_step, n[0])

            pool.dma_start(gB, norm_mix_g[0:1, :].partition_broadcast(128)).then_inc(g_in, 16)
            step(nc.gpsimd.memset(ident, 0.0))
            step(nc.gpsimd.affine_select(out=ident, in_=ident, compare_op=ALU.not_equal, fill=1.0, base=0,
                                         pattern=[[-1, 128]], channel_multiplier=1))
            step(nc.gpsimd.memset(ones, 1.0))
            step(nc.gpsimd.affine_select(out=tri, in_=ones, compare_op=ALU.is_ge, fill=0.0, base=0,
                                         pattern=[[1, 128]], channel_multiplier=-1))
            step(nc.gpsimd.affine_select(out=selb, in_=ones[0:NS, 0:NB], compare_op=ALU.is_ge, fill=0.0, base=0,
                                         pattern=[[-NL, NB]], channel_multiplier=1))
            step(nc.gpsimd.affine_select(out=selb, in_=selb, compare_op=ALU.is_ge, fill=0.0, base=NL - 1,
                                         pattern=[[NL, NB]], channel_multiplier=-1))
            bt = btri.rearrange("p (b t) -> p b t", t=NL)
            step(nc.gpsimd.affine_select(out=bt, in_=ones[0:NS, 0:NS].rearrange("p (b t) -> p b t", t=NL),
                                         compare_op=ALU.is_ge, fill=0.0, base=0,
                                         pattern=[[-NL, NB], [0, NL]], channel_multiplier=1))
            step(nc.gpsimd.affine_select(out=btri, in_=btri, compare_op=ALU.is_ge, fill=0.0, base=0,
                                         pattern=[[1, NS]], channel_multiplier=-1))
            step(nc.gpsimd.memset(selh, 1.0))
            step(nc.gpsimd.affine_select(out=selh, in_=selh, compare_op=ALU.is_equal, fill=0.0, base=0,
                                         pattern=[[-1, H], [0, 128]], channel_multiplier=1))
            step(nc.gpsimd.memset(epsc, EPS))
            step(nc.gpsimd.memset(gst, 1.0))
            step(nc.gpsimd.memset(CT, 0.0))
            step(nc.gpsimd.memset(nT, 0.0))
            step(nc.gpsimd.memset(sm, 0.0))
            nc.gpsimd.memset(wsS, 0.0).then_inc(consts, 1)
            pool.wait_ge(consts, 1)
            pool.dma_start(wsraw, gm_ws[0].rearrange("g t s -> t g s")).then_inc(misc_in, 16)
            pool.dma_start(gmB, gm_norm_g.rearrange("o g d -> o (g d)").partition_broadcast(128)).then_inc(misc_in, 16)
            pool.dma_start(bsB.rearrange("p g t -> p (g t)"),
                           gm_bs.rearrange("o g t -> o (g t)").partition_broadcast(128)).then_inc(misc_in, 16)
            pool.dma_start(gbias[:, 0:1], ml_b_i.rearrange("o h -> h o")).then_inc(misc_in, 16)
            pool.dma_start(gbias[:, 1:2], ml_b_f.rearrange("o h -> h o")).then_inc(misc_in, 16)
            pool.dma_start(m0s, state_m[0].rearrange("b h -> h b"), allow_slow_non_contiguous=True).then_inc(misc_in, 16)
            pool.dma_start(n0s, state_n[0].rearrange("b h d -> b (h d)")).then_inc(misc_in, 16)
            for b in range(NB):
                for g in range(NG):
                    pool.dma_start(wsS[NL * b:NL * b + NL, g, NL * b:NL * b + NL],
                                   gm_ws[0, g, 0:NL, 0:NL].rearrange("t s -> s t"),
                                   allow_slow_non_contiguous=True).then_inc(misc_in, 16)
            pool.dma_start(mlg, ml_norm_g[0].rearrange("h (v p) -> p h v", p=128),
                           allow_slow_non_contiguous=True).then_inc(misc_in, 16)
            def c_load(i):
                pool.dma_start(CIN[i % 3].rearrange("v (b d) -> v b d", b=4), cpiece(state_C, i)) \
                    .then_inc(c_in[i % 3], 16)

            def c_store(i):
                pool.dma_start(cpiece(C_s, i), CIN[i % 3].rearrange("v (b d) -> v b d", b=4)) \
                    .then_inc(c_st[i % 3], 16)

            def c_out_pieces():
                for h in range(H):
                    pool.dma_start(C_p[0, 0, h].rearrange("(v p) d -> p v d", p=128),
                                   E[:, h // 2, 256 * (h % 2):256 * (h % 2) + 256]
                                   .rearrange("p (v d) -> p v d", v=2)).then_inc(out_st, 16)
                pool.dma_start(n_p[0, 0], E[0:H, 2, 0:128]).then_inc(out_st, 16)

            for s in STEPS:
                over = SN[s] + 1
                kind, what, j = s
                if kind == "s_c":
                    k = what
                    pool.wait_ge(side_end, SN[s])
                    if k >= 2:
                        c_store(k - 2)
                    if 2 <= k < 15:
                        pool.wait_ge(c_st[(k - 2) % 3], 16 * ((k - 2) // 3 + 1))
                    if k < 15:
                        c_load(k + 1)
                    if k == 16:
                        pool.wait_ge(side_end, over)
                        c_store(15)
                        for i in range(3):
                            pool.wait_ge(c_st[i], 16 * (6 if i == 0 else 5))
                        nc.gpsimd.memset(sm[0:1, 60:61], 0.0).then_inc(c_free, 1)
                elif s in RN:
                    if kind == "tr" and j == 7:
                        pool.wait_ge(side_end, over)
                        pool.dma_start(v_s[0].rearrange("b t g d -> (b t) (g d)"), xtok[0:NS, NCH, :]) \
                            .then_inc(out_st, 16)
                elif kind == "rows":
                    pool.wait_ge(side_end, over)
                    pool.dma_start(m_s[0].rearrange("b h -> h b"), rws[:, 3, NL - 1:NS:NL],
                                   allow_slow_non_contiguous=True).then_inc(out_st, 16)
                    pool.dma_start(m_p.rearrange("o b h -> h (o b)"), rws[:, 3, T - 1:T]).then_inc(out_st, 16)
                elif kind == "s_pre":
                    pool.wait_ge(side_end, over)
                    c_load(0)
                elif kind == "s_den":
                    pool.wait_ge(side_end, over)
                    pool.dma_start(n_s[0].rearrange("b h d -> b (h d)"), n0s).then_inc(out_st, 16)
                elif kind == "c_out" and what == 1:
                    pool.wait_ge(side_end, over)
                    c_out_pieces()
            pool.dma_start(xres[:, 0:NCH, :], x_prompt[0].rearrange("(t p) d -> p t d", p=128)).then_inc(xr_in, 16)
            pool.dma_start(xres[0:NS, NCH, :], x_sample.rearrange("b t d -> (b t) d")).then_inc(xr_in, 16)
            pool.wait_ge(out_st, 16 * 9)
            pool.wait_ge(side_end, len(STEPS))
            pool.dma_start(rw[:, :, 0:NG], rc_w[0].rearrange("(c p) n -> p c n", p=128),
                           allow_slow_non_contiguous=True).then_inc(moe_consts, 16)
            for g in range(NG):
                pool.dma_start(rw[:, :, NG + NPG * g:NG + NPG * g + NPG],
                               rf_w[0, g].rearrange("(c p) n -> p c n", p=128)).then_inc(moe_consts, 16)
            pool.dma_start(rb[:, 0:NG], rc_b.partition_broadcast(128)).then_inc(moe_consts, 16)
            pool.dma_start(rb[:, NG:NG + NE], rf_b.rearrange("o g n -> o (g n)").partition_broadcast(128)) \
                .then_inc(moe_consts, 16)
            pool.dma_start(gfin, final_norm_g.rearrange("(o d) -> o d", o=1).partition_broadcast(128)) \
                .then_inc(moe_consts, 16)
            nc.gpsimd.iota(io64, pattern=[[1, CAP]], base=0, channel_multiplier=0, allow_small_or_imprecise_dtypes=True)
            nc.gpsimd.iota(w8, pattern=[[-1, NPG]], base=NPG, channel_multiplier=0, allow_small_or_imprecise_dtypes=True)
            nc.gpsimd.iota(tok1, pattern=[[128, NTILE]], base=1, channel_multiplier=1,
                           allow_small_or_imprecise_dtypes=True)
            pool.wait_ge(z_done, AT[("pa", 7)] + 1)
            pool.wait_ge(ev_act, EA[WO0])
            pool.wait_ge(ev_dve, ED[WO0])
            pool.dma_start(gffn, norm_ffn_g.partition_broadcast(128)).then_inc(moe_consts, 16)
            for k in range(2):
                nc.gpsimd.memset(xg[k], 0.0)
            nc.gpsimd.memset(nst, 1.0)
            nc.gpsimd.affine_select(out=triS, in_=ones, compare_op=ALU.is_gt, fill=0.0, base=0,
                                    pattern=[[1, 128]], channel_multiplier=-1).then_inc(moe_made, 1)
            pool.wait_ge(moe_made, 1)
            pool.dma_start(slot_dram[NE * CAP:NBLK * CAP, :].rearrange("(b q) d -> q b d", q=CAP),
                           xg[0].unsqueeze(1).broadcast_to([CAP, NOV, D])).then_inc(zeroed, 16)
            for t in range(NTILE):
                pool.wait_ge(n_xn, t + 1)
                pool.dma_start(xn_dram[128 * t:128 * t + rows(t), :], xn[0:rows(t), t, :]).then_inc(xn_st, 16)
            pool.wait_ge(xn_st, 16 * NTILE)
            pool.wait_ge(zeroed, 16)
            pool.wait_ge(routed, 1)

            def gather(b, k):
                if not (isinstance(b, int) and b < 2):
                    pool.wait_ge(xt_done, b - 1)
                step_r(nc.gpsimd.tensor_copy(idx1[k], idx[:, bass.ds(b, 1)]), b + 1)
                nc.gpsimd.indirect_dma_start(xg[k], None, xn_dram, bass.IndirectOffsetOnAxis(idx1[k], 0),
                                             bounds_check=T - 1, oob_is_err=False).then_inc(rows_in[k], 16)

            def step_r(ins, count):
                ins.then_inc(idx_step, 1)
                pool.wait_ge(idx_step, count)
                nc.gpsimd.tensor_tensor(stat[0:1, 23:24], ones[0:1, 0:1], ones[0:1, 0:1], ALU.mult)

            each_block(pool, gather)
            n_ov = pool.value_load(ctl[0:1, NOV:NOV + 1], min_val=0, max_val=NOV)
            pool.wait_ge(xt_done, NE)
            with pool.If(n_ov > 0):
                with pool.Fori(0, n_ov) as o:
                    pool.wait_ge(xt_done, o + NE)
                    step_r(nc.gpsimd.tensor_copy(idx1[2], idx[:, bass.ds(o + NE, 1)]), o + (NE + 1))
                    nc.gpsimd.indirect_dma_start(xg[0], None, xn_dram, bass.IndirectOffsetOnAxis(idx1[2], 0),
                                                 bounds_check=T - 1, oob_is_err=False).then_inc(o_rows, 16)
            pool.wait_ge(moe_over, 1)
            for t in range(NTILE):
                for j in range(2):
                    g = NTILE * j + t
                    nc.gpsimd.indirect_dma_start(yg[0:rows(t), g, :], None, slot_dram,
                                                 bass.IndirectOffsetOnAxis(slots[0:rows(t), g:g + 1], 0)) \
                        .then_inc(yg_in[t], 16)
            pool.wait_ge(moe_consts, 16 * N_MOE)

        def transpose(out, in_, k):
            return nc.tensor.transpose(out, in_, ident[0:k, 0:k])

        @block.tensor
        def _(pe):
            pe.wait_ge(consts, 1)
            def xbank(c):
                return Z[:, c % 6 // 2, c % 2, :] if c % 6 < 4 else M[:, c % 6 - 4, :]

            pe.wait_ge(x_sc, NTILE)
            for c in range(KC):
                if c >= 6:
                    pe.wait_ge(x_lo, c - 5)
                for t in range(NCH):
                    transpose(xbank(c)[:, 128 * t:128 * t + 128], xtok[:, t, 128 * c:128 * c + 128], 128)
                transpose(M[:, 2, NS * c:NS * c + NS], xtok[0:NS, NCH, 128 * c:128 * c + 128], NS).then_inc(x_tr, 1)
            pe.wait_ge(misc_in, 16 * N_MISC)
            for g in range(NG):
                last = transpose(M[:, 3, 128 * g:128 * g + 128], wsraw[:, g, :], 128)
            last.then_inc(x_tr, 1)
            pe.wait_ge(x_lo, KC + 2)

            def multiply(i):
                kind = BLOCKS[i][0]
                ah, al = (Hh, Hl) if kind in ("pa", "pb") else (Xh, Xl)
                if kind == "pb":
                    pe.wait_ge(ev_dve, ED[AT[("u", 7)] + 1])
                if kind == "pa":
                    pe.wait_ge(ev_dve, ED[AT[("og", 7)] + 1])
                hi = wh[:, i % 2, :].rearrange("p (c n) -> p c n", c=KC)
                lo = wl[:, i % 2, :].rearrange("p (c n) -> p c n", c=KC)
                for c in range(KC):
                    for f in range(2):
                        cols = slice(HALF * f, HALF * f + HALF)
                        z = zz(i)[:, f, :]
                        nc.tensor.matmul(z, hi[:, c, :], ah[:, c, cols], start=c == 0, stop=False)
                        nc.tensor.matmul(z, hi[:, c, :], al[:, c, cols], start=False, stop=False)
                    for f in range(2):
                        cols = slice(HALF * f, HALF * f + HALF)
                        last = nc.tensor.matmul(zz(i)[:, f, :], lo[:, c, :], ah[:, c, cols], start=False,
                                                stop=c == KC - 1)
                last.then_inc(z_done, 1)

            def multiply_out(i):
                half, q = BLOCKS[i][1] // 8, BLOCKS[i][1] % 8
                if i == WO0:
                    pe.wait_ge(ev_dve, ED[WO0])
                for t in range(NTILE):
                    g = NTILE * half + t
                    bank = (Z[:, g % 8 // 2, g % 2, :] if g % 8 < 4 else M[:, g % 8 - 4, :])
                    if q == 0 and g >= 8:
                        pe.wait_ge(ev_dve, ED[WO0 + 7] + 1 + g - 8)
                    cols = slice(tok_cols(t), tok_cols(t) + 128)
                    nc.tensor.matmul(bank, Xh[:, q, cols], wh[:, i % 2, 0:512], start=q == 0, stop=False)
                    nc.tensor.matmul(bank, Xl[:, q, cols], wh[:, i % 2, 0:512], start=False, stop=False)
                    last = nc.tensor.matmul(bank, Xh[:, q, cols], wl[:, i % 2, 0:512], start=False, stop=q == 7)
                last.then_inc(z_done, 1)

            def rows_of(bank, lhs, rhs, n):
                for h in range(H):
                    nc.tensor.matmul(bank[:, n * h:n * h + n], lhs(h), rhs(h), start=True, stop=True)

            def side(step):
                kind, what, j = step
                n = SN[step]
                if n:
                    pe.wait_ge(side_end, n)
                if kind == "tr":
                    pe.wait_ge(ev_act, EA[AT[(what, j)]] + 1)
                    src = kT[:, j, :] if what == "k" else ev[:, AT[(what, j)] % 2, :]
                    for t in range(NCH):
                        transpose(M[:, 0, 128 * t:128 * t + 128], src[:, NS + 128 * t:NS + 128 * t + 128], 128)
                    last = transpose(M[0:NS, 1, 0:128], src[:, 0:NS], 128)
                elif kind == "rows":
                    pe.wait_ge(ev_act, EA[AT[("gates", 0)]] + 1)
                    for f in range(2):
                        last = nc.tensor.matmul(M[0:H, f, 0:HALF], ident[0:2 * H, H:2 * H],
                                                ev[0:2 * H, AT[("gates", 0)] % 2, HALF * f:HALF * f + HALF],
                                                start=True, stop=True)
                elif kind == "mix":
                    g = what // 2
                    for c in range(NCH):
                        nc.tensor.matmul(M[:, 0, 128 * c:128 * c + 128], xtok[:, c, 128 * what:128 * what + 128],
                                         wsT[:, g, :], start=True, stop=True)
                    last = nc.tensor.matmul(M[:, 1, 0:NS], xtok[0:NS, NCH, 128 * what:128 * what + 128],
                                            wsS[:, g, :], start=True, stop=True)
                elif kind == "s_pre":
                    rows_of(M[:, 0, :], lambda h: selh[:, h, :], lambda h: rws[:, 2, 0:NS], NS)
                    rows_of(M[:, 0, 4 * NS:], lambda h: selh[:, h, :], lambda h: m0s, NB)
                    rows_of(M[:, 1, :], lambda h: selh[:, h, :], lambda h: rws[:, 3, 0:NS], NS)
                    rows_of(M[0:NS, 2, :], lambda h: kT[:, h, 0:NS], lambda h: qT[:, h, 0:NS], NS)
                    transpose(M[0:NS, 3, 0:H], rws[:, 0, 0:NS], H)
                    transpose(M[0:NS, 3, H:2 * H], rws[:, 4, 0:NS], H)
                    transpose(M[0:NB, 3, 64:64 + H], rws[:, 4, NS:NS + NB], H)
                    for h in range(H):
                        last = transpose(M[:, 3, 16 + NB * h:16 + NB * h + NB], n0s[:, 128 * h:128 * h + 128], NB)
                elif kind == "s_c":
                    if what < 16:
                        pe.wait_ge(c_in[what % 3], 16 * (what // 3 + 1))
                        for b in range(4):
                            last = transpose(M[:, 0, 128 * b:128 * b + 128],
                                             CIN[what % 3][:, 128 * b:128 * b + 128], 128)
                    if what > 0:
                        i = what - 1
                        h, vh, bh = i // 4, i // 2 % 2, i % 2
                        v = vtok[0:NS, NCH, 256 * h + 128 * vh:256 * h + 128 * vh + 128]
                        num = M[:, 2, NS * (H * vh + h):NS * (H * vh + h) + NS]
                        if bh == 0:
                            nc.tensor.matmul(num, v, E[0:NS, 0, NS * h:NS * h + NS], start=True, stop=False)
                        for b in range(4):
                            c0 = 16 * bh + NL * b
                            nc.tensor.matmul(num[:, c0:c0 + NL], CTS[i % 2][:, 128 * b:128 * b + 128],
                                             E[:, 0, 128 + NS * h + c0:128 + NS * h + c0 + NL], start=False,
                                             stop=bh == 1 and b == 3)
                        last = nc.tensor.matmul(M[:, 1, :], v, KWM, start=True, stop=True)
                elif kind == "s_den":
                    nc.tensor.matmul(M[:, 3, 0:128], ones[0:NS, :], E[0:NS, 0, 0:128], start=True, stop=False)
                    nc.tensor.matmul(M[:, 3, 0:128], ones, E[:, 0, 256:384], start=False, stop=True)
                    for h in range(H):
                        last = nc.tensor.matmul(M[0:NB, 1, 128 * h:128 * h + 128], selb, KWS[:, 128 * h:128 * h + 128],
                                                start=True, stop=True)
                elif kind == "s_ss":
                    nc.tensor.matmul(M[:, 3, 0:128], ones, E[:, 6, 256:384], start=True, stop=False)
                    last = nc.tensor.matmul(M[:, 3, 0:128], ones, E[:, 6, 384:512], start=False, stop=True)
                elif kind == "ml1":
                    seg = slice(NS + 128 * what, NS + 128 * what + 128)
                    rows_of(M[:, 0, :], lambda h: selh[:, h, :], lambda h: rws[:, 2, seg], 128)
                    rows_of(M[:, 1, :], lambda h: selh[:, h, :], lambda h: rws[:, 3, seg], 128)
                    rows_of(M[:, 2, :], lambda h: kT[:, h, seg], lambda h: qT[:, h, seg], 128)
                    last = transpose(M[:, 3, 0:H], rws[:, 0, seg], H)
                elif kind == "ml2":
                    for vh in range(2):
                        for h in range(H):
                            o = M[:, vh, 128 * h:128 * h + 128]
                            nc.tensor.matmul(o, vtok[:, what, 256 * h + 128 * vh:256 * h + 128 * vh + 128],
                                             E[:, 0, 128 * h:128 * h + 128], start=True, stop=False)
                            nc.tensor.matmul(o, CT[:, h, 128 * vh:128 * vh + 128],
                                             E[:, 1, 128 * h:128 * h + 128], start=False, stop=True)
                    nc.tensor.matmul(M[:, 2, :], ones, E[:, 0, :], start=True, stop=False)
                    last = nc.tensor.matmul(M[:, 2, :], ones, E[:, 2, :], start=False, stop=True)
                elif kind == "ml3":
                    nc.tensor.matmul(M[:, 3, :], ones, E[:, 0, :], start=True, stop=False)
                    nc.tensor.matmul(M[:, 3, :], ones, E[:, 1, :], start=False, stop=True)
                    for h in range(H):
                        kw = E[:, 5, 128 * h:128 * h + 128]
                        nc.tensor.matmul(M[:, h // 2, 256 * (h % 2):256 * (h % 2) + 256], kw,
                                         vtok[:, what, 256 * h:256 * h + 256], start=True, stop=True)
                        last = nc.tensor.matmul(M[:, 2, h:h + 1], kw, ones[:, 0:1], start=True, stop=True)
                else:
                    for q in range(4):
                        h, vh = 2 * what + q // 2, q % 2
                        last = transpose(M[:, 0, 128 * q:128 * q + 128], CT[:, h, 128 * vh:128 * vh + 128], 128)
                    if what == 1:
                        last = transpose(M[0:H, 1, 0:128], nT, 128)
                last.then_inc(side_mm, 1)

            for i in range(NBK):
                if 2 <= i < WO0:
                    pe.wait_ge(ev_act, EA[i - 1])
                    pe.wait_ge(ev_dve, ED[i - 1])
                pe.wait_ge(w_lo, i + 1)
                if i >= WO0:
                    multiply_out(i)
                else:
                    multiply(i)
                for s in SIDE[i]:
                    side(s)

            pe.wait_ge(moe_consts, 16 * N_MOE)
            for t in range(NTILE + 1):
                if t < NTILE:
                    r = rows(t)
                    pe.wait_ge(n_xn, t + 1)
                    if t >= 2:
                        pe.wait_ge(n_ev, t - 1)
                    for c in range(KC):
                        last = transpose(Z[:, t % 2, c // 4, 128 * (c % 4):128 * (c % 4) + r],
                                         xn[0:r, t, 128 * c:128 * c + 128], r)
                    last.then_inc(n_tr, 1)
                if t > 0:
                    r = rows(t - 1)
                    pe.wait_ge(n_ev, t)
                    w = NG + NE
                    for c in range(KC):
                        last = nc.tensor.matmul(M[0:r, 0, w * (t - 1):w * t], xnT[(t - 1) % 2][:, c, 0:r], rw[:, c, :],
                                                start=c == 0, stop=c == KC - 1)
                    last.then_inc(n_log, 1)
            pe.wait_ge(r_oh, 1)
            RB = M[:, 1, :]
            c2 = CW.rearrange("p t e -> p (t e)")
            w2 = W1.rearrange("p t e -> p (t e)")
            n4 = NE * NCH
            nc.tensor.matmul(RB[:, 0:n4], triS, w2[:, 0:n4], start=True, stop=False)
            nc.tensor.matmul(RB[:, NE:n4], ones, c2[:, 0:n4 - NE], start=False, stop=True)
            nc.tensor.matmul(RB[0:NS, n4:n4 + NE], triS[0:NS, 0:NS], w2[0:NS, n4:n4 + NE], start=True, stop=False)
            nc.tensor.matmul(RB[0:NS, n4:n4 + NE], ones[:, 0:NS], c2[:, n4 - NE:n4], start=False, stop=True)
            nc.tensor.matmul(RB[:, n4 + NE:n4 + 2 * NE], ones[0:NS, :], w2[0:NS, n4:n4 + NE], start=True, stop=False)
            nc.tensor.matmul(RB[:, n4 + NE:n4 + 2 * NE], ones, c2[:, n4 - NE:n4], start=False, stop=True) \
                .then_inc(r_rank, 1)
            pe.wait_ge(r_ab, 1)
            for g in range(2 * NTILE):
                r = rows(g % NTILE)
                last = nc.tensor.matmul(M[0:CAP, 2, 0:NBLK], Aoh[0:r, g, :], Boh[0:r, g, :], start=g == 0,
                                        stop=g == 2 * NTILE - 1)
            last.then_inc(r_idx, 1)

            def tokens_by_feature(src):
                s = src.rearrange("q (p c) -> q p c", c=KC)
                for c in range(KC):
                    out = bank_xt()[:, CAP * c:CAP * c + CAP]
                    last = nc.tensor.matmul(out, s[:, :, c], ident[0:CAP, 0:CAP], start=True, stop=True) if c == 0 \
                        else transpose(out, s[:, :, c], CAP)
                return last

            def up(k, x, raws):
                for gu in range(2):
                    w = raws[gu].rearrange("p (c n) -> p c n", c=KC)
                    for j in range(2):
                        z = bank_up(k)[:, CAP * (2 * gu + j):CAP * (2 * gu + j) + CAP]
                        for c in range(KC):
                            last = nc.tensor.matmul(z, w[:, c, 128 * j:128 * j + 128], x[:, c, :], start=c == 0,
                                                    stop=c == KC - 1)
                return last

            def down(k, h, raw):
                for f in range(2):
                    for j in range(2):
                        last = nc.tensor.matmul(bank_out(k)[:, f, :], h[:, j, :],
                                                raw[:, D * j + 512 * f:D * j + 512 * f + 512], start=j == 0, stop=j == 1)
                return last

            def down_of(b, k, landed):
                pe.wait_ge(h_ready, b + 1)
                pe.wait_ge(wd_in[k], landed)
                if not (isinstance(b, int) and b < 2):
                    pe.wait_ge(y_copied, b - 1)
                down(k, hT[k], eraw[3 * k + 2]).then_inc(down_done, 1)

            def tokens_of(b, k, landed):
                pe.wait_ge(rows_in[k], landed)
                if not (isinstance(b, int) and b < 1):
                    pe.wait_ge(xt_ready, b)
                tokens_by_feature(xg[k]).then_inc(xt_done, 1)

            def up_of(b, k, landed):
                pe.wait_ge(xt_ready, b + 1)
                pe.wait_ge(wg_in[k], landed)
                pe.wait_ge(wu_in[k], landed)
                up(k, xT[k], eraw[3 * k:3 * k + 2]).then_inc(up_done, 1)

            pe.wait_ge(routed, 1)
            tokens_of(0, 0, 16)
            up_of(0, 0, 16)
            tokens_of(1, 1, 16)
            up_of(1, 1, 16)
            tokens_of(2, 0, 32)
            down_of(0, 0, 16)
            with pe.Fori(1, NE // 2 - 1) as i:
                up_of(i * 2, 0, i * 16 + 16)
                tokens_of(i * 2 + 1, 1, i * 16 + 16)
                down_of(i * 2 - 1, 1, i * 16)
                up_of(i * 2 + 1, 1, i * 16 + 16)
                tokens_of(i * 2 + 2, 0, i * 16 + 32)
                down_of(i * 2, 0, i * 16 + 16)
            up_of(NE - 2, 0, 8 * NE)
            tokens_of(NE - 1, 1, 8 * NE)
            down_of(NE - 3, 1, 8 * NE - 16)
            up_of(NE - 1, 1, 8 * NE)
            down_of(NE - 2, 0, 8 * NE)
            down_of(NE - 1, 1, 8 * NE)
            n_ov = pe.value_load(ctl[0:1, NOV:NOV + 1], min_val=0, max_val=NOV)
            with pe.If(n_ov > 0):
                with pe.Fori(0, n_ov) as o:
                    pe.wait_ge(o_rows, o * 16 + 16)
                    tokens_by_feature(xg[0]).then_inc(xt_done, 1)
                    pe.wait_ge(xt_ready, o + (NE + 1))
                    pe.wait_ge(o_w, o * 48 + 48)
                    up(0, xT[0], eraw[0:2]).then_inc(up_done, 1)
                    pe.wait_ge(h_ready, o + (NE + 1))
                    pe.wait_ge(y_copied, o + NE)
                    down(0, hT[0], eraw[2]).then_inc(down_done, 1)

        @block.scalar
        def _(act):
            n = [0]

            def step(ins):
                ins.then_inc(a_step, 1)
                n[0] += 1
                act.wait_ge(a_step, n[0])

            A = nc.scalar.activation

            def split(i):
                act.wait_ge(raw_in[i % 3], 16 * (i // 3 + 1))
                if i >= 2:
                    act.wait_ge(z_done, i - 1)
                m = wsize(i)
                A(wh[:, i % 2, 0:m], wraw[:, i % 3, 0:m], ACT.Copy).then_inc(w_hi, 1)

            def root(x, k):
                act.wait_ge(root_in, k + 1)
                step(A(x, x, ACT.Ln, bias=epsc[0:x.shape[0], :]))
                A(x, x, ACT.Exp, scale=-0.5).then_inc(root_out, 1)

            act.wait_ge(x_in, 32)
            for t in range(NTILE):
                r = rows(t)
                A(junk[0:r, :], xtok[0:r, t, :], ACT.Square, accum_out=stat[0:r, t:t + 1]).then_inc(x_ss, 1)
                act.wait_ge(x_ss, t + 1)
            act.wait_ge(consts, 1)
            for t in range(NTILE):
                root(stat[0:rows(t), 8 + t:9 + t], t)
            split(0)
            for c in range(KC):
                act.wait_ge(x_tr, c + 1)
                bank = Z[:, c % 6 // 2, c % 2, :] if c % 6 < 4 else M[:, c % 6 - 4, :]
                A(Xh[:, c, NS:T], bank, ACT.Copy).then_inc(x_hi, 1)
            A(Xh[:, :, 0:NS], M[:, 2, 0:KC * NS].rearrange("p (c n) -> p c n", c=KC), ACT.Copy).then_inc(x_hi, 1)

            def evacuate(i):
                kind, j = BLOCKS[i]
                if kind == "wo":
                    return
                e = ev[:, i % 2, :]
                if kind == "pa" and j == 7:
                    for c in range(KC):
                        act.wait_ge(ev_dve, ED[i] if c < 7 else ED[i] + 2)
                        if c == 0:
                            act.wait_ge(z_done, AT[("ga", 7)] + 1)
                        A(Xh[:, c, :], sumT[:, c, :], ACT.Copy).then_inc(ev_act, 1)
                    return
                if kind in ("pa", "pb"):
                    return
                act.wait_ge(z_done, i + 1)
                if kind == "q":
                    A(two(qT[:, j, :]), zz(i), ACT.Copy, scale=float(DQK) ** -0.5).then_inc(ev_act, 1)
                elif kind == "k":
                    A(two(kT[:, j, :]), zz(i), ACT.Copy).then_inc(ev_act, 1)
                else:
                    if i >= 2:
                        act.wait_ge(ev_dve, ED[i] if BLOCKS[i - 1][0] in ("pa", "pb") else ED[i - 1])
                    if kind in ("v", "gv", "gates"):
                        before = BLOCKS[i - 2]
                        tr = ("rows", 0, 0) if before[0] == "gates" else ("tr",) + before
                        if tr in SN:
                            act.wait_ge(side_mm, SN[tr] + 1)
                        func = ACT.Gelu_apprx_tanh if kind == "gv" else ACT.Copy
                        r = 2 * H if kind == "gates" else 128
                        A(two(e[0:r]), zz(i)[0:r], func).then_inc(ev_act, 1)
                    elif kind == "u":
                        if j < 2:
                            act.wait_ge(side_mm, SN[("tr", "gv", 6 + j)] + 1)
                        A(two(e), zz(i), ACT.Gelu_apprx_tanh).then_inc(ev_act, 1)
                        act.wait_ge(ev_dve, ED[i] + 1)
                        A(Hh[:, j, :], e, ACT.Copy).then_inc(ev_act, 1)
                    elif kind in ("gb", "ga"):
                        A(two(e), zz(i), ACT.Tanh, scale=0.5).then_inc(ev_act, 1)
                    elif kind == "og":
                        A(two(e), zz(i), ACT.Tanh, scale=0.5).then_inc(ev_act, 1)
                        act.wait_ge(ev_dve, ED[i] + 1)
                        act.wait_ge(z_done, AT[("pb", 7)] + 1)
                        A(Hh[:, j, :], e, ACT.Copy).then_inc(ev_act, 1)

            def side(st):
                kind, what, j = st
                a, d = HA[st], HD[st]
                if hands(st)[0] == 0 and st not in RN:
                    return
                act.wait_ge(side_mm, SN[st] + 1)
                if kind == "tr":
                    act.wait_ge(side_dve, d + 1)
                    g = j // 2
                    for t in range(NTILE):
                        r = rows(t)
                        last = A(gjunk[0:r, :], xtok[0:r, t, 256 * g:256 * g + 256], ACT.Square,
                                 accum_out=gst[0:r, t:t + 1])
                        if t < NTILE - 1:
                            step(last)
                    last.then_inc(side_act, 1)
                    root(gst, RN[st])
                elif kind == "s_ss":
                    root(E[:, 1, 0:128], RN[st])
                elif kind == "ml3":
                    root(E[:, 0, :], RN[st])
                elif kind == "rows":
                    step(A(two(rws[:, 1, :]), M[0:H, 0:2, 0:HALF], ACT.Identity, bias=gbias[:, 1:2]))
                    A(rws[:, 0, :], ev[0:H, AT[("gates", 0)] % 2, :], ACT.Identity, bias=gbias[:, 0:1]) \
                        .then_inc(side_act, 1)
                    step(A(rws[:, 4, :], rws[:, 1, :], ACT.Abs))
                    step(A(rws[:, 4, :], rws[:, 4, :], ACT.Exp, scale=-1.0))
                    A(rws[:, 4, :], rws[:, 4, :], ACT.Ln, bias=1.0).then_inc(side_act, 1)
                    act.wait_ge(side_dve, d + 1)
                    A(rws[:, 4, NS:NS + NB], rws[:, 4, NS:NS + NB], ACT.Exp).then_inc(side_act, 1)
                elif kind == "s_pre":
                    A(E[:, 0, 384:512], M[:, 1, 0:128], ACT.Exp, scale=-1.0)
                    act.wait_ge(side_dve, d + 1)
                    A(E[0:NS, 0, 0:128], E[0:NS, 0, 0:128], ACT.Exp, scale=-1.0)
                    A(E[:, 0, 128:256], E[:, 0, 128:256], ACT.Exp).then_inc(side_act, 1)
                    A(sm[0:NS, 4:8], sm[0:NS, 4:8], ACT.Exp)
                    A(sm[:, 96:128], sm[:, 96:128], ACT.Exp).then_inc(side_act, 1)
                elif kind == "s_c":
                    if what < 16:
                        A(CTS[what % 2], M[:, 0, :], ACT.Copy).then_inc(side_act, 1)
                    else:
                        A(CTS[0][:, 0:1], sm[:, 0:1], ACT.Copy).then_inc(side_act, 1)
                elif kind == "s_den":
                    act.wait_ge(c_free, 1)
                    A(E[:, 6, 0:256], M[:, 2, 0:256], ACT.Copy)
                    A(E[:, 6, 256:512], M[:, 2, 0:256], ACT.Square).then_inc(side_act, 1)
                elif kind == "ml1":
                    A(E[:, 4, :], M[:, 1, :], ACT.Exp, scale=-1.0)
                    act.wait_ge(side_dve, d + 1)
                    A(E[:, 0, :], E[:, 0, :], ACT.Exp, scale=-1.0)
                    A(sm[:, 4:12], sm[:, 4:12], ACT.Exp).then_inc(side_act, 1)
                    for h in range(H):
                        last = A(E[:, 1, 128 * h:128 * h + 128], M[:, 0, 128 * h:128 * h + 128], ACT.Exp,
                                 scale=-1.0, bias=sm[:, 12 + h:13 + h])
                    last.then_inc(side_act, 1)
                elif kind == "ml2":
                    A(E[:, 2:4, :], M[:, 0:2, :], ACT.Copy)
                    A(E[:, 0:2, :], M[:, 0:2, :], ACT.Square).then_inc(side_act, 1)

            for i in range(NBK):
                if i + 1 < NBK:
                    split(i + 1)
                for s in SIDE[i]:
                    side(s)
                evacuate(i)

            for t in range(NTILE):
                r = rows(t)
                act.wait_ge(ev_dve, ED[NBK - 1] + t + 1)
                if t == 0:
                    act.wait_ge(z_done, NBK)
                    act.wait_ge(moe_made, 1)
                A(sq[0:r, :], xres[0:r, t, :], ACT.Square, accum_out=nst[0:r, 0, t:t + 1]).then_inc(n_ss, 1)
                act.wait_ge(n_ss, t + 1)
            act.wait_ge(n_mean, 1)
            step(A(nst[:, 0, :], nst[:, 0, :], ACT.Ln, bias=epsc))
            A(nst[:, 0, :], nst[:, 0, :], ACT.Exp, scale=-0.5).then_inc(n_root, 1)
            for t in range(NTILE):
                r = rows(t)
                act.wait_ge(n_tr, t + 1)
                if t >= 2:
                    act.wait_ge(n_log, t - 1)
                A(xnT[t % 2][:, :, 0:r], Z[:, t % 2, :, :].rearrange("p a (c n) -> p (a c) n", n=128)[:, :, 0:r],
                  ACT.Copy).then_inc(n_ev, 1)
            act.wait_ge(r_exp_in, 1)
            A(rt[:, 0:25], rt[:, 0:25], ACT.Exp).then_inc(r_exp_out, 1)

            def silu_of(b, k):
                act.wait_ge(up_done, b + 1)
                if not (isinstance(b, int) and b < 2):
                    act.wait_ge(h_ready, b - 1)
                A(sil[k], bank_up(k)[:, 0:2 * CAP], ACT.Silu).then_inc(sil_ready, 1)

            def out_of(b, k, stored=None):
                act.wait_ge(down_done, b + 1)
                if stored is not None:
                    act.wait_ge(y_st[k], stored)
                A(yout[k].rearrange("q (f n) -> q f n", f=2), bank_out(k), ACT.Copy).then_inc(y_copied, 1)
                act.wait_ge(y_copied, b + 1)
                act.dma_start(slot_rows(b), yout[k]).then_inc(y_st[k], 16)

            act.wait_ge(routed, 1)
            silu_of(0, 0)
            silu_of(1, 1)
            out_of(0, 0)
            silu_of(2, 0)
            out_of(1, 1)
            silu_of(3, 1)
            out_of(2, 0, 16)
            with act.Fori(2, NE // 2) as i:
                silu_of(i * 2, 0)
                out_of(i * 2 - 1, 1, i * 16 - 16)
                silu_of(i * 2 + 1, 1)
                out_of(i * 2, 0, i * 16)
            out_of(NE - 1, 1, 8 * NE - 16)
            n_ov = act.value_load(ctl[0:1, NOV:NOV + 1], min_val=0, max_val=NOV)
            for k in range(2):
                act.wait_ge(y_st[k], 8 * NE)
            with act.If(n_ov > 0):
                with act.Fori(0, n_ov) as o:
                    act.wait_ge(up_done, o + (NE + 1))
                    A(sil[0], bank_up(0)[:, 0:2 * CAP], ACT.Silu).then_inc(sil_ready, 1)
                    act.wait_ge(down_done, o + (NE + 1))
                    A(yout[0].rearrange("q (f n) -> q f n", f=2), bank_out(0), ACT.Copy).then_inc(y_copied, 1)
                    act.wait_ge(y_copied, o + (NE + 1))
                    act.dma_start(slot_rows(o + NE), yout[0]).then_inc(o_st, 16)
                    act.wait_ge(o_st, o * 16 + 16)
            A(nst[:, 1, 0:1], nst[:, 1, 0:1], ACT.Copy).then_inc(moe_over, 1)

            for t in range(NTILE):
                r = rows(t)
                act.wait_ge(f_sum, t + 1)
                A(sq[0:r, :], xres[0:r, t, :], ACT.Square, accum_out=nst[0:r, 1, t:t + 1]).then_inc(f_ss, 1)
                act.wait_ge(f_mean, t + 1)
                step(A(nst[0:r, 1, t:t + 1], nst[0:r, 1, t:t + 1], ACT.Ln, bias=epsc[0:r, :]))
                A(nst[0:r, 1, t:t + 1], nst[0:r, 1, t:t + 1], ACT.Exp, scale=-0.5).then_inc(f_root, 1)


        @block.vector
        def _(dve):
            n = [0]
            V = nc.vector

            def step(ins):
                ins.then_inc(v_step, 1)
                n[0] += 1
                dve.wait_ge(v_step, n[0])

            def split(i):
                dve.wait_ge(w_hi, i + 1)
                m = wsize(i)
                V.tensor_tensor(wl[:, i % 2, 0:m], wraw[:, i % 3, 0:m], wh[:, i % 2, 0:m].bitcast(F32),
                                ALU.subtract).then_inc(w_lo, 1)

            dve.wait_ge(x_in, 32)
            dve.wait_ge(g_in, 16)
            for t in range(NTILE):
                r = rows(t)
                dve.wait_ge(x_ss, t + 1)
                V.tensor_scalar(stat[0:r, 8 + t:9 + t], stat[0:r, t:t + 1], 1.0 / D, None, ALU.mult) \
                    .then_inc(root_in, 1)
            for t in range(NTILE):
                r = rows(t)
                dve.wait_ge(root_out, t + 1)
                V.scalar_tensor_tensor(xtok[0:r, t, :], xtok[0:r, t, :], stat[0:r, 8 + t:9 + t], gB[0:r, :],
                                       ALU.mult, ALU.mult).then_inc(x_sc, 1)
            split(0)
            for c in range(KC):
                dve.wait_ge(x_hi, c + 1)
                bank = Z[:, c % 6 // 2, c % 2, :] if c % 6 < 4 else M[:, c % 6 - 4, :]
                V.tensor_tensor(Xl[:, c, NS:T], bank, Xh[:, c, NS:T].bitcast(F32), ALU.subtract).then_inc(x_lo, 1)
            dve.wait_ge(x_hi, KC + 1)
            V.tensor_tensor(Xl[:, :, 0:NS], M[:, 2, 0:KC * NS].rearrange("p (c n) -> p c n", c=KC),
                            Xh[:, :, 0:NS].bitcast(F32), ALU.subtract).then_inc(x_lo, 1)
            dve.wait_ge(x_tr, KC + 1)
            V.tensor_tensor(wsT, M[:, 3, :].rearrange("p (g t) -> p g t", g=NG),
                            tri.unsqueeze(1).broadcast_to([128, NG, 128]), ALU.mult)
            V.tensor_tensor(wsS, wsS, btri.unsqueeze(1).broadcast_to([NS, NG, NS]), ALU.mult).then_inc(x_lo, 1)

            def hm(c, h, vh):
                if c == NCH:
                    return vtok[:, NCH, NS * (H * vh + h):NS * (H * vh + h) + NS]
                return vtok[:, c, 128 * (H * vh + h):128 * (H * vh + h) + 128]

            def evacuate(i):
                kind, j = BLOCKS[i]
                e = ev[:, i % 2, :]
                if kind == "u":
                    dve.wait_ge(ev_act, EA[i] + 1)
                    V.tensor_tensor(e, e, mixT[:, j, :], ALU.mult).then_inc(ev_dve, 1)
                    dve.wait_ge(ev_act, EA[i] + 2)
                    V.tensor_tensor(Hl[:, j, :], e, Hh[:, j, :].bitcast(F32), ALU.subtract).then_inc(ev_dve, 1)
                elif kind in ("gb", "ga"):
                    dve.wait_ge(ev_act, EA[i] + 1)
                    V.tensor_scalar(e, e, 0.5, 0.5, ALU.mult, ALU.add).then_inc(ev_dve, 1)
                elif kind == "pb":
                    dve.wait_ge(z_done, i + 1)
                    dve.wait_ge(ev_dve, ED[i])
                    if j == 0:
                        dve.wait_ge(out_st, 16 * 3)
                    V.tensor_tensor(two(sumT[:, j, :]), zz(i), two(ev[:, (i - 1) % 2, :]), ALU.mult) \
                        .then_inc(ev_dve, 1)
                elif kind == "pa":
                    g = ev[:, (i - 1) % 2, :]
                    dve.wait_ge(z_done, i + 1)
                    dve.wait_ge(ev_dve, ED[i])
                    V.tensor_tensor(two(g), zz(i), two(g), ALU.mult).then_inc(ev_dve, 1)
                    dve.wait_ge(ev_dve, ED[i] + 1)
                    V.tensor_tensor(sumT[:, j, :], sumT[:, j, :], g, ALU.add).then_inc(ev_dve, 1)
                    if j == 7:
                        for c in range(KC):
                            dve.wait_ge(ev_act, EA[i] + c + 1)
                            last = V.tensor_tensor(Xl[:, c, :], sumT[:, c, :], Xh[:, c, :].bitcast(F32), ALU.subtract)
                        last.then_inc(ev_dve, 1)
                elif kind == "og":
                    h, vh = j // 2, j % 2
                    dve.wait_ge(ev_act, EA[i] + 1)
                    step(V.tensor_scalar(e, e, 0.5, 0.5, ALU.mult, ALU.add))
                    V.scalar_tensor_tensor(e[:, NS:T].rearrange("p (c n) -> p c n", c=NCH),
                                           e[:, NS:T].rearrange("p (c n) -> p c n", c=NCH), mlg[:, h, vh:vh + 1],
                                           vtok[:, 0:NCH, 128 * (H * vh + h):128 * (H * vh + h) + 128],
                                           ALU.mult, ALU.mult)
                    V.scalar_tensor_tensor(e[:, 0:NS], e[:, 0:NS], mlg[:, h, vh:vh + 1], hm(NCH, h, vh),
                                           ALU.mult, ALU.mult).then_inc(ev_dve, 1)
                    dve.wait_ge(ev_act, EA[i] + 2)
                    V.tensor_tensor(Hl[:, j, :], e, Hh[:, j, :].bitcast(F32), ALU.subtract).then_inc(ev_dve, 1)
                elif kind == "wo":
                    half, q = j // 8, j % 8
                    if q < 7:
                        return
                    dve.wait_ge(z_done, i + 1)
                    dve.wait_ge(xr_in, 32)
                    for t in range(NTILE):
                        g = NTILE * half + t
                        bank = (Z[:, g % 8 // 2, g % 2, :] if g % 8 < 4 else M[:, g % 8 - 4, :])
                        r = rows(t)
                        xs = xres[0:r, t, 512 * half:512 * half + 512]
                        V.tensor_tensor(xs, xs, bank[0:r, :], ALU.add).then_inc(ev_dve, 1)

            def normalise(st, R, NUM, S, out, w):
                step(V.scalar_tensor_tensor(S, M[:, 3, 0:w], 1.0 / DV, R, ALU.mult, ALU.mult))
                V.tensor_tensor(S, S, R, ALU.mult).then_inc(root_in, 1)
                dve.wait_ge(root_out, RN[st] + 1)
                step(V.tensor_tensor(S, S, R, ALU.mult))
                return V.tensor_tensor(out, NUM, S.unsqueeze(1).broadcast_to([128, 2, w]), ALU.mult)

            def side(st):
                kind, what, j = st
                a, d = HA[st], HD[st]
                dve.wait_ge(side_mm, SN[st] + 1)
                if kind == "tr":
                    dst, w = (ktok, 512) if what == "k" else (vtok, D) if what == "v" else (xtok, D)
                    V.tensor_copy(dst[:, 0:NCH, 128 * j:128 * j + 128], M[:, 0, :].rearrange("p (t n) -> p t n", t=NCH))
                    last = V.tensor_copy(dst[0:NS, NCH, 128 * j:128 * j + 128], M[0:NS, 1, 0:128])
                    if hands(st)[0]:
                        last.then_inc(side_dve, 1)
                        dve.wait_ge(side_act, a + 1)
                        g = j // 2
                        V.tensor_scalar(gst, gst, 1.0 / 256, None, ALU.mult).then_inc(root_in, 1)
                        dve.wait_ge(root_out, RN[st] + 1)
                        for t in range(NTILE):
                            r = rows(t)
                            s = xtok[0:r, t, 256 * g:256 * g + 256]
                            last = V.scalar_tensor_tensor(s, s, gst[0:r, t:t + 1], gmB[0:r, 256 * g:256 * g + 256],
                                                          ALU.mult, ALU.mult)
                elif kind == "rows":
                    LI, LF, MM, mm, tmp = (rws[:, r, :] for r in range(5))
                    dve.wait_ge(side_act, a + 2)
                    step(V.scalar_tensor_tensor(LF, LF, 0.0, tmp, ALU.min, ALU.subtract))
                    zero = CT[0:H, 0, 0:128]
                    for c in range(NCH):
                        seg = slice(NS + 128 * c, NS + 128 * c + 128)
                        V.tensor_tensor_scan(LF[:, seg], LF[:, seg], zero, 0.0, ALU.add, ALU.add)
                    ls = LF[:, 0:NS].rearrange("p (b t) -> p b t", t=NL)
                    for t in range(1, NL):
                        step(V.tensor_tensor(ls[:, :, t], ls[:, :, t], ls[:, :, t - 1], ALU.add))
                    step(V.tensor_tensor(LI, LI, LF, ALU.subtract))
                    for c in range(NCH):
                        seg = slice(NS + 128 * c, NS + 128 * c + 128)
                        m0 = 0.0 if c == 0 else mm[:, NS + 128 * c - 1:NS + 128 * c]
                        step(V.tensor_tensor_scan(MM[:, seg], LI[:, seg], LI[:, seg], m0, ALU.max, ALU.max))
                        step(V.tensor_tensor(mm[:, seg], MM[:, seg], LF[:, seg], ALU.add))
                    Ms, As = (r[:, 0:NS].rearrange("p (b t) -> p b t", t=NL) for r in (MM, LI))
                    step(V.tensor_tensor(Ms[:, :, 0], As[:, :, 0], m0s, ALU.max))
                    for t in range(1, NL):
                        step(V.tensor_tensor(Ms[:, :, t], As[:, :, t], Ms[:, :, t - 1], ALU.max))
                    V.tensor_tensor(mm[:, 0:NS], MM[:, 0:NS], LF[:, 0:NS], ALU.add)
                    last_m = Ms[:, :, NL - 1:NL].broadcast_to([H, NB, NL])
                    V.tensor_tensor(tmp[:, 0:NS].rearrange("p (b t) -> p b t", t=NL), As, last_m, ALU.subtract)
                    V.tensor_tensor(tmp[:, NS:NS + NB], m0s, Ms[:, :, NL - 1], ALU.subtract).then_inc(side_dve, 1)
                    dve.wait_ge(side_act, a + 3)
                    last = V.tensor_copy(stat[:, 21:22], stat[:, 0:1])
                elif kind == "mix":
                    g = what // 2
                    V.tensor_tensor(mixT[:, what, NS:T].rearrange("p (c n) -> p c n", c=NCH),
                                    M[:, 0, :].rearrange("p (c n) -> p c n", c=NCH),
                                    bsB[:, g, :].unsqueeze(1).broadcast_to([128, NCH, 128]), ALU.add)
                    last = V.tensor_tensor(mixT[:, what, 0:NS].rearrange("p (b t) -> p b t", b=NB),
                                           M[:, 1, 0:NS].rearrange("p (b t) -> p b t", b=NB),
                                           bsB[:, g, 0:NL].unsqueeze(1).broadcast_to([128, NB, NL]), ALU.add)
                elif kind == "s_pre":
                    V.tensor_copy(sm[0:NS, 0:8], M[0:NS, 3, 0:8])
                    V.tensor_copy(sm[:, 16:48], M[:, 3, 16:48])
                    V.tensor_copy(sm[0:NB, 48:52], M[0:NB, 3, 64:68])
                    step(V.tensor_copy(sm[:, 128:160], M[:, 0, 128:160]))
                    for h in range(H):
                        V.tensor_scalar(E[0:NS, 0, NS * h:NS * h + NS], M[0:NS, 0, NS * h:NS * h + NS],
                                        sm[0:NS, h:h + 1], 0.0, ALU.subtract, ALU.max)
                    Mb = M[:, 0, 0:128].rearrange("p (x t) -> p x t", t=NL)
                    V.tensor_tensor(E[:, 0, 128:256].rearrange("p (x t) -> p x t", t=NL),
                                    sm[:, 128:160].unsqueeze(2).broadcast_to([128, H * NB, NL]), Mb, ALU.subtract)
                    V.tensor_tensor(sm[:, 96:128], sm[:, 128:160], Mb[:, :, NL - 1], ALU.subtract) \
                        .then_inc(side_dve, 1)
                    dve.wait_ge(side_act, a + 2)
                    P = E[0:NS, 0, 0:128].rearrange("p (h t) -> p h t", h=H)
                    step(V.tensor_tensor(P, P, btri.unsqueeze(1).broadcast_to([NS, H, NS]), ALU.mult))
                    V.tensor_tensor(E[0:NS, 0, 0:128], E[0:NS, 0, 0:128], M[0:NS, 2, 0:128], ALU.mult)
                    q = E[:, 0, 128:256].rearrange("p (h t) -> p h t", h=H)
                    step(V.tensor_tensor(q, q, qT[:, :, 0:NS], ALU.mult))
                    V.tensor_tensor(E[:, 0, 256:384].rearrange("p (x t) -> p x t", t=NL),
                                    E[:, 0, 128:256].rearrange("p (x t) -> p x t", t=NL),
                                    sm[:, 16:48].unsqueeze(2).broadcast_to([128, H * NB, NL]), ALU.mult)
                    for h in range(H):
                        last = V.tensor_scalar(KWS[:, 128 * h:128 * h + 128], ktok[0:NS, NCH, 128 * h:128 * h + 128],
                                               sm[0:NS, 4 + h:5 + h], None, ALU.mult)
                elif kind == "s_c":
                    dve.wait_ge(side_act, a + 1)
                    if what > 0:
                        i = what - 1
                        h, bh = i // 4, i % 2
                        for b in range(4):
                            s = CIN[i % 3][:, 128 * b:128 * b + 128]
                            x = 96 + NB * h + 4 * bh + b
                            last = V.scalar_tensor_tensor(s, s, sm[:, x:x + 1], M[:, 1, 128 * b:128 * b + 128],
                                                          ALU.mult, ALU.add)
                    if what < 16:
                        h, bh = what // 4, what % 2
                        last = V.tensor_tensor(KWM.rearrange("p (b d) -> p b d", b=4),
                                               KWS[:, 128 * h:128 * h + 128].unsqueeze(1).broadcast_to([NS, 4, 128]),
                                               selb[:, 4 * bh:4 * bh + 4].unsqueeze(2).broadcast_to([NS, 4, 128]),
                                               ALU.mult)
                elif kind == "s_den":
                    R = E[:, 0, 384:512]
                    step(V.tensor_tensor(R, M[:, 3, 0:128], R, ALU.max))
                    step(V.scalar_tensor_tensor(R, M[:, 3, 0:128], -1.0, R, ALU.mult, ALU.max))
                    V.reciprocal(R, R)
                    dve.wait_ge(side_act, a + 1)
                    for h in range(H):
                        x = n0s[:, 128 * h:128 * h + 128]
                        last = V.scalar_tensor_tensor(x, x, sm[0:NB, 48 + h:49 + h], M[0:NB, 1, 128 * h:128 * h + 128],
                                                      ALU.mult, ALU.add)
                elif kind == "s_ss":
                    last = normalise(st, E[:, 0, 384:512], E[:, 6, 0:256].rearrange("p (v x) -> p v x", v=2),
                                     E[:, 1, 0:128], vtok[:, NCH, 0:256].rearrange("p (v x) -> p v x", v=2), 128)
                elif kind == "ml1":
                    step(V.tensor_copy(sm[:, 0:4], M[:, 3, 0:4]))
                    for h in range(H):
                        V.tensor_scalar(E[:, 0, 128 * h:128 * h + 128], M[:, 0, 128 * h:128 * h + 128],
                                        sm[:, h:h + 1], 0.0, ALU.subtract, ALU.max)
                    ML = M[:, 0, 127:512:128]
                    if what == 0:
                        V.memset(sm[:, 12:16], 0.0)
                    else:
                        V.tensor_copy(sm[:, 12:16], sm[:, 52:56])
                    V.tensor_tensor(sm[:, 4:8], sm[:, 0:4], ML, ALU.subtract)
                    m0 = sm[:, 56:60] if what == 0 else sm[:, 52:56]
                    V.tensor_tensor(sm[:, 8:12], m0, ML, ALU.subtract).then_inc(side_dve, 1)
                    dve.wait_ge(side_act, a + 1)
                    P = E[:, 0, :].rearrange("p (h t) -> p h t", h=H)
                    step(V.tensor_tensor(P, P, tri.unsqueeze(1).broadcast_to([128, H, 128]), ALU.mult))
                    V.tensor_tensor(E[:, 0, :], E[:, 0, :], M[:, 2, :], ALU.mult)
                    for h in range(H):
                        V.tensor_scalar(E[:, 5, 128 * h:128 * h + 128], ktok[:, what, 128 * h:128 * h + 128],
                                        sm[:, 4 + h:5 + h], None, ALU.mult)
                    dve.wait_ge(side_act, a + 2)
                    seg = slice(NS + 128 * what, NS + 128 * what + 128)
                    V.tensor_copy(sm[:, 52:56], M[:, 1, 127:512:128])
                    q = E[:, 1, :].rearrange("p (h t) -> p h t", h=H)
                    step(V.tensor_tensor(q, q, qT[:, :, seg], ALU.mult))
                    for h in range(H):
                        last = V.tensor_scalar(E[:, 2, 128 * h:128 * h + 128], E[:, 1, 128 * h:128 * h + 128],
                                               nT[:, h:h + 1], None, ALU.mult)
                elif kind == "ml2":
                    R = E[:, 4, :]
                    step(V.tensor_tensor(R, M[:, 2, :], R, ALU.max))
                    step(V.scalar_tensor_tensor(R, M[:, 2, :], -1.0, R, ALU.mult, ALU.max))
                    dve.wait_ge(side_act, a + 1)
                    last = V.reciprocal(R, R)
                elif kind == "ml3":
                    for h in range(H):
                        V.scalar_tensor_tensor(CT[:, h, :], CT[:, h, :], sm[:, 8 + h:9 + h],
                                               M[:, h // 2, 256 * (h % 2):256 * (h % 2) + 256], ALU.mult, ALU.add)
                    step(V.tensor_tensor(nT, nT, sm[:, 8:12], ALU.mult))
                    V.tensor_tensor(nT, nT, M[:, 2, 0:H], ALU.add)
                    last = normalise(st, E[:, 4, :], E[:, 2:4, :], E[:, 0, :],
                                     vtok[:, what, :].rearrange("p (v x) -> p v x", v=2), 512)
                else:
                    last = V.tensor_copy(E[:, what, :], M[:, 0, :])
                    if what == 1:
                        last = V.tensor_copy(E[0:H, 2, 0:128], M[0:H, 1, 0:128])
                last.then_inc(side_end, 1)
                dve.wait_ge(side_end, SN[st] + 1)

            for i in range(NBK):
                if i + 1 < NBK:
                    split(i + 1)
                for s in SIDE[i]:
                    side(s)
                evacuate(i)

            dve.wait_ge(moe_consts, 16 * N_MOE)
            dve.wait_ge(moe_made, 1)
            dve.wait_ge(n_ss, NTILE)
            V.tensor_scalar(nst[:, 0, :], nst[:, 0, :], 1.0 / D, None, ALU.mult).then_inc(n_mean, 1)
            V.memset(Lg, 0.0)
            dve.wait_ge(n_root, 1)
            for t in range(NTILE):
                r = rows(t)
                V.scalar_tensor_tensor(xn[0:r, t, :], xres[0:r, t, :], nst[0:r, 0, t:t + 1], gffn[0:r, :],
                                       ALU.mult, ALU.mult).then_inc(n_xn, 1)
            dve.wait_ge(n_log, NTILE)
            nw = NG + NE
            L4 = M[:, 0, 0:NCH * nw].rearrange("p (t n) -> p t n", n=nw)
            V.tensor_tensor(Lg[:, 0:NCH, :], L4, rb.unsqueeze(1).broadcast_to([128, NCH, nw]), ALU.add)
            step(V.tensor_tensor(Lg[0:NS, NCH, :], M[0:NS, 0, NCH * nw:NTILE * nw], rb[0:NS, :], ALU.add))
            G = Lg[:, :, 0:NG]
            fine = Lg[:, :, NG:nw].rearrange("p t (g e) -> p t g e", g=NG)

            cur_rt = [32]

            def tmp(*shape):
                m = int(np.prod(shape))
                o = cur_rt[0]
                cur_rt[0] += m
                assert cur_rt[0] <= 512
                ap = rt[:, o:o + m]
                if len(shape) == 2:
                    ap = ap.rearrange("p (a b) -> p a b", a=shape[0])
                return ap

            def spread(x, m):
                return x.unsqueeze(2).broadcast_to([128, x.shape[1], m])

            def first_max(x, m, mx, hot, work):
                step(V.tensor_reduce(mx, x, AX, ALU.max))
                step(V.tensor_tensor(work, x, spread(mx, m), ALU.is_ge))
                step(V.tensor_tensor(work, work, w8[:, NPG - m:NPG].unsqueeze(1).broadcast_to([128, NTILE, m]), ALU.mult))
                best = tmp(NTILE)
                step(V.tensor_reduce(best, work, AX, ALU.max))
                step(V.tensor_tensor(hot, work, spread(best, m), ALU.is_equal))

            gm, m1, m2 = tmp(NTILE), tmp(NTILE), tmp(NTILE)
            ohg, gwork = tmp(NTILE, NG), tmp(NTILE, NG)
            first_max(G, NG, gm, ohg, gwork)
            V.tensor_tensor(rt[:, 0:20].rearrange("p (t g) -> p t g", g=NG), G, spread(gm, NG), ALU.subtract)
            step(V.tensor_tensor(F4, fine, ohg.unsqueeze(3).broadcast_to([128, NTILE, NG, NPG]), ALU.mult))
            fs, oh1, oh2, fwork = tmp(NTILE, NPG), tmp(NTILE, NPG), tmp(NTILE, NPG), tmp(NTILE, NPG)
            step(V.tensor_tensor(fs, F4[:, :, 0, :], F4[:, :, 1, :], ALU.add))
            for g in range(2, NG):
                step(V.tensor_tensor(fs, fs, F4[:, :, g, :], ALU.add))
            first_max(fs, NPG, m1, oh1, fwork)
            step(V.scalar_tensor_tensor(fs, oh1, -BIG, fs, ALU.mult, ALU.add))
            first_max(fs, NPG, m2, oh2, fwork)
            V.tensor_tensor(rt[:, 20:25], m2, m1, ALU.subtract).then_inc(r_exp_in, 1)
            for j, hot in enumerate((oh1, oh2)):
                for t in range(NTILE):
                    last = V.tensor_tensor(OH[:, j, t, :].rearrange("p (g e) -> p g e", g=NG),
                                           ohg[:, t, :].unsqueeze(2).broadcast_to([128, NG, NPG]),
                                           hot[:, t, :].unsqueeze(1).broadcast_to([128, NG, NPG]), ALU.mult)
            step(last)
            step(V.tensor_tensor(W1, OH[:, 0], OH[:, 1], ALU.add))
            step(V.tensor_copy(CW[:, 0, :], W1[:, 0, :]))
            for t in range(1, NCH):
                last = V.tensor_tensor(CW[:, t, :], CW[:, t - 1, :], W1[:, t, :], ALU.add)
                if t < NCH - 1:
                    step(last)
            last.then_inc(r_oh, 1)
            dve.wait_ge(r_exp_out, 1)
            se = tmp(NTILE)
            step(V.tensor_reduce(se, rt[:, 0:20].rearrange("p (t g) -> p t g", g=NG), AX, ALU.add))
            step(V.scalar_tensor_tensor(GT[:, 0, :], rt[:, 20:25], 1.0, se, ALU.add, ALU.mult))
            step(V.reciprocal(GT[:, 0, :], GT[:, 0, :]))
            V.tensor_tensor(GT[:, 1, :], GT[:, 0, :], rt[:, 20:25], ALU.mult)
            dve.wait_ge(r_rank, 1)
            n4 = NE * NCH
            V.memset(RK[:, NCH, :], 0.0)
            step(V.tensor_copy(RK[:, 0:NCH, :], M[:, 1, 0:n4].rearrange("p (t e) -> p t e", e=NE)))
            V.tensor_copy(RK[0:NS, NCH, :], M[0:NS, 1, n4:n4 + NE])
            step(V.tensor_copy(RK[:, NTILE, :], M[:, 1, n4 + NE:n4 + 2 * NE]))
            cn = RK[:, NTILE, :]
            nb, S, zero = tmp(NE), tmp(NE), tmp(NE)
            V.memset(zero, 0.0)
            step(V.tensor_scalar(nb, cn, float(CAP), None, ALU.is_gt))
            for q in range(2, MAXK + 1):
                step(V.scalar_tensor_tensor(nb, cn, float(CAP * q), nb, ALU.is_gt, ALU.add))
            step(V.tensor_tensor_scan(S, nb, zero, 0.0, ALU.add, ALU.add))
            step(V.tensor_tensor(nb, S, nb, ALU.subtract))

            def pick(out, x):
                step(V.tensor_tensor(OT, OH, x, ALU.mult))
                step(V.tensor_reduce(out.rearrange("p (j t) -> p j t", j=2), OT, AX, ALU.add))

            n10 = 2 * NTILE
            full = [128, 2, NTILE, NE]
            rank, base, ex, kb, hit = tmp(n10), tmp(n10), tmp(n10), tmp(n10), tmp(n10)
            pick(rank, RK[:, 0:NTILE, :].unsqueeze(1).broadcast_to(full))
            pick(base, nb.unsqueeze(1).unsqueeze(1).broadcast_to(full))
            pick(ex, io64[:, 0:NE].unsqueeze(1).unsqueeze(1).broadcast_to(full))
            step(V.tensor_scalar(kb, rank, float(CAP), None, ALU.is_ge))
            V.tensor_copy(hit, kb)
            for q in range(2, MAXK + 1):
                step(V.scalar_tensor_tensor(kb, rank, float(CAP * q), kb, ALU.is_ge, ALU.add))
            step(V.tensor_tensor(base, base, kb, ALU.add))
            step(V.tensor_tensor(base, base, ex, ALU.subtract))
            step(V.scalar_tensor_tensor(base, base, float(NE - 1), hit, ALU.add, ALU.mult))
            step(V.tensor_tensor(base, base, ex, ALU.add))
            step(V.scalar_tensor_tensor(rank, kb, float(-CAP), rank, ALU.mult, ALU.add))
            step(V.scalar_tensor_tensor(ex, base, float(CAP), rank, ALU.mult, ALU.add))
            V.tensor_copy(slots, ex)
            V.tensor_tensor(Aoh, io64.unsqueeze(1).broadcast_to([128, n10, CAP]), spread(rank, CAP), ALU.is_equal)
            step(V.tensor_tensor(Boh, io64[:, 0:NBLK].unsqueeze(1).broadcast_to([128, n10, NBLK]), spread(base, NBLK),
                                 ALU.is_equal))
            for j in range(2):
                last = V.tensor_tensor(Boh[:, NTILE * j:NTILE * j + NTILE, :], Boh[:, NTILE * j:NTILE * j + NTILE, :],
                                       spread(tok1, NBLK), ALU.mult)
            last.then_inc(r_ab, 1)
            step(V.tensor_tensor(CO, S[0:1].unsqueeze(1).broadcast_to([1, NOV, NE]),
                                 io64[0:1, 0:NOV].unsqueeze(2).broadcast_to([1, NOV, NE]), ALU.is_le))
            own = tmp(NOV)
            step(V.tensor_reduce(own[0:1], CO, AX, ALU.add))
            V.tensor_scalar(ctl[:, 0:NOV], own[0:1], float(NE - 1), None, ALU.min)
            V.tensor_copy(ctl[:, NOV:NOV + 1], S[0:1, NE - 1:NE])
            dve.wait_ge(r_idx, 1)
            step(V.tensor_scalar(VI, M[0:CAP, 2, 0:NBLK], 0.0, float(4 * T), ALU.is_equal, ALU.mult))
            step(V.scalar_tensor_tensor(VI, M[0:CAP, 2, 0:NBLK], -1.0, VI, ALU.add, ALU.add))
            step(V.tensor_copy(idx, VI))
            V.tensor_copy(rt[0:1, 0:1], rt[0:1, 0:1]).then_inc(routed, 1)

            def tokens(k):
                return V.tensor_copy(xT[k], bank_xt().rearrange("p (c n) -> p c n", c=KC))

            def gated(k):
                return V.tensor_tensor(hT[k].rearrange("p j n -> p (j n)"), sil[k], bank_up(k)[:, 2 * CAP:4 * CAP], ALU.mult)

            def tokens_of(b, k):
                dve.wait_ge(xt_done, b + 1)
                if not (isinstance(b, int) and b < 2):
                    dve.wait_ge(up_done, b - 1)
                tokens(k).then_inc(xt_ready, 1)

            def gated_of(b, k):
                dve.wait_ge(sil_ready, b + 1)
                if not (isinstance(b, int) and b < 2):
                    dve.wait_ge(down_done, b - 1)
                gated(k).then_inc(h_ready, 1)

            tokens_of(0, 0)
            tokens_of(1, 1)
            gated_of(0, 0)
            with dve.Fori(1, NE // 2) as i:
                tokens_of(i * 2, 0)
                gated_of(i * 2 - 1, 1)
                tokens_of(i * 2 + 1, 1)
                gated_of(i * 2, 0)
            gated_of(NE - 1, 1)
            n_ov = dve.value_load(ctl[0:1, NOV:NOV + 1], min_val=0, max_val=NOV)
            with dve.If(n_ov > 0):
                with dve.Fori(0, n_ov) as o:
                    dve.wait_ge(xt_done, o + (NE + 1))
                    dve.wait_ge(up_done, o + NE)
                    tokens(0).then_inc(xt_ready, 1)
                    dve.wait_ge(sil_ready, o + (NE + 1))
                    gated(0).then_inc(h_ready, 1)

            for t in range(NTILE + 1):
                if t < NTILE:
                    r = rows(t)
                    x = xres[0:r, t, :]
                    dve.wait_ge(yg_in[t], 32)
                    step(V.scalar_tensor_tensor(x, yg[0:r, t, :], GT[0:r, 0, t:t + 1], x, ALU.mult, ALU.add))
                    V.scalar_tensor_tensor(x, yg[0:r, NTILE + t, :], GT[0:r, 1, t:t + 1], x, ALU.mult, ALU.add) \
                        .then_inc(f_sum, 1)
                if t > 0:
                    u = t - 1
                    r = rows(u)
                    dve.wait_ge(f_ss, u + 1)
                    V.tensor_scalar(nst[0:r, 1, u:u + 1], nst[0:r, 1, u:u + 1], 1.0 / D, None, ALU.mult).then_inc(f_mean, 1)
                    dve.wait_ge(f_root, u + 1)
                    V.scalar_tensor_tensor(yg[0:r, u, :], xres[0:r, u, :], nst[0:r, 1, u:u + 1], gfin[0:r, :],
                                           ALU.mult, ALU.mult).then_inc(f_out, 1)


_INS = ["x_prompt", "x_sample", "state_mlstm_C", "state_mlstm_n", "state_mlstm_m", "norm_mix_g", "w_in", "ml_b_i",
        "ml_b_f", "ml_norm_g", "gm_norm_g", "gm_ws", "gm_bs", "p_a", "p_b", "w_out", "norm_ffn_g", "rc_w", "rc_b",
        "rf_w", "rf_b", "e_wg", "e_wu", "e_wd", "final_norm_g"]
_OUTS = [(1, NP_TOK, D), (NB, NL, D), (1, 1, H, DV, DQK), (1, 1, H, DQK), (1, 1, H), (1, NB, H, DV, DQK),
         (1, NB, H, DQK), (1, NB, H), (1, NB, NL, 4, 256)]


def kernel(**inputs):
    import concourse.bacc as bacc
    from concourse.bass_utils import run_bass_kernel_spmd

    nc = bacc.Bacc("TRN2", target_bir_lowering=False, num_devices=1)
    arrays, args = {}, []
    for name in _INS:
        a = np.ascontiguousarray(inputs[name])
        arrays[f"in_{name}"] = a
        args.append(nc.dram_tensor(f"in_{name}", a.shape, mybir.dt.from_np(a.dtype), kind="ExternalInput").ap())
    for i, shape in enumerate(_OUTS):
        args.append(nc.dram_tensor(f"out_{i}", shape, F32, kind="ExternalOutput").ap())
    build(nc, *args)
    r = run_bass_kernel_spmd(nc, [arrays], core_ids=[0])
    return tuple(r.results[0][f"out_{i}"] for i in range(len(_OUTS)))
```

```python
from contextlib import ExitStack

import numpy as np

import concourse.bass as bass
from concourse import mybir

ALU = mybir.AluOpType
ACT = mybir.ActivationFunctionType
F32 = mybir.dt.float32
F32R = mybir.dt.float32r
I32 = mybir.dt.int32
U32 = mybir.dt.uint32
AX = mybir.AxisListType.X

D = 1024
NP_TOK, NB, NL = 512, 8, 4
NS = NB * NL
T = NS + NP_TOK
HALF = T // 2
NCH = NP_TOK // 128
H, DQK, DV = 4, 128, 256
KC = D // 128
NE, NG, NPG, EH = 32, 4, 8, 256
EPS = 1e-6
CAP = 64
MAXK = T // CAP
NOV = (2 * T) // CAP
NBLK = NE + NOV
BIG = 1.0e30
COL = {"q": 0, "k": 512, "v": 1024, "og": 2048, "gates": 3072, "u": 3080, "gv": 4104, "ga": 5128, "gb": 6152}
NTILE = NCH + 1


UE = 2048
RING = 4


def tok_cols(t):
    return NS + 128 * t if t < NCH else 0


def rows(t):
    return 128 if t < NCH else NS


BLOCKS = ([("q", j) for j in range(4)] + [("k", j) for j in range(4)] + [("gates", 0)]
          + [("v", j) for j in range(8)] + [("gv", j) for j in range(8)] + [("u", j) for j in range(8)]
          + [b for j in range(8) for b in (("gb", j), ("pb", j))] + [("og", j) for j in range(8)]
          + [b for j in range(8) for b in (("ga", j), ("pa", j))]
          + [("wo", i) for i in range(16)])
NBK = len(BLOCKS)
AT = {b: i for i, b in enumerate(BLOCKS)}
BY_ACT = ("q", "k", "v", "gv", "u", "gb", "og", "ga", "gates")
WO0 = AT[("wo", 0)]

X_ORDER = (0, 1, KC, 2, 3, 4, 5, 6, 7)

SIDE = {i: [] for i in range(NBK)}


def _place_side_steps():
    def place(block, *steps):
        SIDE[block] += [step + (0,) * (3 - len(step)) for step in steps]

    for j in range(4):
        place(AT[("k", j)] + 1, ("tr", "k", j))
    place(AT[("gates", 0)] + 1, ("rows", 0))
    place(AT[("v", 2)], ("tr", "v", 0), ("tr", "v", 1))
    for j in range(2, 8):
        place(AT[("v", j)] + 1, ("tr", "v", j))
    place(AT[("gv", 0)], ("s_pre", 0))
    for j in range(8):
        place(AT[("gv", j)] + 1, *([("mix", 0)] if j == 7 else []), ("s_c", j), ("tr", "gv", j))
    for j in range(1, 8):
        place(AT[("u", j)], ("mix", j), ("s_c", 7 + j))
    k = AT[("gb", 0)]
    place(k, ("s_c", 15), ("s_c", 16))
    k += 1
    place(k, ("s_den", 0), ("s_ss", 0))
    for c in range(NCH):
        for stage in ("ml1", "ml2", "ml3"):
            k += 1
            place(k, (stage, c))
    for i in range(2):
        k += 1
        place(k, ("c_out", i))
    assert k < AT[("og", 0)]


_place_side_steps()
STEPS = [s for i in range(NBK) for s in SIDE[i]]
SN = {s: n for n, s in enumerate(STEPS)}


def hands(step):
    kind, what, j = step
    if kind == "tr":
        return (1, 1) if what == "gv" and j % 2 else (0, 0)
    return {"rows": (2, 0), "mix": (0, 0), "s_pre": (2, 1), "s_c": (1, 0), "s_den": (1, 0), "s_ss": (0, 0),
            "ml1": (2, 1), "ml2": (1, 0), "ml3": (0, 0), "c_out": (0, 0)}[kind]


def evacs(kind, j):
    if kind == "pa" and j == 7:
        return 8, 10
    if kind == "wo":
        return 0, NTILE if j % 8 == 7 else 0
    return {"q": (1, 0), "k": (1, 0), "v": (1, 0), "gv": (1, 0), "gates": (1, 0), "u": (2, 2), "og": (2, 2),
            "gb": (1, 1), "ga": (1, 1), "pb": (0, 1), "pa": (0, 2)}[kind]


HA, HD, _a, _d = {}, {}, 0, 0
for _s in STEPS:
    HA[_s], HD[_s] = _a, _d
    _a, _d = _a + hands(_s)[0], _d + hands(_s)[1]
EA, ED, _a, _d = [], [], 0, 0
for _b in BLOCKS:
    EA.append(_a)
    ED.append(_d)
    _a, _d = _a + evacs(*_b)[0], _d + evacs(*_b)[1]
EA.append(_a)
ED.append(_d)


ROOTS = [s for s in STEPS if s[0] in ("s_ss", "ml3")]
RN = {s: n for n, s in enumerate(ROOTS)}


def build(nc, x_prompt, x_sample, state_C, state_n, state_m, norm_mix_g, w_in, ml_b_i, ml_b_f, ml_norm_g,
          gm_norm_g, gm_ws, gm_bs, p_a, p_b, w_out, norm_ffn_g, rc_w, rc_b, rf_w, rf_b, e_wg, e_wu, e_wd,
          final_norm_g, y_p, y_s, C_p, n_p, m_p, C_s, n_s, m_s, v_s):
    place = {}
    cur = [(nc.sbuf_base + 63) // 64 * 64]

    def at(name, shape, dt, offset):
        return nc.alloc_sbuf_tensor_at(name, shape, dt, offset=offset)[:]

    def take(name, shape, dt=F32):
        place[name] = cur[0]
        cur[0] += (4 * int(np.prod(shape[1:])) + 31) // 32 * 32
        return at(name, shape, dt, place[name])

    ident = take("ident", [128, 128])
    ones = take("ones", [128, 128])
    epsc = take("epsc", [128, 1])
    stat = take("stat", [128, 24])
    newt = take("newt", [128, 2, NTILE])
    xtok = take("xtok", [128, NTILE, D])
    mixer0 = cur[0]
    tri = take("tri", [128, 128])
    btri = take("btri", [NS, NS])
    selb = take("selb", [NS, NB])
    selh = take("selh", [H, H, 128])
    mlg = take("mlg", [128, H, 2])
    gbias = take("gbias", [H, 2])
    CT = take("CT", [128, H, DV])
    nT = take("nT", [128, H])
    wsT = take("wsT", [128, NG, 128])
    wsS = take("wsS", [NS, NG, NS])
    rep4 = take("rep4", [NL, NS])
    ws4 = take("ws4", [NL, NG * NL])
    gst = take("gst", [128, NTILE])
    sm = take("sm", [128, 160])
    m0s = take("m0s", [H, NB])
    n0s = take("n0s", [NB, H * DQK])
    Xh = take("Xh", [128, KC, T], F32R)
    Xl = take("Xl", [128, KC, T], F32R)
    Hh = take("Hh", [128, KC, T], F32R)
    Hl = take("Hl", [128, KC, T], F32R)
    wraw = take("wraw", [128, 3, KC * 128])
    wh = take("wh", [128, 2, KC * 128], F32R)
    wl = take("wl", [128, 2, KC * 128], F32R)
    ev = take("ev", [128, 2, T])
    rws = take("rws", [H, 5, T])
    E = take("E", [128, 8, 512])
    qT = take("qT", [128, H, T])
    kT = take("kT", [128, H, T])
    ktok = take("ktok", [128, NTILE, 512])
    vtok = take("vtok", [128, NTILE, D])
    assert cur[0] <= nc.sbuf_usable_end, (cur[0], nc.sbuf_usable_end)
    sumT = at("sumT", [128, KC, T], F32, place["xtok"])
    xres = at("xres", [128, NTILE, D], F32, place["qT"])
    mixT = at("mixT", [128, KC, T], F32, place["Hl"])
    junk = at("junk", [128, D], F32, place["Hl"])
    gB = at("gB", [128, D], F32, place["Hl"] + 4 * D)
    gmB = at("gmB", [128, D], F32, place["Hh"] + 5 * 4 * T)
    bsB = at("bsB", [128, NG, 128], F32, place["Hh"] + 7 * 4 * T)
    gjunk = at("gjunk", [128, 256], F32, place["Hh"] + 4 * 4 * T)
    wsraw = at("wsraw", [128, NG, 128], F32, place["Hh"])

    xn_dram = nc.dram_tensor("xn_rows", (T, D), F32).ap()
    slot_dram = nc.dram_tensor("slot_rows", (NBLK * CAP, D), F32).ap()
    zone = {"A": [mixer0, place["Xh"]], "B": [place["Xh"], place["Hh"]], "C": [place["Hh"], place["wraw"]],
            "D": [place["wraw"], place["ev"]], "F": [place["ev"], place["rws"]], "E": [place["rws"], place["qT"]],
            "I": [place["qT"] + 4 * NTILE * D, cur[0]]}

    def put(zone_name, name, shape, dt=F32):
        z = zone[zone_name]
        o = (z[0] + 31) // 32 * 32
        z[0] = o + 4 * int(np.prod(shape[1:]))
        assert z[0] <= z[1], (name, zone_name)
        return at(name, shape, dt, o)

    eraw = ([put("I", f"eraw{i}", [128, UE]) for i in range(3)] + [put("E", f"eraw{i}", [128, UE]) for i in range(3, 6)]
            + [put("A", "eraw6", [128, UE])] + [put("C", f"eraw{i}", [128, UE]) for i in range(7, 11)]
            + [put("B", "eraw11", [128, UE])])
    xn = at("xn", [128, NTILE, D], F32, place["xtok"])
    yg = at("yg", [128, 2 * NTILE, D], F32, place["Xh"])
    sqf = at("sqf", [128, D], F32, place["wraw"])
    xnT = [put("D", f"xnT{i}", [128, KC, 128]) for i in range(2)]
    xT = [put("D", f"xT{i}", [128, KC, CAP]) for i in range(2)]
    yout = [put("D", f"yout{i}", [CAP, D]) for i in range(2)]
    gfin = put("B", "gfin_", [128, D]) if False else put("D", "gfin", [128, D])
    xg = [put("B", f"xg{i}", [CAP, D]) for i in range(2)]
    gffn = put("F", "gffn", [128, D])
    sq = put("A", "sq", [128, 512])
    sil = [put("D", f"sil{i}", [128, 2 * CAP]) for i in range(2)]
    hT = [put("D", f"hT{i}", [128, 2, CAP]) for i in range(2)]
    rw = put("I", "rw", [128, KC, NG + NE])
    rb = put("I", "rb", [128, NG + NE])
    io64 = put("I", "io64", [128, CAP])
    w8 = put("I", "w8", [128, NPG])
    tok1 = put("I", "tok1", [128, NTILE])
    nst = put("I", "nst", [128, 2, NTILE])
    ctl = put("I", "ctl", [1, 32], I32)
    idx1 = [put("I", f"idx1_{i}", [CAP, 1], I32) for i in range(3)]
    idx = put("I", "idx", [CAP, NBLK], I32)
    slots = put("I", "slots", [128, 2 * NTILE], I32)
    GT = put("I", "GT", [128, 2, NTILE])
    triS = put("A", "triS", [128, 128])
    OH = put("B", "OH", [128, 2, NTILE, NE])
    RK = put("B", "RK", [128, NTILE + 1, NE])
    Lg = put("B", "Lg", [128, NTILE, NG + NE])
    W1 = put("B", "W1", [128, NTILE, NE])
    CW = put("B", "CW", [128, NCH, NE])
    OT = put("B", "OT", [128, 2, NTILE, NE])
    F4 = put("B", "F4", [128, NTILE, NG, NPG])
    rt = put("B", "rt", [128, 512])
    Aoh = put("B", "Aoh", [128, 2 * NTILE, CAP])
    Boh = put("B", "Boh", [128, 2 * NTILE, NBLK])
    VI = put("B", "VI", [CAP, NBLK])
    CO = put("B", "CO", [1, NOV, NE])

    ctx = ExitStack()
    with ctx:
        Z = ctx.enter_context(nc.psum_tensor("Z", [128, 2, 2, 512], F32))[:]
        M = ctx.enter_context(nc.psum_tensor("M", [128, 4, 512], F32))[:]

        def sem(name):
            return ctx.enter_context(nc.semaphore(name))

        x_in = [sem(f"x_in{t}") for t in range(NTILE)]
        stat_made = sem("stat_made")
        ws_tr = sem("ws_tr")
        ws_made = sem("ws_made")
        misc_in = sem("misc_in")
        consts = sem("consts")
        pool_step = sem("pool_step")
        g_in = sem("g_in")
        x_ss = sem("x_ss")
        x_sc = sem("x_sc")
        x_tr = sem("x_tr")
        x_hi = sem("x_hi")
        x_lo = sem("x_lo")
        raw_in = [sem(f"raw_in{i}") for i in range(3)]
        w_hi = sem("w_hi")
        w_lo = sem("w_lo")
        z_done = sem("z_done")
        ev_act = sem("ev_act")
        ev_dve = sem("ev_dve")
        side_mm = sem("side_mm")
        side_act = sem("side_act")
        side_dve = sem("side_dve")
        side_end = sem("side_end")
        a_step = sem("a_step")
        v_step = sem("v_step")
        c_in = [sem(f"c_in{i}") for i in range(3)]
        c_st = [sem(f"c_st{i}") for i in range(3)]
        c_free = sem("c_free")
        out_st = sem("out_st")
        root_in = sem("root_in")
        root_out = sem("root_out")
        xr_in = sem("xr_in")
        moe_consts = sem("moe_consts")
        xg_made = sem("xg_made")
        gfin_in = sem("gfin_in")
        zeroed = sem("zeroed")
        moe_made = sem("moe_made")
        n_set = sem("n_set")
        n_ss = sem("n_ss")
        n_xn = sem("n_xn")
        n_tr = sem("n_tr")
        n_ev = sem("n_ev")
        n_log = sem("n_log")
        xn_st = sem("xn_st")
        r_exp_in = sem("r_exp_in")
        r_exp_out = sem("r_exp_out")
        r_oh = sem("r_oh")
        r_rank = sem("r_rank")
        r_ab = sem("r_ab")
        r_idx = sem("r_idx")
        routed = sem("routed")
        ew_in = [sem(f"ew_in{i}") for i in range(3 * RING)]
        rows_in = [sem(f"rows_in{i}") for i in range(2)]
        xt_done = sem("xt_done")
        xt_ready = sem("xt_ready")
        up_done = sem("up_done")
        sil_ready = sem("sil_ready")
        h_ready = sem("h_ready")
        down_done = sem("down_done")
        y_copied = sem("y_copied")
        y_st = [sem(f"y_st{i}") for i in range(2)]
        o_w = sem("o_w")
        o_rows = sem("o_rows")
        o_st = sem("o_st")
        idx_step = sem("idx_step")
        moe_over = sem("moe_over")
        yg_in = [sem(f"yg_in{i}") for i in range(NTILE)]
        f_sum = sem("f_sum")
        f_ss = sem("f_ss")
        f_out = sem("f_out")
        out_y = sem("out_y")

        N_MOE = 1 + NG + 3
        N_MISC = 8

        def cpiece(ap, i):
            h, vh, bh = i // 4, i // 2 % 2, i % 2
            return ap[0, 4 * bh:4 * bh + 4, h, 128 * vh:128 * vh + 128, :].rearrange("b v d -> v b d")

        CIN = [E[:, 3, :], E[:, 4, :], E[:, 6, :]]
        CTS = [E[:, 7, :], E[:, 2, :]]
        KWM = E[0:NS, 1, :]
        KWS = E[0:NS, 5, :]

        def bank(c):
            return Z[:, c // 2, c % 2, :] if c < 4 else M[:, c - 4, :]

        def zz(t):
            return Z[:, t % 2, :, 0:HALF]

        def two(ap):
            return ap.rearrange("p (a b) -> p a b", a=2)

        def weight_src(i):
            kind, j = BLOCKS[i]
            if kind == "wo":
                half, q = j // 8, j % 8
                return w_out[0, 128 * q:128 * q + 128, 512 * half:512 * half + 512]
            if kind in ("pa", "pb"):
                w = p_a if kind == "pa" else p_b
                return w[0].rearrange("(c p) n -> p c n", p=128)[:, :, 128 * j:128 * j + 128]
            c0 = COL[kind] + 128 * j
            return w_in[0].rearrange("(c p) n -> p c n", p=128)[:, :, c0:c0 + 128]

        def bank_up(k):
            return Z[:, k, 0, 0:4 * CAP]

        def bank_xt():
            return Z[:, 0, 1, :]

        def bank_out(k):
            return M[0:CAP, 2 * k:2 * k + 2, :]

        def each_block(eng, body):
            for b in (0, 1):
                body(b, b)
            with eng.Fori(1, NE // 2 - 1) as i:
                for k in range(2):
                    body(i * 2 + k, k)
            for b in (NE - 2, NE - 1):
                body(b, b % 2)

        def one(ap, e):
            return ap[e] if isinstance(e, int) else ap[bass.ds(e, 1)].rearrange("o a b -> (o a) b")

        def up_rows(w, e):
            return one(w[0], e).rearrange("(p c) n -> p (c n)", c=KC)

        def down_rows(w, e):
            return one(w[0], e).rearrange("(j p) n -> p j n", p=128)

        def slot_rows(b):
            return slot_dram[bass.ds(b * CAP, CAP), :]

        def wsize(i):
            return 512 if BLOCKS[i][0] == "wo" else KC * 128

        block = ctx.enter_context(nc.Block())

        @block.sync
        def _(sp):
            for t in range(NTILE):
                src = x_prompt[0, 128 * t:128 * t + 128, :] if t < NCH else x_sample.rearrange("b t d -> (b t) d")
                sp.dma_start(xtok[0:rows(t), t, :], src).then_inc(x_in[t], 16)
            def load_expert(b, k, part):
                src = (up_rows(e_wg, b), up_rows(e_wu, b), down_rows(e_wd, b))[part]
                dst = eraw[3 * k + part]
                if part == 2:
                    dst = dst.rearrange("p (j n) -> p j n", j=2)
                sp.dma_start(dst, src).then_inc(ew_in[3 * k + part], 16)

            def ahead(u):
                if u == 0:
                    sp.wait_ge(side_end, len(STEPS))
                    sp.wait_ge(out_st, 16 * 9)
                    sp.wait_ge(ev_dve, ED[AT[("og", 7)] + 1])
                if u == 7:
                    sp.wait_ge(z_done, AT[("pa", 7)] + 1)
                if u == 11:
                    sp.wait_ge(z_done, NBK)
                load_expert(u // 3, u // 3, u % 3)

            ahead_at = {AT[("ga", 2)] + 2 * u: u for u in range(7)}
            ahead_at.update({WO0 + 4 + 2 * u: 7 + u for u in range(4)})
            assert max(ahead_at) < NBK
            for i in range(NBK):
                if i >= 3:
                    sp.wait_ge(w_lo, i - 2)
                n = wsize(i)
                dst = wraw[:, i % 3, 0:n]
                if n != 512:
                    dst = dst.rearrange("p (c n) -> p c n", c=KC)
                sp.dma_start(dst, weight_src(i)).then_inc(raw_in[i % 3], 16)
                if i in ahead_at:
                    ahead(ahead_at[i])
            ahead(3 * RING - 1)
            with sp.Fori(1, NE // RING) as i:
                for k in range(RING):
                    b = i * RING + k
                    sp.wait_ge(up_done, b - (RING - 1))
                    load_expert(b, k, 0)
                    load_expert(b, k, 1)
                    sp.wait_ge(down_done, b - (RING - 1))
                    load_expert(b, k, 2)
            sp.wait_ge(routed, 1)
            sp.wait_ge(down_done, NE)
            n_ov = sp.value_load(ctl[0:1, NOV:NOV + 1], min_val=0, max_val=NOV)
            with sp.If(n_ov > 0):
                with sp.Fori(0, n_ov) as o:
                    e = sp.value_load(ctl[0:1, bass.ds(o, 1)], min_val=0, max_val=NE - 1)
                    sp.wait_ge(down_done, o + NE)
                    sp.dma_start(eraw[0], up_rows(e_wg, e)).then_inc(o_w, 16)
                    sp.dma_start(eraw[1], up_rows(e_wu, e)).then_inc(o_w, 16)
                    sp.dma_start(eraw[2].rearrange("p (j n) -> p j n", j=2), down_rows(e_wd, e)).then_inc(o_w, 16)
            for t in range(NTILE):
                sp.wait_ge(f_out, t + 1)
                dst = y_p[0, 128 * t:128 * t + 128, :] if t < NCH else y_s.rearrange("b t d -> (b t) d")
                sp.dma_start(dst, yg[0:rows(t), t, :]).then_inc(out_y, 16)
            sp.wait_ge(out_y, 16 * NTILE)

        @block.gpsimd
        def _(pool):
            n = [0]

            def step(ins):
                ins.then_inc(pool_step, 1)
                n[0] += 1
                pool.wait_ge(pool_step, n[0])

            pool.dma_start(gB, norm_mix_g[0:1, :].partition_broadcast(128)).then_inc(g_in, 16)
            step(nc.gpsimd.memset(ident, 0.0))
            step(nc.gpsimd.affine_select(out=ident, in_=ident, compare_op=ALU.not_equal, fill=1.0, base=0,
                                         pattern=[[-1, 128]], channel_multiplier=1))
            step(nc.gpsimd.memset(ones, 1.0))
            step(nc.gpsimd.affine_select(out=tri, in_=ones, compare_op=ALU.is_ge, fill=0.0, base=0,
                                         pattern=[[1, 128]], channel_multiplier=-1))
            step(nc.gpsimd.affine_select(out=selb, in_=ones[0:NS, 0:NB], compare_op=ALU.is_ge, fill=0.0, base=0,
                                         pattern=[[-NL, NB]], channel_multiplier=1))
            step(nc.gpsimd.affine_select(out=selb, in_=selb, compare_op=ALU.is_ge, fill=0.0, base=NL - 1,
                                         pattern=[[NL, NB]], channel_multiplier=-1))
            bt = btri.rearrange("p (b t) -> p b t", t=NL)
            step(nc.gpsimd.affine_select(out=bt, in_=ones[0:NS, 0:NS].rearrange("p (b t) -> p b t", t=NL),
                                         compare_op=ALU.is_ge, fill=0.0, base=0,
                                         pattern=[[-NL, NB], [0, NL]], channel_multiplier=1))
            step(nc.gpsimd.affine_select(out=btri, in_=btri, compare_op=ALU.is_ge, fill=0.0, base=0,
                                         pattern=[[1, NS]], channel_multiplier=-1))
            step(nc.gpsimd.memset(selh, 1.0))
            step(nc.gpsimd.affine_select(out=selh, in_=selh, compare_op=ALU.is_equal, fill=0.0, base=0,
                                         pattern=[[-1, H], [0, 128]], channel_multiplier=1))
            step(nc.gpsimd.memset(epsc, EPS))
            step(nc.gpsimd.memset(gst, 1.0))
            step(nc.gpsimd.memset(CT, 0.0))
            step(nc.gpsimd.memset(nT, 0.0))
            nc.gpsimd.memset(sm, 0.0).then_inc(consts, 1)
            pool.wait_ge(consts, 1)
            pool.dma_start(wsraw, gm_ws[0].rearrange("g t s -> t g s")).then_inc(misc_in, 16)
            pool.dma_start(gmB, gm_norm_g.rearrange("o g d -> o (g d)").partition_broadcast(128)).then_inc(misc_in, 16)
            pool.dma_start(bsB.rearrange("p g t -> p (g t)"),
                           gm_bs.rearrange("o g t -> o (g t)").partition_broadcast(128)).then_inc(misc_in, 16)
            pool.dma_start(gbias[:, 0:1], ml_b_i.rearrange("o h -> h o")).then_inc(misc_in, 16)
            pool.dma_start(gbias[:, 1:2], ml_b_f.rearrange("o h -> h o")).then_inc(misc_in, 16)
            pool.dma_start(m0s, state_m[0].rearrange("b h -> h b"), allow_slow_non_contiguous=True).then_inc(misc_in, 16)
            pool.dma_start(n0s, state_n[0].rearrange("b h d -> b (h d)")).then_inc(misc_in, 16)
            pool.dma_start(mlg, ml_norm_g[0].rearrange("h (v p) -> p h v", p=128),
                           allow_slow_non_contiguous=True).then_inc(misc_in, 16)
            def c_load(i):
                pool.dma_start(CIN[i % 3].rearrange("v (b d) -> v b d", b=4), cpiece(state_C, i)) \
                    .then_inc(c_in[i % 3], 16)

            def c_store(i):
                pool.dma_start(cpiece(C_s, i), CIN[i % 3].rearrange("v (b d) -> v b d", b=4)) \
                    .then_inc(c_st[i % 3], 16)

            def c_out_pieces():
                for h in range(H):
                    pool.dma_start(C_p[0, 0, h].rearrange("(v p) d -> p v d", p=128),
                                   E[:, h // 2, 256 * (h % 2):256 * (h % 2) + 256]
                                   .rearrange("p (v d) -> p v d", v=2)).then_inc(out_st, 16)
                pool.dma_start(n_p[0, 0], E[0:H, 2, 0:128]).then_inc(out_st, 16)

            for s in STEPS:
                over = SN[s] + 1
                kind, what, j = s
                if kind == "s_c":
                    k = what
                    pool.wait_ge(side_end, SN[s])
                    if k >= 2:
                        c_store(k - 2)
                    if 2 <= k < 15:
                        pool.wait_ge(c_st[(k - 2) % 3], 16 * ((k - 2) // 3 + 1))
                    if k < 15:
                        c_load(k + 1)
                    if k == 16:
                        pool.wait_ge(side_end, over)
                        c_store(15)
                        for i in range(3):
                            pool.wait_ge(c_st[i], 16 * (6 if i == 0 else 5))
                        nc.gpsimd.memset(sm[0:1, 60:61], 0.0).then_inc(c_free, 1)
                elif kind == "tr" and what == "gv" and j == 7:
                    pool.wait_ge(side_end, over)
                    pool.dma_start(v_s[0].rearrange("b t g d -> (b t) (g d)"), xtok[0:NS, NCH, :]).then_inc(out_st, 16)
                elif kind == "rows":
                    pool.wait_ge(side_end, over)
                    pool.dma_start(m_s[0].rearrange("b h -> h b"), rws[:, 3, NL - 1:NS:NL],
                                   allow_slow_non_contiguous=True).then_inc(out_st, 16)
                    pool.dma_start(m_p.rearrange("o b h -> h (o b)"), rws[:, 3, T - 1:T]).then_inc(out_st, 16)
                elif kind == "s_pre":
                    pool.wait_ge(side_end, over)
                    c_load(0)
                elif kind == "s_den":
                    pool.wait_ge(side_end, over)
                    pool.dma_start(n_s[0].rearrange("b h d -> b (h d)"), n0s).then_inc(out_st, 16)
                elif kind == "c_out" and what == 1:
                    pool.wait_ge(side_end, over)
                    c_out_pieces()
            pool.dma_start(xres[:, 0:NCH, :], x_prompt[0].rearrange("(t p) d -> p t d", p=128)).then_inc(xr_in, 16)
            pool.dma_start(xres[0:NS, NCH, :], x_sample.rearrange("b t d -> (b t) d")).then_inc(xr_in, 16)
            pool.wait_ge(out_st, 16 * 9)
            pool.wait_ge(side_end, len(STEPS))
            nc.gpsimd.memset(nst, 1.0).then_inc(n_set, 1)
            pool.dma_start(rw[:, :, 0:NG], rc_w[0].rearrange("(c p) n -> p c n", p=128),
                           allow_slow_non_contiguous=True).then_inc(moe_consts, 16)
            for g in range(NG):
                pool.dma_start(rw[:, :, NG + NPG * g:NG + NPG * g + NPG],
                               rf_w[0, g].rearrange("(c p) n -> p c n", p=128)).then_inc(moe_consts, 16)
            pool.dma_start(rb[:, 0:NG], rc_b.partition_broadcast(128)).then_inc(moe_consts, 16)
            pool.dma_start(rb[:, NG:NG + NE], rf_b.rearrange("o g n -> o (g n)").partition_broadcast(128)) \
                .then_inc(moe_consts, 16)
            nc.gpsimd.iota(io64, pattern=[[1, CAP]], base=0, channel_multiplier=0, allow_small_or_imprecise_dtypes=True)
            nc.gpsimd.iota(w8, pattern=[[-1, NPG]], base=NPG, channel_multiplier=0, allow_small_or_imprecise_dtypes=True)
            nc.gpsimd.iota(tok1, pattern=[[128, NTILE]], base=1, channel_multiplier=1,
                           allow_small_or_imprecise_dtypes=True)
            pool.wait_ge(z_done, AT[("pa", 7)] + 1)
            pool.wait_ge(ev_act, EA[WO0])
            pool.wait_ge(ev_dve, ED[WO0])
            pool.dma_start(gffn, norm_ffn_g.partition_broadcast(128)).then_inc(moe_consts, 16)
            nc.gpsimd.affine_select(out=triS, in_=ones, compare_op=ALU.is_gt, fill=0.0, base=0,
                                    pattern=[[1, 128]], channel_multiplier=-1).then_inc(moe_made, 1)
            pool.wait_ge(z_done, NBK)
            for k in range(2):
                nc.gpsimd.memset(xg[k], 0.0).then_inc(xg_made, 1)
            pool.wait_ge(xg_made, 2)
            pool.dma_start(slot_dram[NE * CAP:NBLK * CAP, :].rearrange("(b q) d -> q b d", q=CAP),
                           xg[0].unsqueeze(1).broadcast_to([CAP, NOV, D])).then_inc(zeroed, 16)
            pool.dma_start(gfin, final_norm_g.rearrange("(o d) -> o d", o=1).partition_broadcast(128)).then_inc(gfin_in, 16)
            for t in range(NTILE):
                pool.wait_ge(n_xn, t + 1)
                pool.dma_start(xn_dram[128 * t:128 * t + rows(t), :], xn[0:rows(t), t, :]).then_inc(xn_st, 16)
            pool.wait_ge(xn_st, 16 * NTILE)
            pool.wait_ge(zeroed, 16)
            pool.wait_ge(routed, 1)

            def gather(b, k):
                if not (isinstance(b, int) and b < 2):
                    pool.wait_ge(xt_done, b - 1)
                step_r(nc.gpsimd.tensor_copy(idx1[k], idx[:, bass.ds(b, 1)]), b + 1)
                nc.gpsimd.indirect_dma_start(xg[k], None, xn_dram, bass.IndirectOffsetOnAxis(idx1[k], 0),
                                             bounds_check=T - 1, oob_is_err=False).then_inc(rows_in[k], 16)

            def step_r(ins, count):
                ins.then_inc(idx_step, 1)
                pool.wait_ge(idx_step, count)
                nc.gpsimd.tensor_tensor(stat[0:1, 23:24], ones[0:1, 0:1], ones[0:1, 0:1], ALU.mult)

            each_block(pool, gather)
            n_ov = pool.value_load(ctl[0:1, NOV:NOV + 1], min_val=0, max_val=NOV)
            pool.wait_ge(xt_done, NE)
            with pool.If(n_ov > 0):
                with pool.Fori(0, n_ov) as o:
                    pool.wait_ge(xt_done, o + NE)
                    step_r(nc.gpsimd.tensor_copy(idx1[2], idx[:, bass.ds(o + NE, 1)]), o + (NE + 1))
                    nc.gpsimd.indirect_dma_start(xg[0], None, xn_dram, bass.IndirectOffsetOnAxis(idx1[2], 0),
                                                 bounds_check=T - 1, oob_is_err=False).then_inc(o_rows, 16)
            pool.wait_ge(moe_over, 1)
            for t in range(NTILE):
                for j in range(2):
                    g = NTILE * j + t
                    nc.gpsimd.indirect_dma_start(yg[0:rows(t), g, :], None, slot_dram,
                                                 bass.IndirectOffsetOnAxis(slots[0:rows(t), g:g + 1], 0)) \
                        .then_inc(yg_in[t], 16)
            pool.wait_ge(moe_consts, 16 * N_MOE)

        def transpose(out, in_, k):
            return nc.tensor.transpose(out, in_, ident[0:k, 0:k])

        @block.tensor
        def _(pe):
            pe.wait_ge(consts, 1)
            for t in range(NCH):
                pe.wait_ge(x_sc, t + 1)
                for c in range(KC):
                    last = transpose(bank(c)[:, 128 * t:128 * t + 128], xtok[:, t, 128 * c:128 * c + 128], 128)
                    if t == NCH - 1:
                        last.then_inc(x_tr, 1)
            pe.wait_ge(x_sc, NTILE)
            pe.wait_ge(x_lo, 2)
            for c in range(KC):
                last = transpose(bank(0)[:, NS * c:NS * c + NS], xtok[0:NS, NCH, 128 * c:128 * c + 128], NS)
            last.then_inc(x_tr, 1)

            def position_weights(i):
                if i == 0:
                    pe.wait_ge(misc_in, 16 * N_MISC)
                    pe.wait_ge(x_lo, KC + 1)
                    for g in range(NG):
                        last = transpose(M[:, 3, 128 * g:128 * g + 128], wsraw[:, g, :], 128)
                    last.then_inc(ws_tr, 1)
                elif i == 1:
                    pe.wait_ge(ws_made, 1)
                    nc.tensor.matmul(M[0:NS, 0, 0:NG * NL], rep4, ws4, start=True, stop=True).then_inc(ws_tr, 1)

            def multiply(i):
                kind = BLOCKS[i][0]
                ah, al = (Hh, Hl) if kind in ("pa", "pb") else (Xh, Xl)
                if kind == "pb":
                    pe.wait_ge(ev_dve, ED[AT[("u", 7)] + 1])
                if kind == "pa":
                    pe.wait_ge(ev_dve, ED[AT[("og", 7)] + 1])
                hi = wh[:, i % 2, :].rearrange("p (c n) -> p c n", c=KC)
                lo = wl[:, i % 2, :].rearrange("p (c n) -> p c n", c=KC)
                steps = SIDE[i]
                at_piece = {KC * (m + 1) // (len(steps) + 1): st for m, st in enumerate(steps)}
                assert len(at_piece) == len(steps)
                for c in range(KC):
                    if i == 0:
                        pe.wait_ge(x_lo, max(3, c + 2))
                    if c in at_piece:
                        side(at_piece[c])
                    for f in range(2):
                        cols = slice(HALF * f, HALF * f + HALF)
                        z = zz(i)[:, f, :]
                        nc.tensor.matmul(z, hi[:, c, :], ah[:, c, cols], start=c == 0, stop=False)
                        nc.tensor.matmul(z, hi[:, c, :], al[:, c, cols], start=False, stop=False)
                    for f in range(2):
                        cols = slice(HALF * f, HALF * f + HALF)
                        last = nc.tensor.matmul(zz(i)[:, f, :], lo[:, c, :], ah[:, c, cols], start=False,
                                                stop=c == KC - 1)
                last.then_inc(z_done, 1)

            def multiply_out(i):
                half, q = BLOCKS[i][1] // 8, BLOCKS[i][1] % 8
                if half == 0:
                    pe.wait_ge(ev_dve, ED[WO0] - (3 if q < 7 else 0))
                for t in range(NTILE):
                    g = NTILE * half + t
                    out = bank((g + 2) % 8)
                    if q == 0 and g >= 8:
                        pe.wait_ge(ev_dve, ED[WO0 + 7] + 1 + g - 8)
                    cols = slice(tok_cols(t), tok_cols(t) + 128)
                    nc.tensor.matmul(out, Xh[:, q, cols], wh[:, i % 2, 0:512], start=q == 0, stop=False)
                    nc.tensor.matmul(out, Xl[:, q, cols], wh[:, i % 2, 0:512], start=False, stop=False)
                    last = nc.tensor.matmul(out, Xh[:, q, cols], wl[:, i % 2, 0:512], start=False, stop=q == 7)
                last.then_inc(z_done, 1)

            def rows_of(bank, lhs, rhs, n):
                for h in range(H):
                    nc.tensor.matmul(bank[:, n * h:n * h + n], lhs(h), rhs(h), start=True, stop=True)

            def side(step):
                kind, what, j = step
                n = SN[step]
                before = STEPS[n - 1] if n else None
                if before and before[0] == "rows":
                    pe.wait_ge(side_act, HA[before] + 1)
                elif before and before[0] == "tr" and hands(before)[0]:
                    pe.wait_ge(side_dve, HD[before] + 1)
                elif before and before[0] == "ml3":
                    pe.wait_ge(root_in, RN[before] + 1)
                elif before:
                    pe.wait_ge(side_end, n)
                if kind == "tr":
                    pe.wait_ge(ev_act, EA[AT[(what, j)]] + 1)
                    src = kT[:, j, :] if what == "k" else ev[:, AT[(what, j)] % 2, :]
                    for t in range(NCH):
                        transpose(M[:, 0, 128 * t:128 * t + 128], src[:, NS + 128 * t:NS + 128 * t + 128], 128)
                    last = transpose(M[0:NS, 1, 0:128], src[:, 0:NS], 128)
                elif kind == "rows":
                    pe.wait_ge(ev_act, EA[AT[("gates", 0)]] + 1)
                    for f in range(2):
                        last = nc.tensor.matmul(M[0:H, f, 0:HALF], ident[0:2 * H, H:2 * H],
                                                ev[0:2 * H, AT[("gates", 0)] % 2, HALF * f:HALF * f + HALF],
                                                start=True, stop=True)
                elif kind == "mix":
                    g = what // 2
                    for c in range(NCH):
                        nc.tensor.matmul(M[:, 0, 128 * c:128 * c + 128], xtok[:, c, 128 * what:128 * what + 128],
                                         wsT[:, g, :], start=True, stop=True)
                    last = nc.tensor.matmul(M[:, 1, 0:NS], xtok[0:NS, NCH, 128 * what:128 * what + 128],
                                            wsS[:, g, :], start=True, stop=True)
                elif kind == "s_pre":
                    rows_of(M[:, 0, :], lambda h: selh[:, h, :], lambda h: rws[:, 2, 0:NS], NS)
                    rows_of(M[:, 0, 4 * NS:], lambda h: selh[:, h, :], lambda h: m0s, NB)
                    rows_of(M[:, 1, :], lambda h: selh[:, h, :], lambda h: rws[:, 3, 0:NS], NS)
                    rows_of(M[0:NS, 2, :], lambda h: kT[:, h, 0:NS], lambda h: qT[:, h, 0:NS], NS)
                    transpose(M[0:NS, 3, 0:H], rws[:, 0, 0:NS], H)
                    transpose(M[0:NS, 3, H:2 * H], rws[:, 4, 0:NS], H)
                    transpose(M[0:NB, 3, 64:64 + H], rws[:, 4, NS:NS + NB], H)
                    for h in range(H):
                        last = transpose(M[:, 3, 16 + NB * h:16 + NB * h + NB], n0s[:, 128 * h:128 * h + 128], NB)
                elif kind == "s_c":
                    if what < 16:
                        pe.wait_ge(c_in[what % 3], 16 * (what // 3 + 1))
                        for b in range(4):
                            last = transpose(M[:, 0, 128 * b:128 * b + 128],
                                             CIN[what % 3][:, 128 * b:128 * b + 128], 128)
                    if what > 0:
                        i = what - 1
                        h, vh, bh = i // 4, i // 2 % 2, i % 2
                        v = vtok[0:NS, NCH, 256 * h + 128 * vh:256 * h + 128 * vh + 128]
                        num = M[:, 2, NS * (H * vh + h):NS * (H * vh + h) + NS]
                        if bh == 0:
                            nc.tensor.matmul(num, v, E[0:NS, 0, NS * h:NS * h + NS], start=True, stop=False)
                        for b in range(4):
                            c0 = 16 * bh + NL * b
                            nc.tensor.matmul(num[:, c0:c0 + NL], CTS[i % 2][:, 128 * b:128 * b + 128],
                                             E[:, 0, 128 + NS * h + c0:128 + NS * h + c0 + NL], start=False,
                                             stop=bh == 1 and b == 3)
                        last = nc.tensor.matmul(M[:, 1, :], v, KWM, start=True, stop=True)
                elif kind == "s_den":
                    nc.tensor.matmul(M[:, 3, 0:128], ones[0:NS, :], E[0:NS, 0, 0:128], start=True, stop=False)
                    nc.tensor.matmul(M[:, 3, 0:128], ones, E[:, 0, 256:384], start=False, stop=True)
                    for h in range(H):
                        last = nc.tensor.matmul(M[0:NB, 1, 128 * h:128 * h + 128], selb, KWS[:, 128 * h:128 * h + 128],
                                                start=True, stop=True)
                elif kind == "s_ss":
                    nc.tensor.matmul(M[:, 3, 0:128], ones, E[:, 6, 256:384], start=True, stop=False)
                    last = nc.tensor.matmul(M[:, 3, 0:128], ones, E[:, 6, 384:512], start=False, stop=True)
                elif kind == "ml1":
                    seg = slice(NS + 128 * what, NS + 128 * what + 128)
                    rows_of(M[:, 0, :], lambda h: selh[:, h, :], lambda h: rws[:, 2, seg], 128)
                    rows_of(M[:, 1, :], lambda h: selh[:, h, :], lambda h: rws[:, 3, seg], 128)
                    rows_of(M[:, 2, :], lambda h: kT[:, h, seg], lambda h: qT[:, h, seg], 128)
                    last = transpose(M[:, 3, 0:H], rws[:, 0, seg], H)
                elif kind == "ml2":
                    for vh in range(2):
                        for h in range(H):
                            o = M[:, vh, 128 * h:128 * h + 128]
                            nc.tensor.matmul(o, vtok[:, what, 256 * h + 128 * vh:256 * h + 128 * vh + 128],
                                             E[:, 0, 128 * h:128 * h + 128], start=True, stop=False)
                            nc.tensor.matmul(o, CT[:, h, 128 * vh:128 * vh + 128],
                                             E[:, 1, 128 * h:128 * h + 128], start=False, stop=True)
                    nc.tensor.matmul(M[:, 2, :], ones, E[:, 0, :], start=True, stop=False)
                    last = nc.tensor.matmul(M[:, 2, :], ones, E[:, 2, :], start=False, stop=True)
                elif kind == "ml3":
                    nc.tensor.matmul(M[:, 3, :], ones, E[:, 0, :], start=True, stop=False)
                    nc.tensor.matmul(M[:, 3, :], ones, E[:, 1, :], start=False, stop=True)
                    for h in range(H):
                        kw = E[:, 5, 128 * h:128 * h + 128]
                        nc.tensor.matmul(M[:, h // 2, 256 * (h % 2):256 * (h % 2) + 256], kw,
                                         vtok[:, what, 256 * h:256 * h + 256], start=True, stop=True)
                        last = nc.tensor.matmul(M[:, 2, h:h + 1], kw, ones[:, 0:1], start=True, stop=True)
                else:
                    for q in range(4):
                        h, vh = 2 * what + q // 2, q % 2
                        last = transpose(M[:, 0, 128 * q:128 * q + 128], CT[:, h, 128 * vh:128 * vh + 128], 128)
                    if what == 1:
                        last = transpose(M[0:H, 1, 0:128], nT, 128)
                last.then_inc(side_mm, 1)

            for i in range(NBK):
                if 2 <= i < WO0:
                    pe.wait_ge(ev_act, EA[i - 1])
                    pe.wait_ge(ev_dve, ED[i - 1])
                pe.wait_ge(w_lo, i + 1)
                if i >= WO0:
                    multiply_out(i)
                else:
                    multiply(i)
                    position_weights(i)

            pe.wait_ge(moe_consts, 16 * N_MOE)
            for t in range(NTILE + 1):
                if t < NTILE:
                    r = rows(t)
                    pe.wait_ge(n_xn, t + 1)
                    if t >= 2:
                        pe.wait_ge(n_ev, t - 1)
                    for c in range(KC):
                        last = transpose(Z[:, t % 2, c // 4, 128 * (c % 4):128 * (c % 4) + r],
                                         xn[0:r, t, 128 * c:128 * c + 128], r)
                    last.then_inc(n_tr, 1)
                if t > 0:
                    r = rows(t - 1)
                    pe.wait_ge(n_ev, t)
                    w = NG + NE
                    for c in range(KC):
                        last = nc.tensor.matmul(M[0:r, 0, w * (t - 1):w * t], xnT[(t - 1) % 2][:, c, 0:r], rw[:, c, :],
                                                start=c == 0, stop=c == KC - 1)
                    last.then_inc(n_log, 1)
            pe.wait_ge(r_oh, 1)
            RB = M[:, 1, :]
            c2 = CW.rearrange("p t e -> p (t e)")
            w2 = W1.rearrange("p t e -> p (t e)")
            n4 = NE * NCH
            nc.tensor.matmul(RB[:, 0:n4], triS, w2[:, 0:n4], start=True, stop=False)
            nc.tensor.matmul(RB[:, NE:n4], ones, c2[:, 0:n4 - NE], start=False, stop=True)
            nc.tensor.matmul(RB[0:NS, n4:n4 + NE], triS[0:NS, 0:NS], w2[0:NS, n4:n4 + NE], start=True, stop=False)
            nc.tensor.matmul(RB[0:NS, n4:n4 + NE], ones[:, 0:NS], c2[:, n4 - NE:n4], start=False, stop=True)
            nc.tensor.matmul(RB[:, n4 + NE:n4 + 2 * NE], ones[0:NS, :], w2[0:NS, n4:n4 + NE], start=True, stop=False)
            nc.tensor.matmul(RB[:, n4 + NE:n4 + 2 * NE], ones, c2[:, n4 - NE:n4], start=False, stop=True) \
                .then_inc(r_rank, 1)
            pe.wait_ge(r_ab, 1)
            for g in range(2 * NTILE):
                r = rows(g % NTILE)
                last = nc.tensor.matmul(M[0:CAP, 2, 0:NBLK], Aoh[0:r, g, :], Boh[0:r, g, :], start=g == 0,
                                        stop=g == 2 * NTILE - 1)
            last.then_inc(r_idx, 1)

            def tokens_by_feature(src):
                s = src.rearrange("q (p c) -> q p c", c=KC)
                for c in range(KC):
                    out = bank_xt()[:, CAP * c:CAP * c + CAP]
                    last = nc.tensor.matmul(out, s[:, :, c], ident[0:CAP, 0:CAP], start=True, stop=True) if c == 0 \
                        else transpose(out, s[:, :, c], CAP)
                return last

            def up(k, x, raws):
                for gu in range(2):
                    w = raws[gu].rearrange("p (c n) -> p c n", c=KC)
                    for j in range(2):
                        z = bank_up(k)[:, CAP * (2 * gu + j):CAP * (2 * gu + j) + CAP]
                        for c in range(KC):
                            last = nc.tensor.matmul(z, w[:, c, 128 * j:128 * j + 128], x[:, c, :], start=c == 0,
                                                    stop=c == KC - 1)
                return last

            def down(k, h, raw):
                for f in range(2):
                    for j in range(2):
                        last = nc.tensor.matmul(bank_out(k)[:, f, :], h[:, j, :],
                                                raw[:, D * j + 512 * f:D * j + 512 * f + 512], start=j == 0, stop=j == 1)
                return last

            def up_of(b, r, landed):
                pe.wait_ge(xt_ready, b + 1)
                pe.wait_ge(ew_in[3 * r], landed)
                pe.wait_ge(ew_in[3 * r + 1], landed)
                up(r % 2, xT[r % 2], eraw[3 * r:3 * r + 2]).then_inc(up_done, 1)

            def tokens_of(b, k, landed):
                pe.wait_ge(rows_in[k], landed)
                if not (isinstance(b, int) and b < 1):
                    pe.wait_ge(xt_ready, b)
                tokens_by_feature(xg[k]).then_inc(xt_done, 1)

            def down_of(b, r, landed):
                pe.wait_ge(h_ready, b + 1)
                pe.wait_ge(ew_in[3 * r + 2], landed)
                if not (isinstance(b, int) and b < 2):
                    pe.wait_ge(y_copied, b - 1)
                down(r % 2, hT[r % 2], eraw[3 * r + 2]).then_inc(down_done, 1)

            pe.wait_ge(routed, 1)
            tokens_of(0, 0, 16)
            up_of(0, 0, 16)
            tokens_of(1, 1, 16)
            for b in range(1, RING):
                up_of(b, b, 16)
                tokens_of(b + 1, (b + 1) % 2, 16 * ((b + 1) // 2 + 1))
                down_of(b - 1, b - 1, 16)
            with pe.Fori(1, NE // RING - 1) as i:
                for r in range(RING):
                    b = i * RING + r
                    up_of(b, r, i * 16 + 16)
                    tokens_of(b + 1, (r + 1) % 2, i * 32 + 16 * ((r + 1) // 2 + 1))
                    down_of(b - 1, (r - 1) % RING, i * 16 + (16 if r else 0))
            last_round = 16 * (NE // RING)
            for b in range(NE - RING, NE):
                up_of(b, b % RING, last_round)
                if b + 1 < NE:
                    tokens_of(b + 1, (b + 1) % 2, 16 * ((b + 1) // 2 + 1))
                down_of(b - 1, (b - 1) % RING, last_round if b % RING else last_round - 16)
            down_of(NE - 1, RING - 1, last_round)
            n_ov = pe.value_load(ctl[0:1, NOV:NOV + 1], min_val=0, max_val=NOV)
            with pe.If(n_ov > 0):
                with pe.Fori(0, n_ov) as o:
                    pe.wait_ge(o_rows, o * 16 + 16)
                    tokens_by_feature(xg[0]).then_inc(xt_done, 1)
                    pe.wait_ge(xt_ready, o + (NE + 1))
                    pe.wait_ge(o_w, o * 48 + 48)
                    up(0, xT[0], eraw[0:2]).then_inc(up_done, 1)
                    pe.wait_ge(h_ready, o + (NE + 1))
                    pe.wait_ge(y_copied, o + NE)
                    down(0, hT[0], eraw[2]).then_inc(down_done, 1)

        @block.scalar
        def _(act):
            n = [0]

            def step(ins):
                ins.then_inc(a_step, 1)
                n[0] += 1
                act.wait_ge(a_step, n[0])

            A = nc.scalar.activation

            def split(i):
                act.wait_ge(raw_in[i % 3], 16 * (i // 3 + 1))
                if i >= 2:
                    act.wait_ge(z_done, i - 1)
                m = wsize(i)
                A(wh[:, i % 2, 0:m], wraw[:, i % 3, 0:m], ACT.Copy).then_inc(w_hi, 1)

            def root(x, k):
                act.wait_ge(root_in, k + 1)
                step(A(x, x, ACT.Ln, bias=epsc[0:x.shape[0], :]))
                A(x, x, ACT.Exp, scale=-0.5).then_inc(root_out, 1)

            act.wait_ge(stat_made, 1)
            for t in range(NTILE):
                r = rows(t)
                act.wait_ge(x_in[t], 16)
                A(junk[0:r, :], xtok[0:r, t, :], ACT.Square, accum_out=stat[0:r, 8 + t:9 + t]).then_inc(x_ss, 1)
                act.wait_ge(x_ss, t + 1)
            split(0)
            for c in X_ORDER:
                act.wait_ge(x_tr, KC + 1 if c == KC else c + 1)
                if c == KC:
                    A(Xh[:, :, 0:NS], bank(0)[:, 0:KC * NS].rearrange("p (c n) -> p c n", c=KC), ACT.Copy).then_inc(x_hi, 1)
                else:
                    A(Xh[:, c, NS:T], bank(c), ACT.Copy).then_inc(x_hi, 1)

            def squares(half):
                act.wait_ge(n_set, 1)
                for t in range(NTILE):
                    r = rows(t)
                    act.wait_ge(ev_dve, ED[WO0 + 7 + 8 * half] + t + 1)
                    x = xres[0:r, t, 512 * half:512 * half + 512]
                    A(sq[0:r, :], x, ACT.Square, accum_out=nst[0:r, half, t:t + 1]).then_inc(n_ss, 1)
                    act.wait_ge(n_ss, NTILE * half + t + 1)

            def evacuate(i):
                kind, j = BLOCKS[i]
                if kind == "wo":
                    if j == 9:
                        squares(0)
                    return
                e = ev[:, i % 2, :]
                if kind == "pa" and j == 7:
                    for c in range(KC):
                        act.wait_ge(ev_dve, ED[i] if c < 7 else ED[i] + 9)
                        if c == 0:
                            act.wait_ge(z_done, AT[("ga", 7)] + 1)
                        A(Xh[:, c, :], sumT[:, c, :], ACT.Copy).then_inc(ev_act, 1)
                    return
                if kind in ("pa", "pb"):
                    return
                act.wait_ge(z_done, i + 1)
                if kind == "q":
                    A(two(qT[:, j, :]), zz(i), ACT.Copy, scale=float(DQK) ** -0.5).then_inc(ev_act, 1)
                elif kind == "k":
                    A(two(kT[:, j, :]), zz(i), ACT.Copy).then_inc(ev_act, 1)
                else:
                    if i >= 2:
                        act.wait_ge(ev_dve, ED[i] if BLOCKS[i - 1][0] in ("pa", "pb") else ED[i - 1])
                    if kind in ("v", "gv", "gates"):
                        before = BLOCKS[i - 2]
                        tr = ("rows", 0, 0) if before[0] == "gates" else ("tr",) + before
                        if tr in SN:
                            act.wait_ge(side_mm, SN[tr] + 1)
                        func = ACT.Gelu_apprx_tanh if kind == "gv" else ACT.Copy
                        r = 2 * H if kind == "gates" else 128
                        A(two(e[0:r]), zz(i)[0:r], func).then_inc(ev_act, 1)
                    elif kind == "u":
                        if j < 2:
                            act.wait_ge(side_mm, SN[("tr", "gv", 6 + j)] + 1)
                        A(two(e), zz(i), ACT.Gelu_apprx_tanh).then_inc(ev_act, 1)
                        act.wait_ge(ev_dve, ED[i] + 1)
                        A(Hh[:, j, :], e, ACT.Copy).then_inc(ev_act, 1)
                    elif kind in ("gb", "ga"):
                        A(two(e), zz(i), ACT.Tanh, scale=0.5).then_inc(ev_act, 1)
                    elif kind == "og":
                        A(two(e), zz(i), ACT.Tanh, scale=0.5).then_inc(ev_act, 1)
                        act.wait_ge(ev_dve, ED[i] + 1)
                        act.wait_ge(z_done, AT[("pb", 7)] + 1)
                        A(Hh[:, j, :], e, ACT.Copy).then_inc(ev_act, 1)

            def side(st):
                kind, what, j = st
                a, d = HA[st], HD[st]
                if hands(st)[0] == 0 and st not in RN:
                    return
                act.wait_ge(side_mm, SN[st] + 1)
                if kind == "tr":
                    act.wait_ge(side_dve, d + 1)
                    g = j // 2
                    for t in range(NTILE):
                        r = rows(t)
                        last = A(gjunk[0:r, :], xtok[0:r, t, 256 * g:256 * g + 256], ACT.Square,
                                 accum_out=gst[0:r, t:t + 1])
                        if t < NTILE - 1:
                            step(last)
                    last.then_inc(side_act, 1)
                elif kind == "s_ss":
                    root(E[:, 1, 0:128], RN[st])
                elif kind == "ml3":
                    root(E[:, 0, :], RN[st])
                elif kind == "rows":
                    step(A(two(rws[:, 1, :]), M[0:H, 0:2, 0:HALF], ACT.Identity, bias=gbias[:, 1:2]))
                    A(rws[:, 0, :], ev[0:H, AT[("gates", 0)] % 2, :], ACT.Identity, bias=gbias[:, 0:1]) \
                        .then_inc(side_act, 1)
                    step(A(rws[:, 4, :], rws[:, 1, :], ACT.Abs))
                    step(A(rws[:, 4, :], rws[:, 4, :], ACT.Exp, scale=-1.0))
                    A(rws[:, 4, :], rws[:, 4, :], ACT.Ln, bias=1.0).then_inc(side_act, 1)
                elif kind == "s_pre":
                    A(E[:, 0, 384:512], M[:, 1, 0:128], ACT.Exp, scale=-1.0)
                    act.wait_ge(side_dve, d + 1)
                    A(E[0:NS, 0, 0:128], E[0:NS, 0, 0:128], ACT.Exp, scale=-1.0)
                    A(E[:, 0, 128:256], E[:, 0, 128:256], ACT.Exp).then_inc(side_act, 1)
                    A(sm[0:NS, 4:8], sm[0:NS, 4:8], ACT.Exp)
                    A(sm[0:NB, 48:52], sm[0:NB, 48:52], ACT.Exp)
                    A(sm[:, 96:128], sm[:, 96:128], ACT.Exp).then_inc(side_act, 1)
                elif kind == "s_c":
                    if what < 16:
                        A(CTS[what % 2], M[:, 0, :], ACT.Copy).then_inc(side_act, 1)
                    else:
                        A(CTS[0][:, 0:1], sm[:, 0:1], ACT.Copy).then_inc(side_act, 1)
                elif kind == "s_den":
                    act.wait_ge(c_free, 1)
                    A(E[:, 6, 0:256], M[:, 2, 0:256], ACT.Copy)
                    A(E[:, 6, 256:512], M[:, 2, 0:256], ACT.Square).then_inc(side_act, 1)
                elif kind == "ml1":
                    act.wait_ge(side_end, SN[st])
                    A(E[:, 4, :], M[:, 1, :], ACT.Exp, scale=-1.0)
                    act.wait_ge(side_dve, d + 1)
                    A(E[:, 0, :], E[:, 0, :], ACT.Exp, scale=-1.0)
                    A(sm[:, 4:12], sm[:, 4:12], ACT.Exp).then_inc(side_act, 1)
                    for h in range(H):
                        last = A(E[:, 1, 128 * h:128 * h + 128], M[:, 0, 128 * h:128 * h + 128], ACT.Exp,
                                 scale=-1.0, bias=sm[:, 12 + h:13 + h])
                    last.then_inc(side_act, 1)
                elif kind == "ml2":
                    A(E[:, 2:4, :], M[:, 0:2, :], ACT.Copy)
                    A(E[:, 0:2, :], M[:, 0:2, :], ACT.Square).then_inc(side_act, 1)

            for i in range(NBK):
                if i + 1 < NBK:
                    split(i + 1)
                for s in SIDE[i]:
                    side(s)
                evacuate(i)

            squares(1)
            for t in range(NTILE):
                r = rows(t)
                act.wait_ge(n_tr, t + 1)
                if t >= 2:
                    act.wait_ge(n_log, t - 1)
                A(xnT[t % 2][:, :, 0:r], Z[:, t % 2, :, :].rearrange("p a (c n) -> p (a c) n", n=128)[:, :, 0:r],
                  ACT.Copy).then_inc(n_ev, 1)
            act.wait_ge(r_exp_in, 1)
            A(rt[:, 0:25], rt[:, 0:25], ACT.Exp).then_inc(r_exp_out, 1)

            def silu_of(b, k):
                act.wait_ge(up_done, b + 1)
                if not (isinstance(b, int) and b < 2):
                    act.wait_ge(h_ready, b - 1)
                A(sil[k], bank_up(k)[:, 0:2 * CAP], ACT.Silu).then_inc(sil_ready, 1)

            def out_of(b, k, stored=None):
                act.wait_ge(down_done, b + 1)
                if stored is not None:
                    act.wait_ge(y_st[k], stored)
                A(yout[k].rearrange("q (f n) -> q f n", f=2), bank_out(k), ACT.Copy).then_inc(y_copied, 1)
                act.wait_ge(y_copied, b + 1)
                act.dma_start(slot_rows(b), yout[k]).then_inc(y_st[k], 16)

            act.wait_ge(routed, 1)
            silu_of(0, 0)
            silu_of(1, 1)
            out_of(0, 0)
            silu_of(2, 0)
            out_of(1, 1)
            silu_of(3, 1)
            out_of(2, 0, 16)
            with act.Fori(2, NE // 2) as i:
                silu_of(i * 2, 0)
                out_of(i * 2 - 1, 1, i * 16 - 16)
                silu_of(i * 2 + 1, 1)
                out_of(i * 2, 0, i * 16)
            out_of(NE - 1, 1, 8 * NE - 16)
            n_ov = act.value_load(ctl[0:1, NOV:NOV + 1], min_val=0, max_val=NOV)
            for k in range(2):
                act.wait_ge(y_st[k], 8 * NE)
            with act.If(n_ov > 0):
                with act.Fori(0, n_ov) as o:
                    act.wait_ge(up_done, o + (NE + 1))
                    A(sil[0], bank_up(0)[:, 0:2 * CAP], ACT.Silu).then_inc(sil_ready, 1)
                    act.wait_ge(down_done, o + (NE + 1))
                    A(yout[0].rearrange("q (f n) -> q f n", f=2), bank_out(0), ACT.Copy).then_inc(y_copied, 1)
                    act.wait_ge(y_copied, o + (NE + 1))
                    act.dma_start(slot_rows(o + NE), yout[0]).then_inc(o_st, 16)
                    act.wait_ge(o_st, o * 16 + 16)
            A(nst[:, 1, 0:1], nst[:, 1, 0:1], ACT.Copy).then_inc(moe_over, 1)

            for t in range(NTILE):
                r = rows(t)
                act.wait_ge(f_sum, t + 1)
                A(sqf[0:r, :], xres[0:r, t, :], ACT.Square, accum_out=nst[0:r, 1, t:t + 1]).then_inc(f_ss, 1)
                act.wait_ge(f_ss, t + 1)

        @block.vector
        def _(dve):
            n = [0]
            V = nc.vector

            def step(ins):
                ins.then_inc(v_step, 1)
                n[0] += 1
                dve.wait_ge(v_step, n[0])

            def split(i):
                dve.wait_ge(w_hi, i + 1)
                m = wsize(i)
                V.tensor_tensor(wl[:, i % 2, 0:m], wraw[:, i % 3, 0:m], wh[:, i % 2, 0:m].bitcast(F32),
                                ALU.subtract).then_inc(w_lo, 1)

            def root_of(x, inv):
                y, u = newt[0:x.shape[0], 0, 0:x.shape[1]], newt[0:x.shape[0], 1, 0:x.shape[1]]
                step(V.tensor_scalar(x, x, inv, EPS, ALU.mult, ALU.add))
                step(V.tensor_scalar(y.bitcast(I32), x.bitcast(I32), -0.5, float(0x5f3759df), ALU.mult, ALU.add))
                for k in range(4):
                    step(V.tensor_tensor(u, y, y, ALU.mult))
                    step(V.scalar_tensor_tensor(u, u, -0.5, x, ALU.mult, ALU.mult))
                    out = x if k == 3 else y
                    step(V.scalar_tensor_tensor(out, u, 1.5, y, ALU.add, ALU.mult))

            V.memset(stat, 1.0).then_inc(stat_made, 1)
            dve.wait_ge(x_ss, NTILE)
            root_of(stat[:, 8:8 + NTILE], 1.0 / D)
            dve.wait_ge(g_in, 16)
            for t in range(NTILE):
                r = rows(t)
                V.scalar_tensor_tensor(xtok[0:r, t, :], xtok[0:r, t, :], stat[0:r, 8 + t:9 + t], gB[0:r, :],
                                       ALU.mult, ALU.mult).then_inc(x_sc, 1)
            split(0)
            for m, c in enumerate(X_ORDER):
                dve.wait_ge(x_hi, m + 1)
                if c == KC:
                    V.tensor_tensor(Xl[:, :, 0:NS], bank(0)[:, 0:KC * NS].rearrange("p (c n) -> p c n", c=KC),
                                    Xh[:, :, 0:NS].bitcast(F32), ALU.subtract).then_inc(x_lo, 1)
                else:
                    V.tensor_tensor(Xl[:, c, NS:T], bank(c), Xh[:, c, NS:T].bitcast(F32), ALU.subtract).then_inc(x_lo, 1)

            def position_weights(i):
                dve.wait_ge(ws_tr, i + 1)
                if i == 0:
                    dve.wait_ge(consts, 1)
                    V.tensor_tensor(wsT, M[:, 3, :].rearrange("p (g t) -> p g t", g=NG),
                                    tri.unsqueeze(1).broadcast_to([128, NG, 128]), ALU.mult)
                    step(V.tensor_copy(rep4.rearrange("p (b t) -> p b t", t=NL),
                                       ident[0:NL, 0:NL].unsqueeze(1).broadcast_to([NL, NB, NL])))
                    V.tensor_copy(ws4.rearrange("p (g t) -> p g t", g=NG), wsT[0:NL, :, 0:NL]).then_inc(ws_made, 1)
                else:
                    for g in range(NG):
                        V.tensor_tensor(wsS[:, g, :].rearrange("p (b t) -> p b t", t=NL),
                                        M[0:NS, 0, NL * g:NL * g + NL].unsqueeze(1).broadcast_to([NS, NB, NL]),
                                        btri.rearrange("p (b t) -> p b t", t=NL), ALU.mult)

            def hm(c, h, vh):
                if c == NCH:
                    return vtok[:, NCH, NS * (H * vh + h):NS * (H * vh + h) + NS]
                return vtok[:, c, 128 * (H * vh + h):128 * (H * vh + h) + 128]

            def evacuate(i):
                kind, j = BLOCKS[i]
                e = ev[:, i % 2, :]
                if kind == "u":
                    dve.wait_ge(ev_act, EA[i] + 1)
                    V.tensor_tensor(e, e, mixT[:, j, :], ALU.mult).then_inc(ev_dve, 1)
                    dve.wait_ge(ev_act, EA[i] + 2)
                    V.tensor_tensor(Hl[:, j, :], e, Hh[:, j, :].bitcast(F32), ALU.subtract).then_inc(ev_dve, 1)
                elif kind in ("gb", "ga"):
                    dve.wait_ge(ev_act, EA[i] + 1)
                    V.tensor_scalar(e, e, 0.5, 0.5, ALU.mult, ALU.add).then_inc(ev_dve, 1)
                elif kind == "pb":
                    dve.wait_ge(z_done, i + 1)
                    dve.wait_ge(ev_dve, ED[i])
                    if j == 0:
                        dve.wait_ge(out_st, 16 * 3)
                    V.tensor_tensor(two(sumT[:, j, :]), zz(i), two(ev[:, (i - 1) % 2, :]), ALU.mult) \
                        .then_inc(ev_dve, 1)
                elif kind == "pa":
                    g = ev[:, (i - 1) % 2, :]
                    d0 = ED[i]

                    def rest(c):
                        dve.wait_ge(ev_act, EA[i] + c + 1)
                        V.tensor_tensor(Xl[:, c, :], sumT[:, c, :], Xh[:, c, :].bitcast(F32), ALU.subtract) \
                            .then_inc(ev_dve, 1)

                    if j == 7:
                        for c in range(KC - 1):
                            rest(c)
                        d0 += KC - 1
                    dve.wait_ge(z_done, i + 1)
                    dve.wait_ge(ev_dve, d0)
                    V.tensor_tensor(two(g), zz(i), two(g), ALU.mult).then_inc(ev_dve, 1)
                    dve.wait_ge(ev_dve, d0 + 1)
                    V.tensor_tensor(sumT[:, j, :], sumT[:, j, :], g, ALU.add).then_inc(ev_dve, 1)
                    if j == 7:
                        rest(KC - 1)
                elif kind == "og":
                    h, vh = j // 2, j % 2
                    dve.wait_ge(ev_act, EA[i] + 1)
                    step(V.tensor_scalar(e, e, 0.5, 0.5, ALU.mult, ALU.add))
                    V.scalar_tensor_tensor(e[:, NS:T].rearrange("p (c n) -> p c n", c=NCH),
                                           e[:, NS:T].rearrange("p (c n) -> p c n", c=NCH), mlg[:, h, vh:vh + 1],
                                           vtok[:, 0:NCH, 128 * (H * vh + h):128 * (H * vh + h) + 128],
                                           ALU.mult, ALU.mult)
                    V.scalar_tensor_tensor(e[:, 0:NS], e[:, 0:NS], mlg[:, h, vh:vh + 1], hm(NCH, h, vh),
                                           ALU.mult, ALU.mult).then_inc(ev_dve, 1)
                    dve.wait_ge(ev_act, EA[i] + 2)
                    V.tensor_tensor(Hl[:, j, :], e, Hh[:, j, :].bitcast(F32), ALU.subtract).then_inc(ev_dve, 1)
                elif kind == "wo":
                    half, q = j // 8, j % 8
                    if q < 7:
                        return
                    dve.wait_ge(z_done, i + 1)
                    dve.wait_ge(xr_in, 32)
                    for t in range(NTILE):
                        g = NTILE * half + t
                        out = bank((g + 2) % 8)
                        r = rows(t)
                        xs = xres[0:r, t, 512 * half:512 * half + 512]
                        V.tensor_tensor(xs, xs, out[0:r, :], ALU.add).then_inc(ev_dve, 1)

            def normalise(st, R, NUM, S, out, w):
                step(V.scalar_tensor_tensor(S, M[:, 3, 0:w], 1.0 / DV, R, ALU.mult, ALU.mult))
                V.tensor_tensor(S, S, R, ALU.mult).then_inc(root_in, 1)
                dve.wait_ge(root_out, RN[st] + 1)
                step(V.tensor_tensor(S, S, R, ALU.mult))
                return V.tensor_tensor(out, NUM, S.unsqueeze(1).broadcast_to([128, 2, w]), ALU.mult)

            def side(st):
                kind, what, j = st
                a, d = HA[st], HD[st]
                dve.wait_ge(side_mm, SN[st] + 1)
                if kind == "tr":
                    dst, w = (ktok, 512) if what == "k" else (vtok, D) if what == "v" else (xtok, D)
                    V.tensor_copy(dst[:, 0:NCH, 128 * j:128 * j + 128], M[:, 0, :].rearrange("p (t n) -> p t n", t=NCH))
                    last = V.tensor_copy(dst[0:NS, NCH, 128 * j:128 * j + 128], M[0:NS, 1, 0:128])
                    if hands(st)[0]:
                        last.then_inc(side_dve, 1)
                        dve.wait_ge(side_act, a + 1)
                        g = j // 2
                        root_of(gst, 1.0 / 256)
                        for t in range(NTILE):
                            r = rows(t)
                            s = xtok[0:r, t, 256 * g:256 * g + 256]
                            last = V.scalar_tensor_tensor(s, s, gst[0:r, t:t + 1], gmB[0:r, 256 * g:256 * g + 256],
                                                          ALU.mult, ALU.mult)
                elif kind == "rows":
                    LI, LF, MM, mm, tmp = (rws[:, r, :] for r in range(5))
                    dve.wait_ge(side_act, a + 2)
                    step(V.scalar_tensor_tensor(LF, LF, 0.0, tmp, ALU.min, ALU.subtract))
                    zero = CT[0:H, 0, 0:128]
                    for c in range(NCH):
                        seg = slice(NS + 128 * c, NS + 128 * c + 128)
                        V.tensor_tensor_scan(LF[:, seg], LF[:, seg], zero, 0.0, ALU.add, ALU.add)
                    ls = LF[:, 0:NS].rearrange("p (b t) -> p b t", t=NL)
                    for t in range(1, NL):
                        step(V.tensor_tensor(ls[:, :, t], ls[:, :, t], ls[:, :, t - 1], ALU.add))
                    step(V.tensor_tensor(LI, LI, LF, ALU.subtract))
                    for c in range(NCH):
                        seg = slice(NS + 128 * c, NS + 128 * c + 128)
                        m0 = 0.0 if c == 0 else mm[:, NS + 128 * c - 1:NS + 128 * c]
                        step(V.tensor_tensor_scan(MM[:, seg], LI[:, seg], LI[:, seg], m0, ALU.max, ALU.max))
                        step(V.tensor_tensor(mm[:, seg], MM[:, seg], LF[:, seg], ALU.add))
                    Ms, As = (r[:, 0:NS].rearrange("p (b t) -> p b t", t=NL) for r in (MM, LI))
                    step(V.tensor_tensor(Ms[:, :, 0], As[:, :, 0], m0s, ALU.max))
                    for t in range(1, NL):
                        step(V.tensor_tensor(Ms[:, :, t], As[:, :, t], Ms[:, :, t - 1], ALU.max))
                    V.tensor_tensor(mm[:, 0:NS], MM[:, 0:NS], LF[:, 0:NS], ALU.add)
                    last_m = Ms[:, :, NL - 1:NL].broadcast_to([H, NB, NL])
                    V.tensor_tensor(tmp[:, 0:NS].rearrange("p (b t) -> p b t", t=NL), As, last_m, ALU.subtract)
                    last = V.tensor_tensor(tmp[:, NS:NS + NB], m0s, Ms[:, :, NL - 1], ALU.subtract)
                elif kind == "mix":
                    g = what // 2
                    V.tensor_tensor(mixT[:, what, NS:T].rearrange("p (c n) -> p c n", c=NCH),
                                    M[:, 0, :].rearrange("p (c n) -> p c n", c=NCH),
                                    bsB[:, g, :].unsqueeze(1).broadcast_to([128, NCH, 128]), ALU.add)
                    last = V.tensor_tensor(mixT[:, what, 0:NS].rearrange("p (b t) -> p b t", b=NB),
                                           M[:, 1, 0:NS].rearrange("p (b t) -> p b t", b=NB),
                                           bsB[:, g, 0:NL].unsqueeze(1).broadcast_to([128, NB, NL]), ALU.add)
                elif kind == "s_pre":
                    V.tensor_copy(sm[0:NS, 0:8], M[0:NS, 3, 0:8])
                    V.tensor_copy(sm[:, 16:48], M[:, 3, 16:48])
                    V.tensor_copy(sm[0:NB, 48:52], M[0:NB, 3, 64:68])
                    step(V.tensor_copy(sm[:, 128:160], M[:, 0, 128:160]))
                    for h in range(H):
                        V.tensor_scalar(E[0:NS, 0, NS * h:NS * h + NS], M[0:NS, 0, NS * h:NS * h + NS],
                                        sm[0:NS, h:h + 1], 0.0, ALU.subtract, ALU.max)
                    Mb = M[:, 0, 0:128].rearrange("p (x t) -> p x t", t=NL)
                    V.tensor_tensor(E[:, 0, 128:256].rearrange("p (x t) -> p x t", t=NL),
                                    sm[:, 128:160].unsqueeze(2).broadcast_to([128, H * NB, NL]), Mb, ALU.subtract)
                    V.tensor_tensor(sm[:, 96:128], sm[:, 128:160], Mb[:, :, NL - 1], ALU.subtract) \
                        .then_inc(side_dve, 1)
                    dve.wait_ge(side_act, a + 2)
                    P = E[0:NS, 0, 0:128].rearrange("p (h t) -> p h t", h=H)
                    step(V.tensor_tensor(P, P, btri.unsqueeze(1).broadcast_to([NS, H, NS]), ALU.mult))
                    V.tensor_tensor(E[0:NS, 0, 0:128], E[0:NS, 0, 0:128], M[0:NS, 2, 0:128], ALU.mult)
                    q = E[:, 0, 128:256].rearrange("p (h t) -> p h t", h=H)
                    step(V.tensor_tensor(q, q, qT[:, :, 0:NS], ALU.mult))
                    V.tensor_tensor(E[:, 0, 256:384].rearrange("p (x t) -> p x t", t=NL),
                                    E[:, 0, 128:256].rearrange("p (x t) -> p x t", t=NL),
                                    sm[:, 16:48].unsqueeze(2).broadcast_to([128, H * NB, NL]), ALU.mult)
                    for h in range(H):
                        last = V.tensor_scalar(KWS[:, 128 * h:128 * h + 128], ktok[0:NS, NCH, 128 * h:128 * h + 128],
                                               sm[0:NS, 4 + h:5 + h], None, ALU.mult)
                elif kind == "s_c":
                    dve.wait_ge(side_act, a + 1)
                    if what > 0:
                        i = what - 1
                        h, bh = i // 4, i % 2
                        for b in range(4):
                            s = CIN[i % 3][:, 128 * b:128 * b + 128]
                            x = 96 + NB * h + 4 * bh + b
                            last = V.scalar_tensor_tensor(s, s, sm[:, x:x + 1], M[:, 1, 128 * b:128 * b + 128],
                                                          ALU.mult, ALU.add)
                    if what < 16:
                        h, bh = what // 4, what % 2
                        last = V.tensor_tensor(KWM.rearrange("p (b d) -> p b d", b=4),
                                               KWS[:, 128 * h:128 * h + 128].unsqueeze(1).broadcast_to([NS, 4, 128]),
                                               selb[:, 4 * bh:4 * bh + 4].unsqueeze(2).broadcast_to([NS, 4, 128]),
                                               ALU.mult)
                elif kind == "s_den":
                    R = E[:, 0, 384:512]
                    step(V.tensor_tensor(R, M[:, 3, 0:128], R, ALU.max))
                    step(V.scalar_tensor_tensor(R, M[:, 3, 0:128], -1.0, R, ALU.mult, ALU.max))
                    V.reciprocal(R, R)
                    dve.wait_ge(side_act, a + 1)
                    for h in range(H):
                        x = n0s[:, 128 * h:128 * h + 128]
                        last = V.scalar_tensor_tensor(x, x, sm[0:NB, 48 + h:49 + h], M[0:NB, 1, 128 * h:128 * h + 128],
                                                      ALU.mult, ALU.add)
                elif kind == "s_ss":
                    last = normalise(st, E[:, 0, 384:512], E[:, 6, 0:256].rearrange("p (v x) -> p v x", v=2),
                                     E[:, 1, 0:128], vtok[:, NCH, 0:256].rearrange("p (v x) -> p v x", v=2), 128)
                elif kind == "ml1":
                    step(V.tensor_copy(sm[:, 0:4], M[:, 3, 0:4]))
                    for h in range(H):
                        V.tensor_scalar(E[:, 0, 128 * h:128 * h + 128], M[:, 0, 128 * h:128 * h + 128],
                                        sm[:, h:h + 1], 0.0, ALU.subtract, ALU.max)
                    ML = M[:, 0, 127:512:128]
                    if what == 0:
                        V.memset(sm[:, 12:16], 0.0)
                    else:
                        V.tensor_copy(sm[:, 12:16], sm[:, 52:56])
                    V.tensor_tensor(sm[:, 4:8], sm[:, 0:4], ML, ALU.subtract)
                    m0 = sm[:, 56:60] if what == 0 else sm[:, 52:56]
                    V.tensor_tensor(sm[:, 8:12], m0, ML, ALU.subtract).then_inc(side_dve, 1)
                    dve.wait_ge(side_act, a + 1)
                    P = E[:, 0, :].rearrange("p (h t) -> p h t", h=H)
                    step(V.tensor_tensor(P, P, tri.unsqueeze(1).broadcast_to([128, H, 128]), ALU.mult))
                    V.tensor_tensor(E[:, 0, :], E[:, 0, :], M[:, 2, :], ALU.mult)
                    for h in range(H):
                        V.tensor_scalar(E[:, 5, 128 * h:128 * h + 128], ktok[:, what, 128 * h:128 * h + 128],
                                        sm[:, 4 + h:5 + h], None, ALU.mult)
                    dve.wait_ge(side_act, a + 2)
                    seg = slice(NS + 128 * what, NS + 128 * what + 128)
                    V.tensor_copy(sm[:, 52:56], M[:, 1, 127:512:128])
                    q = E[:, 1, :].rearrange("p (h t) -> p h t", h=H)
                    step(V.tensor_tensor(q, q, qT[:, :, seg], ALU.mult))
                    for h in range(H):
                        last = V.tensor_scalar(E[:, 2, 128 * h:128 * h + 128], E[:, 1, 128 * h:128 * h + 128],
                                               nT[:, h:h + 1], None, ALU.mult)
                elif kind == "ml2":
                    R = E[:, 4, :]
                    step(V.tensor_tensor(R, M[:, 2, :], R, ALU.max))
                    step(V.scalar_tensor_tensor(R, M[:, 2, :], -1.0, R, ALU.mult, ALU.max))
                    dve.wait_ge(side_act, a + 1)
                    last = V.reciprocal(R, R)
                elif kind == "ml3":
                    for h in range(H):
                        V.scalar_tensor_tensor(CT[:, h, :], CT[:, h, :], sm[:, 8 + h:9 + h],
                                               M[:, h // 2, 256 * (h % 2):256 * (h % 2) + 256], ALU.mult, ALU.add)
                    step(V.tensor_tensor(nT, nT, sm[:, 8:12], ALU.mult))
                    V.tensor_tensor(nT, nT, M[:, 2, 0:H], ALU.add)
                    last = normalise(st, E[:, 4, :], E[:, 2:4, :], E[:, 0, :],
                                     vtok[:, what, :].rearrange("p (v x) -> p v x", v=2), 512)
                else:
                    last = V.tensor_copy(E[:, what, :], M[:, 0, :])
                    if what == 1:
                        last = V.tensor_copy(E[0:H, 2, 0:128], M[0:H, 1, 0:128])
                last.then_inc(side_end, 1)
                dve.wait_ge(side_end, SN[st] + 1)

            for i in range(NBK):
                if i + 1 < NBK:
                    split(i + 1)
                if i in (1, 2):
                    position_weights(i - 1)
                for s in SIDE[i]:
                    side(s)
                evacuate(i)

            dve.wait_ge(moe_consts, 16 * N_MOE)
            dve.wait_ge(moe_made, 1)
            dve.wait_ge(n_ss, 2 * NTILE)
            step(V.tensor_tensor(nst[:, 0, :], nst[:, 0, :], nst[:, 1, :], ALU.add))
            root_of(nst[:, 0, :], 1.0 / D)
            for t in range(NTILE):
                r = rows(t)
                V.scalar_tensor_tensor(xn[0:r, t, :], xres[0:r, t, :], nst[0:r, 0, t:t + 1], gffn[0:r, :],
                                       ALU.mult, ALU.mult).then_inc(n_xn, 1)
            step(V.memset(Lg, 0.0))
            dve.wait_ge(n_log, NTILE)
            nw = NG + NE
            L4 = M[:, 0, 0:NCH * nw].rearrange("p (t n) -> p t n", n=nw)
            V.tensor_tensor(Lg[:, 0:NCH, :], L4, rb.unsqueeze(1).broadcast_to([128, NCH, nw]), ALU.add)
            step(V.tensor_tensor(Lg[0:NS, NCH, :], M[0:NS, 0, NCH * nw:NTILE * nw], rb[0:NS, :], ALU.add))
            G = Lg[:, :, 0:NG]
            fine = Lg[:, :, NG:nw].rearrange("p t (g e) -> p t g e", g=NG)

            cur_rt = [32]

            def tmp(*shape):
                m = int(np.prod(shape))
                o = cur_rt[0]
                cur_rt[0] += m
                assert cur_rt[0] <= 512
                ap = rt[:, o:o + m]
                if len(shape) == 2:
                    ap = ap.rearrange("p (a b) -> p a b", a=shape[0])
                return ap

            def spread(x, m):
                return x.unsqueeze(2).broadcast_to([128, x.shape[1], m])

            def first_max(x, m, mx, hot, work):
                step(V.tensor_reduce(mx, x, AX, ALU.max))
                step(V.tensor_tensor(work, x, spread(mx, m), ALU.is_ge))
                step(V.tensor_tensor(work, work, w8[:, NPG - m:NPG].unsqueeze(1).broadcast_to([128, NTILE, m]), ALU.mult))
                best = tmp(NTILE)
                step(V.tensor_reduce(best, work, AX, ALU.max))
                step(V.tensor_tensor(hot, work, spread(best, m), ALU.is_equal))

            gm, m1, m2 = tmp(NTILE), tmp(NTILE), tmp(NTILE)
            ohg, gwork = tmp(NTILE, NG), tmp(NTILE, NG)
            first_max(G, NG, gm, ohg, gwork)
            V.tensor_tensor(rt[:, 0:20].rearrange("p (t g) -> p t g", g=NG), G, spread(gm, NG), ALU.subtract)
            step(V.tensor_tensor(F4, fine, ohg.unsqueeze(3).broadcast_to([128, NTILE, NG, NPG]), ALU.mult))
            fs, oh1, oh2, fwork = tmp(NTILE, NPG), tmp(NTILE, NPG), tmp(NTILE, NPG), tmp(NTILE, NPG)
            step(V.tensor_tensor(fs, F4[:, :, 0, :], F4[:, :, 1, :], ALU.add))
            for g in range(2, NG):
                step(V.tensor_tensor(fs, fs, F4[:, :, g, :], ALU.add))
            first_max(fs, NPG, m1, oh1, fwork)
            step(V.scalar_tensor_tensor(fs, oh1, -BIG, fs, ALU.mult, ALU.add))
            first_max(fs, NPG, m2, oh2, fwork)
            V.tensor_tensor(rt[:, 20:25], m2, m1, ALU.subtract).then_inc(r_exp_in, 1)
            for j, hot in enumerate((oh1, oh2)):
                for t in range(NTILE):
                    last = V.tensor_tensor(OH[:, j, t, :].rearrange("p (g e) -> p g e", g=NG),
                                           ohg[:, t, :].unsqueeze(2).broadcast_to([128, NG, NPG]),
                                           hot[:, t, :].unsqueeze(1).broadcast_to([128, NG, NPG]), ALU.mult)
            step(last)
            step(V.tensor_tensor(W1, OH[:, 0], OH[:, 1], ALU.add))
            step(V.tensor_copy(CW[:, 0, :], W1[:, 0, :]))
            for t in range(1, NCH):
                last = V.tensor_tensor(CW[:, t, :], CW[:, t - 1, :], W1[:, t, :], ALU.add)
                if t < NCH - 1:
                    step(last)
            last.then_inc(r_oh, 1)
            dve.wait_ge(r_exp_out, 1)
            se = tmp(NTILE)
            step(V.tensor_reduce(se, rt[:, 0:20].rearrange("p (t g) -> p t g", g=NG), AX, ALU.add))
            step(V.scalar_tensor_tensor(GT[:, 0, :], rt[:, 20:25], 1.0, se, ALU.add, ALU.mult))
            step(V.reciprocal(GT[:, 0, :], GT[:, 0, :]))
            V.tensor_tensor(GT[:, 1, :], GT[:, 0, :], rt[:, 20:25], ALU.mult)
            dve.wait_ge(r_rank, 1)
            n4 = NE * NCH
            V.memset(RK[:, NCH, :], 0.0)
            step(V.tensor_copy(RK[:, 0:NCH, :], M[:, 1, 0:n4].rearrange("p (t e) -> p t e", e=NE)))
            V.tensor_copy(RK[0:NS, NCH, :], M[0:NS, 1, n4:n4 + NE])
            step(V.tensor_copy(RK[:, NTILE, :], M[:, 1, n4 + NE:n4 + 2 * NE]))
            cn = RK[:, NTILE, :]
            nb, S, zero = tmp(NE), tmp(NE), tmp(NE)
            V.memset(zero, 0.0)
            step(V.tensor_scalar(nb, cn, float(CAP), None, ALU.is_gt))
            for q in range(2, MAXK + 1):
                step(V.scalar_tensor_tensor(nb, cn, float(CAP * q), nb, ALU.is_gt, ALU.add))
            step(V.tensor_tensor_scan(S, nb, zero, 0.0, ALU.add, ALU.add))
            step(V.tensor_tensor(nb, S, nb, ALU.subtract))

            def pick(out, x):
                step(V.tensor_tensor(OT, OH, x, ALU.mult))
                step(V.tensor_reduce(out.rearrange("p (j t) -> p j t", j=2), OT, AX, ALU.add))

            n10 = 2 * NTILE
            full = [128, 2, NTILE, NE]
            rank, base, ex, kb, hit = tmp(n10), tmp(n10), tmp(n10), tmp(n10), tmp(n10)
            pick(rank, RK[:, 0:NTILE, :].unsqueeze(1).broadcast_to(full))
            pick(base, nb.unsqueeze(1).unsqueeze(1).broadcast_to(full))
            pick(ex, io64[:, 0:NE].unsqueeze(1).unsqueeze(1).broadcast_to(full))
            step(V.tensor_scalar(kb, rank, float(CAP), None, ALU.is_ge))
            V.tensor_copy(hit, kb)
            for q in range(2, MAXK + 1):
                step(V.scalar_tensor_tensor(kb, rank, float(CAP * q), kb, ALU.is_ge, ALU.add))
            step(V.tensor_tensor(base, base, kb, ALU.add))
            step(V.tensor_tensor(base, base, ex, ALU.subtract))
            step(V.scalar_tensor_tensor(base, base, float(NE - 1), hit, ALU.add, ALU.mult))
            step(V.tensor_tensor(base, base, ex, ALU.add))
            step(V.scalar_tensor_tensor(rank, kb, float(-CAP), rank, ALU.mult, ALU.add))
            step(V.scalar_tensor_tensor(ex, base, float(CAP), rank, ALU.mult, ALU.add))
            V.tensor_copy(slots, ex)
            V.tensor_tensor(Aoh, io64.unsqueeze(1).broadcast_to([128, n10, CAP]), spread(rank, CAP), ALU.is_equal)
            step(V.tensor_tensor(Boh, io64[:, 0:NBLK].unsqueeze(1).broadcast_to([128, n10, NBLK]), spread(base, NBLK),
                                 ALU.is_equal))
            for j in range(2):
                last = V.tensor_tensor(Boh[:, NTILE * j:NTILE * j + NTILE, :], Boh[:, NTILE * j:NTILE * j + NTILE, :],
                                       spread(tok1, NBLK), ALU.mult)
            last.then_inc(r_ab, 1)
            step(V.tensor_tensor(CO, S[0:1].unsqueeze(1).broadcast_to([1, NOV, NE]),
                                 io64[0:1, 0:NOV].unsqueeze(2).broadcast_to([1, NOV, NE]), ALU.is_le))
            own = tmp(NOV)
            step(V.tensor_reduce(own[0:1], CO, AX, ALU.add))
            V.tensor_scalar(ctl[:, 0:NOV], own[0:1], float(NE - 1), None, ALU.min)
            V.tensor_copy(ctl[:, NOV:NOV + 1], S[0:1, NE - 1:NE])
            dve.wait_ge(r_idx, 1)
            step(V.tensor_scalar(VI, M[0:CAP, 2, 0:NBLK], 0.0, float(4 * T), ALU.is_equal, ALU.mult))
            step(V.scalar_tensor_tensor(VI, M[0:CAP, 2, 0:NBLK], -1.0, VI, ALU.add, ALU.add))
            step(V.tensor_copy(idx, VI))
            V.tensor_copy(rt[0:1, 0:1], rt[0:1, 0:1]).then_inc(routed, 1)

            def tokens(k):
                return V.tensor_copy(xT[k], bank_xt().rearrange("p (c n) -> p c n", c=KC))

            def gated(k):
                return V.tensor_tensor(hT[k].rearrange("p j n -> p (j n)"), sil[k], bank_up(k)[:, 2 * CAP:4 * CAP], ALU.mult)

            def tokens_of(b, k):
                dve.wait_ge(xt_done, b + 1)
                if not (isinstance(b, int) and b < 2):
                    dve.wait_ge(up_done, b - 1)
                tokens(k).then_inc(xt_ready, 1)

            def gated_of(b, k):
                dve.wait_ge(sil_ready, b + 1)
                if not (isinstance(b, int) and b < 2):
                    dve.wait_ge(down_done, b - 1)
                gated(k).then_inc(h_ready, 1)

            tokens_of(0, 0)
            tokens_of(1, 1)
            gated_of(0, 0)
            with dve.Fori(1, NE // 2) as i:
                tokens_of(i * 2, 0)
                gated_of(i * 2 - 1, 1)
                tokens_of(i * 2 + 1, 1)
                gated_of(i * 2, 0)
            gated_of(NE - 1, 1)
            n_ov = dve.value_load(ctl[0:1, NOV:NOV + 1], min_val=0, max_val=NOV)
            with dve.If(n_ov > 0):
                with dve.Fori(0, n_ov) as o:
                    dve.wait_ge(xt_done, o + (NE + 1))
                    dve.wait_ge(up_done, o + NE)
                    tokens(0).then_inc(xt_ready, 1)
                    dve.wait_ge(sil_ready, o + (NE + 1))
                    gated(0).then_inc(h_ready, 1)

            dve.wait_ge(gfin_in, 16)
            for t in range(NTILE + 1):
                if t < NTILE:
                    r = rows(t)
                    x = xres[0:r, t, :]
                    dve.wait_ge(yg_in[t], 32)
                    step(V.scalar_tensor_tensor(x, yg[0:r, t, :], GT[0:r, 0, t:t + 1], x, ALU.mult, ALU.add))
                    V.scalar_tensor_tensor(x, yg[0:r, NTILE + t, :], GT[0:r, 1, t:t + 1], x, ALU.mult, ALU.add) \
                        .then_inc(f_sum, 1)
                if t > 0:
                    u = t - 1
                    r = rows(u)
                    dve.wait_ge(f_ss, u + 1)
                    root_of(nst[0:r, 1, u:u + 1], 1.0 / D)
                    V.scalar_tensor_tensor(yg[0:r, u, :], xres[0:r, u, :], nst[0:r, 1, u:u + 1], gfin[0:r, :],
                                           ALU.mult, ALU.mult).then_inc(f_out, 1)


_INS = ["x_prompt", "x_sample", "state_mlstm_C", "state_mlstm_n", "state_mlstm_m", "norm_mix_g", "w_in", "ml_b_i",
        "ml_b_f", "ml_norm_g", "gm_norm_g", "gm_ws", "gm_bs", "p_a", "p_b", "w_out", "norm_ffn_g", "rc_w", "rc_b",
        "rf_w", "rf_b", "e_wg", "e_wu", "e_wd", "final_norm_g"]
_OUTS = [(1, NP_TOK, D), (NB, NL, D), (1, 1, H, DV, DQK), (1, 1, H, DQK), (1, 1, H), (1, NB, H, DV, DQK),
         (1, NB, H, DQK), (1, NB, H), (1, NB, NL, 4, 256)]


def kernel(**inputs):
    import concourse.bacc as bacc
    from concourse.bass_utils import run_bass_kernel_spmd

    nc = bacc.Bacc("TRN2", target_bir_lowering=False, num_devices=1)
    arrays, args = {}, []
    for name in _INS:
        a = np.ascontiguousarray(inputs[name])
        arrays[f"in_{name}"] = a
        args.append(nc.dram_tensor(f"in_{name}", a.shape, mybir.dt.from_np(a.dtype), kind="ExternalInput").ap())
    for i, shape in enumerate(_OUTS):
        args.append(nc.dram_tensor(f"out_{i}", shape, F32, kind="ExternalOutput").ap())
    build(nc, *args)
    r = run_bass_kernel_spmd(nc, [arrays], core_ids=[0])
    return tuple(r.results[0][f"out_{i}"] for i in range(len(_OUTS)))
```

```python
from contextlib import ExitStack

import numpy as np

import concourse.bass as bass
from concourse import mybir

ALU = mybir.AluOpType
ACT = mybir.ActivationFunctionType
F32 = mybir.dt.float32
F32R = mybir.dt.float32r
I32 = mybir.dt.int32
U32 = mybir.dt.uint32
AX = mybir.AxisListType.X

D = 1024
NP_TOK, NB, NL = 512, 8, 4
NS = NB * NL
T = NS + NP_TOK
HALF = T // 2
NCH = NP_TOK // 128
H, DQK, DV = 4, 128, 256
KC = D // 128
NE, NG, NPG, EH = 32, 4, 8, 256
EPS = 1e-6
CAP = 64
MAXK = T // CAP
NOV = (2 * T) // CAP
NBLK = NE + NOV
BIG = 1.0e30
COL = {"q": 0, "k": 512, "v": 1024, "og": 2048, "gates": 3072, "u": 3080, "gv": 4104, "ga": 5128, "gb": 6152}
NTILE = NCH + 1


UE = 2048
RING = 4


def tok_cols(t):
    return NS + 128 * t if t < NCH else 0


def rows(t):
    return 128 if t < NCH else NS


BLOCKS = ([("q", j) for j in range(4)] + [("k", j) for j in range(4)] + [("gates", 0)]
          + [("v", j) for j in range(8)] + [("gv", j) for j in range(8)] + [("u", j) for j in range(8)]
          + [b for j in range(8) for b in (("gb", j), ("pb", j))] + [("og", j) for j in range(8)]
          + [b for j in range(8) for b in (("ga", j), ("pa", j))]
          + [("wo", i) for i in range(16)])
NBK = len(BLOCKS)
AT = {b: i for i, b in enumerate(BLOCKS)}
BY_ACT = ("q", "k", "v", "gv", "u", "gb", "og", "ga", "gates")
WO0 = AT[("wo", 0)]

X_ORDER = (0, 1, 2, 3, KC, 4, 5, 6, 7)

SIDE = {i: [] for i in range(NBK)}


def _place_side_steps():
    def place(block, *steps):
        SIDE[block] += [step + (0,) * (3 - len(step)) for step in steps]

    for j in range(4):
        place(AT[("k", j)] + 1, ("tr", "k", j))
    place(AT[("gates", 0)] + 1, ("rows", 0))
    place(AT[("v", 2)], ("tr", "v", 0), ("tr", "v", 1))
    for j in range(2, 8):
        place(AT[("v", j)] + 1, ("tr", "v", j))
        if j == 6:
            place(AT[("v", 7)], ("s_pre", 0))
    for j in range(8):
        place(AT[("gv", j)] + 1, *([("mix", 0)] if j == 7 else []), ("s_c", j), ("tr", "gv", j))
    for j in range(1, 8):
        place(AT[("u", j)], ("mix", j), ("s_c", 7 + j))
    k = AT[("gb", 0)]
    place(k, ("s_c", 15), ("s_c", 16))
    k += 1
    place(k, ("s_den", 0), ("s_ss", 0))
    for c in range(NCH):
        for stage in ("ml1", "ml2", "ml3"):
            k += 1
            place(k, (stage, c))
    for i in range(2):
        k += 1
        place(k, ("c_out", i))
    assert k < AT[("og", 0)]


def piece_of(step, m, n):
    kind, what, j = step
    if kind in ("ml1", "ml2", "ml3", "s_pre"):
        return {"ml1": 1, "ml2": 5, "ml3": 4, "s_pre": 5}[kind]
    if kind == "mix":
        return 3 if what else 1
    if kind == "s_c" and what < 15:
        return 3 if what < 7 else 4 if what == 7 else 7
    if kind == "tr" and what == "gv":
        return 7
    return KC * (m + 1) // (n + 1)


_place_side_steps()
STEPS = [s for i in range(NBK) for s in SIDE[i]]
SN = {s: n for n, s in enumerate(STEPS)}


def hands(step):
    kind, what, j = step
    if kind == "tr":
        return (1, 1) if what == "gv" and j % 2 else (0, 0)
    return {"rows": (2, 0), "mix": (0, 0), "s_pre": (2, 1), "s_c": (1, 0), "s_den": (1, 0), "s_ss": (0, 0),
            "ml1": (2, 1), "ml2": (1, 0), "ml3": (0, 0), "c_out": (0, 0)}[kind]


def evacs(kind, j):
    if kind == "pa" and j == 7:
        return 8, 10
    if kind == "wo":
        return 0, 2 * NTILE if j % 8 == 7 else 0
    return {"q": (1, 0), "k": (1, 0), "v": (1, 0), "gv": (1, 0), "gates": (1, 0), "u": (2, 2), "og": (2, 2),
            "gb": (1, 1), "ga": (1, 1), "pb": (0, 1), "pa": (0, 2)}[kind]


HA, HD, _a, _d = {}, {}, 0, 0
for _s in STEPS:
    HA[_s], HD[_s] = _a, _d
    _a, _d = _a + hands(_s)[0], _d + hands(_s)[1]
EA, ED, _a, _d = [], [], 0, 0
for _b in BLOCKS:
    EA.append(_a)
    ED.append(_d)
    _a, _d = _a + evacs(*_b)[0], _d + evacs(*_b)[1]
EA.append(_a)
ED.append(_d)


ROOTS = [s for s in STEPS if s[0] in ("s_ss", "ml3")]
RN = {s: n for n, s in enumerate(ROOTS)}


def build(nc, x_prompt, x_sample, state_C, state_n, state_m, norm_mix_g, w_in, ml_b_i, ml_b_f, ml_norm_g,
          gm_norm_g, gm_ws, gm_bs, p_a, p_b, w_out, norm_ffn_g, rc_w, rc_b, rf_w, rf_b, e_wg, e_wu, e_wd,
          final_norm_g, y_p, y_s, C_p, n_p, m_p, C_s, n_s, m_s, v_s):
    place = {}
    cur = [(nc.sbuf_base + 63) // 64 * 64]

    def at(name, shape, dt, offset):
        return nc.alloc_sbuf_tensor_at(name, shape, dt, offset=offset)[:]

    def take(name, shape, dt=F32):
        place[name] = cur[0]
        cur[0] += (4 * int(np.prod(shape[1:])) + 31) // 32 * 32
        return at(name, shape, dt, place[name])

    ident = take("ident", [128, 128])
    ones = take("ones", [128, 128])
    epsc = take("epsc", [128, 1])
    stat = take("stat", [128, 24])
    newt = take("newt", [128, 2, NTILE])
    xtok = take("xtok", [128, NTILE, D])
    mixer0 = cur[0]
    tri = take("tri", [128, 128])
    btri = take("btri", [NS, NS])
    selb = take("selb", [NS, NB])
    selh = take("selh", [H, H, 128])
    mlg = take("mlg", [128, H, 2])
    gbias = take("gbias", [H, 2])
    CT = take("CT", [128, H, DV])
    nT = take("nT", [128, H])
    wsT = take("wsT", [128, NG, 128])
    wsS = take("wsS", [NS, NG, NS])
    rep4 = take("rep4", [NL, NS])
    ws4 = take("ws4", [NL, NG * NL])
    gst = take("gst", [128, NTILE])
    sm = take("sm", [128, 160])
    m0s = take("m0s", [H, NB])
    n0s = take("n0s", [NB, H * DQK])
    Xh = take("Xh", [128, KC, T], F32R)
    Xl = take("Xl", [128, KC, T], F32R)
    Hh = take("Hh", [128, KC, T], F32R)
    Hl = take("Hl", [128, KC, T], F32R)
    wraw = take("wraw", [128, 3, KC * 128])
    wh = take("wh", [128, 2, KC * 128], F32R)
    wl = take("wl", [128, 2, KC * 128], F32R)
    ev = take("ev", [128, 2, T])
    rws = take("rws", [H, 5, T])
    E = take("E", [128, 8, 512])
    qT = take("qT", [128, H, T])
    kT = take("kT", [128, H, T])
    ktok = take("ktok", [128, NTILE, 512])
    vtok = take("vtok", [128, NTILE, D])
    assert cur[0] <= nc.sbuf_usable_end, (cur[0], nc.sbuf_usable_end)
    sumT = at("sumT", [128, KC, T], F32, place["xtok"])
    xres = at("xres", [128, NTILE, D], F32, place["qT"])
    mixT = at("mixT", [128, KC, T], F32, place["Hl"])
    junk = at("junk", [128, D], F32, place["Hl"])
    gB = at("gB", [128, D], F32, place["Hl"] + 4 * D)
    gmB = at("gmB", [128, D], F32, place["Hh"] + 5 * 4 * T)
    bsB = at("bsB", [128, NG, 128], F32, place["Hh"] + 7 * 4 * T)
    gjunk = at("gjunk", [128, 256], F32, place["Hh"] + 4 * 4 * T)
    wsraw = at("wsraw", [128, NG, 128], F32, place["Hh"])

    xn_dram = nc.dram_tensor("xn_rows", (T, D), F32).ap()
    slot_dram = nc.dram_tensor("slot_rows", (NBLK * CAP, D), F32).ap()
    zone = {"A": [mixer0, place["Xh"]], "B": [place["Xh"], place["Hh"]], "C": [place["Hh"], place["wraw"]],
            "D": [place["wraw"], place["ev"]], "F": [place["ev"], place["rws"]], "E": [place["rws"], place["qT"]],
            "I": [place["qT"] + 4 * NTILE * D, cur[0]]}

    def put(zone_name, name, shape, dt=F32):
        z = zone[zone_name]
        o = (z[0] + 31) // 32 * 32
        z[0] = o + 4 * int(np.prod(shape[1:]))
        assert z[0] <= z[1], (name, zone_name)
        return at(name, shape, dt, o)

    eup = [put(z, f"eup{i}", [128, 2, KC, EH]) for i, z in enumerate("IECC")]
    edn = [put(z, f"edn{i}", [128, 2, D]) for i, z in enumerate("IEAB")]
    xn = at("xn", [128, NTILE, D], F32, place["xtok"])
    dnh = at("dnh", [128, 2, D], F32R, place["xtok"])
    dnl = at("dnl", [128, 2, D], F32R, place["xtok"] + 4 * 2 * D)
    yg = at("yg", [128, 2 * NTILE, D], F32, place["Xh"])
    sqf = at("sqf", [128, D], F32, place["wraw"])
    xnT = [at(f"xnT{i}", [128, 4, 128], F32, place["wraw"] + 4 * (1024 * i + 512)) for i in range(2)]
    zone["D"][0] += 2 * 4 * D
    xT = [put("D", f"xT{i}", [128, KC, CAP]) for i in range(2)]
    yout = [put("D", f"yout{i}", [CAP, D]) for i in range(2)]
    gfin = put("B", "gfin_", [128, D]) if False else put("D", "gfin", [128, D])
    xg = [put("B", f"xg{i}", [CAP, D]) for i in range(2)]
    gffn = put("F", "gffn", [128, D])
    sq = put("A", "sq", [128, 512])
    sil = [put("D", f"sil{i}", [CAP, EH]) for i in range(2)]
    hid = [put("B", f"hid{i}", [CAP, EH]) for i in range(2)]
    hTh = put("B", "hTh", [128, 2, 128], F32R)
    hTl = put("B", "hTl", [128, 2, 128], F32R)
    rw = put("I", "rw", [128, KC, NG + NE])
    rb = put("I", "rb", [128, NG + NE])
    io64 = put("I", "io64", [128, CAP])
    caps = put("I", "caps", [128, MAXK])
    w8 = put("I", "w8", [128, NPG])
    tok1 = put("I", "tok1", [128, NTILE])
    nst = put("I", "nst", [128, 2, NTILE])
    ctl = put("I", "ctl", [1, 32], I32)
    idx1 = [put("I", f"idx1_{i}", [CAP, 1], I32) for i in range(3)]
    idx = put("I", "idx", [CAP, NBLK], I32)
    slots = put("I", "slots", [128, 2 * NTILE], I32)
    GT = put("I", "GT", [128, 2, NTILE])
    triS = put("A", "triS", [128, 128])
    OH = put("B", "OH", [128, 2, NTILE, NE])
    Lg = put("B", "Lg", [128, NTILE, NG + NE])
    W1 = put("B", "W1", [128, NTILE, NE])
    CW = put("B", "CW", [128, NCH, NE])
    OT = put("B", "OT", [128, 2, NTILE, NE])
    HT = put("B", "HT", [128, NE, MAXK])
    F4 = put("B", "F4", [128, NTILE, NG, NPG])
    rt = put("B", "rt", [128, 512])
    Aoh = put("B", "Aoh", [128, 2 * NTILE, CAP])
    Boh = put("B", "Boh", [128, 2 * NTILE, NBLK])
    VI = put("B", "VI", [CAP, NBLK])
    CO = at("CO", [1, NOV, NE], F32, place["wraw"])

    ctx = ExitStack()
    with ctx:
        Z = ctx.enter_context(nc.psum_tensor("Z", [128, 2, 2, 512], F32))[:]
        M = ctx.enter_context(nc.psum_tensor("M", [128, 4, 512], F32))[:]

        def sem(name):
            return ctx.enter_context(nc.semaphore(name))

        x_in = [sem(f"x_in{t}") for t in range(NTILE)]
        stat_made = sem("stat_made")
        ws_tr = sem("ws_tr")
        ws_made = sem("ws_made")
        misc_in = sem("misc_in")
        consts = sem("consts")
        pool_step = sem("pool_step")
        g_in = sem("g_in")
        x_ss = sem("x_ss")
        x_g = sem("x_g")
        x_root = sem("x_root")
        x_sc = sem("x_sc")
        x_sc2 = sem("x_sc2")
        x_tr = sem("x_tr")
        x_hi = sem("x_hi")
        x_lo = sem("x_lo")
        raw_in = [sem(f"raw_in{i}") for i in range(3)]
        w_hi = sem("w_hi")
        w_lo = sem("w_lo")
        z_done = sem("z_done")
        ev_act = sem("ev_act")
        ev_dve = sem("ev_dve")
        side_mm = sem("side_mm")
        side_act = sem("side_act")
        side_dve = sem("side_dve")
        side_end = sem("side_end")
        a_step = sem("a_step")
        v_step = sem("v_step")
        c_in = [sem(f"c_in{i}") for i in range(3)]
        c_st = [sem(f"c_st{i}") for i in range(3)]
        c_free = sem("c_free")
        out_st = sem("out_st")
        root_in = sem("root_in")
        root_out = sem("root_out")
        xr_in = sem("xr_in")
        moe_consts = sem("moe_consts")
        xg_made = sem("xg_made")
        gfin_in = sem("gfin_in")
        zeroed = sem("zeroed")
        moe_made = sem("moe_made")
        n_set = sem("n_set")
        n_ss = sem("n_ss")
        n_rstd = sem("n_rstd")
        n_xn = sem("n_xn")
        n_tr = sem("n_tr")
        n_ev = sem("n_ev")
        n_log = sem("n_log")
        xn_st = sem("xn_st")
        r_exp_in = sem("r_exp_in")
        r_exp_out = sem("r_exp_out")
        r_oh = sem("r_oh")
        r_rank = sem("r_rank")
        r_ab = sem("r_ab")
        r_idx = sem("r_idx")
        routed = sem("routed")
        eup_in = [sem(f"eup_in{i}") for i in range(RING)]
        edn_in = [sem(f"edn_in{i}") for i in range(RING)]
        rows_in = [sem(f"rows_in{i}") for i in range(2)]
        xt_done = sem("xt_done")
        xt_ready = sem("xt_ready")
        up_done = sem("up_done")
        sil_ready = sem("sil_ready")
        hid_ready = sem("hid_ready")
        ht_done = sem("ht_done")
        hth_ready = sem("hth_ready")
        h_ready = sem("h_ready")
        dnh_ready = sem("dnh_ready")
        dnl_ready = sem("dnl_ready")
        down_done = sem("down_done")
        y_copied = sem("y_copied")
        y_st = [sem(f"y_st{i}") for i in range(2)]
        o_w = sem("o_w")
        o_rows = sem("o_rows")
        o_st = sem("o_st")
        idx_step = sem("idx_step")
        moe_over = sem("moe_over")
        yg_in = [sem(f"yg_in{i}") for i in range(NTILE)]
        f_sum = sem("f_sum")
        f_ss = sem("f_ss")
        f_out = sem("f_out")
        out_y = sem("out_y")

        N_MOE = 1 + NG + 3
        N_MISC = 8

        def cpiece(ap, i):
            h, vh, bh = i // 4, i // 2 % 2, i % 2
            return ap[0, 4 * bh:4 * bh + 4, h, 128 * vh:128 * vh + 128, :].rearrange("b v d -> v b d")

        CIN = [E[:, 3, :], E[:, 4, :], E[:, 6, :]]
        CTS = [E[:, 7, :], E[:, 2, :]]
        KWM = E[0:NS, 1, :]
        KWS = E[0:NS, 5, :]

        def bank(c):
            return Z[:, c // 2, c % 2, :] if c < 4 else M[:, c - 4, :]

        def zz(t):
            return Z[:, t % 2, :, 0:HALF]

        def two(ap):
            return ap.rearrange("p (a b) -> p a b", a=2)

        def weight_src(i):
            kind, j = BLOCKS[i]
            if kind == "wo":
                half, q = j // 8, j % 8
                return w_out[0, 128 * q:128 * q + 128, 512 * half:512 * half + 512]
            if kind in ("pa", "pb"):
                w = p_a if kind == "pa" else p_b
                return w[0].rearrange("(c p) n -> p c n", p=128)[:, :, 128 * j:128 * j + 128]
            c0 = COL[kind] + 128 * j
            return w_in[0].rearrange("(c p) n -> p c n", p=128)[:, :, c0:c0 + 128]

        def split_to(w, i):
            o = 512 * ((i - WO0) // 2 % 2) if i >= WO0 else 0
            return w[:, i % 2, o:o + wsize(i)]

        def splits_before(i):
            ahead = [i + 1] if i < WO0 + 1 else [i + 1, i + 2] if i == WO0 + 1 else [i + 2]
            return [m for m in ahead if m < NBK]

        def bank_up(k):
            return Z[0:CAP, k, 0, :]

        def bank_h():
            return Z[:, 1, 1, 0:2 * CAP]

        def bank_xt():
            return Z[:, 0, 1, :]

        def bank_out(k):
            return M[:, 2 * k:2 * k + 2, :]

        def each_block(eng, body):
            for b in (0, 1):
                body(b, b)
            with eng.Fori(1, NE // 2 - 1) as i:
                for k in range(2):
                    body(i * 2 + k, k)
            for b in (NE - 2, NE - 1):
                body(b, b % 2)

        def one(ap, e):
            return ap[e] if isinstance(e, int) else ap[bass.ds(e, 1)].rearrange("o a b -> (o a) b")

        def up_rows(w, e):
            return one(w[0], e).rearrange("(p c) n -> p (c n)", c=KC)

        def down_rows(w, e):
            return one(w[0], e).rearrange("(j p) n -> p j n", p=128)

        def slot_rows(b):
            return slot_dram[bass.ds(b * CAP, CAP), :]

        def wsize(i):
            return 512 if BLOCKS[i][0] == "wo" else KC * 128

        block = ctx.enter_context(nc.Block())

        @block.sync
        def _(sp):
            for t in range(NTILE):
                src = x_prompt[0, 128 * t:128 * t + 128, :] if t < NCH else x_sample.rearrange("b t d -> (b t) d")
                sp.dma_start(xtok[0:rows(t), t, :], src).then_inc(x_in[t], 16)
            def load_up(b, k, signal):
                sp.dma_start(eup[k][:, 0, :, :].rearrange("p c n -> p (c n)"), up_rows(e_wg, b)).then_inc(signal, 16)
                sp.dma_start(eup[k][:, 1, :, :].rearrange("p c n -> p (c n)"), up_rows(e_wu, b)).then_inc(signal, 16)

            def load_down(b, k, signal):
                sp.dma_start(edn[k], down_rows(e_wd, b)).then_inc(signal, 16)

            def ahead(u):
                if u == 0:
                    sp.wait_ge(side_end, len(STEPS))
                    sp.wait_ge(out_st, 16 * 9)
                    sp.wait_ge(ev_dve, ED[AT[("og", 7)] + 1])
                if u == 5:
                    sp.wait_ge(z_done, AT[("pa", 7)] + 1)
                k, down = ((0, False), (0, True), (1, False), (1, True), (2, True), (2, False), (3, False))[u]
                if down:
                    load_down(k, k, edn_in[k])
                else:
                    load_up(k, k, eup_in[k])

            ahead_at = {AT[("ga", 2)] + 2 * u: u for u in range(5)}
            ahead_at.update({WO0 + 4: 5, WO0 + 7: 6})
            assert max(ahead_at) < NBK
            for i in range(NBK):
                if i >= 3:
                    sp.wait_ge(w_lo, i - 2)
                n = wsize(i)
                dst = wraw[:, i % 3, 0:n]
                if n != 512:
                    dst = dst.rearrange("p (c n) -> p c n", c=KC)
                sp.dma_start(dst, weight_src(i)).then_inc(raw_in[i % 3], 16)
                if i in ahead_at:
                    ahead(ahead_at[i])
            sp.wait_ge(z_done, NBK)
            load_down(3, 3, edn_in[3])
            with sp.Fori(1, NE // RING) as i:
                for k in range(RING):
                    b = i * RING + k
                    sp.wait_ge(up_done, b - (RING - 1))
                    load_up(b, k, eup_in[k])
                    sp.wait_ge(dnl_ready, b - (RING - 1))
                    load_down(b, k, edn_in[k])
            sp.wait_ge(routed, 1)
            sp.wait_ge(down_done, NE)
            n_ov = sp.value_load(ctl[0:1, NOV:NOV + 1], min_val=0, max_val=NOV)
            with sp.If(n_ov > 0):
                with sp.Fori(0, n_ov) as o:
                    e = sp.value_load(ctl[0:1, bass.ds(o, 1)], min_val=0, max_val=NE - 1)
                    sp.wait_ge(down_done, o + NE)
                    load_up(e, 0, o_w)
                    load_down(e, 0, o_w)
            for t in range(NTILE):
                sp.wait_ge(f_out, t + 1)
                dst = y_p[0, 128 * t:128 * t + 128, :] if t < NCH else y_s.rearrange("b t d -> (b t) d")
                sp.dma_start(dst, yg[0:rows(t), t, :]).then_inc(out_y, 16)
            sp.wait_ge(out_y, 16 * NTILE)

        @block.gpsimd
        def _(pool):
            n = [0]

            def step(ins):
                ins.then_inc(pool_step, 1)
                n[0] += 1
                pool.wait_ge(pool_step, n[0])

            pool.dma_start(gB, norm_mix_g[0:1, :].partition_broadcast(128)).then_inc(g_in, 16)
            step(nc.gpsimd.memset(ident, 0.0))
            step(nc.gpsimd.affine_select(out=ident, in_=ident, compare_op=ALU.not_equal, fill=1.0, base=0,
                                         pattern=[[-1, 128]], channel_multiplier=1))
            step(nc.gpsimd.memset(ones, 1.0))
            step(nc.gpsimd.affine_select(out=tri, in_=ones, compare_op=ALU.is_ge, fill=0.0, base=0,
                                         pattern=[[1, 128]], channel_multiplier=-1))
            step(nc.gpsimd.affine_select(out=selb, in_=ones[0:NS, 0:NB], compare_op=ALU.is_ge, fill=0.0, base=0,
                                         pattern=[[-NL, NB]], channel_multiplier=1))
            step(nc.gpsimd.affine_select(out=selb, in_=selb, compare_op=ALU.is_ge, fill=0.0, base=NL - 1,
                                         pattern=[[NL, NB]], channel_multiplier=-1))
            bt = btri.rearrange("p (b t) -> p b t", t=NL)
            step(nc.gpsimd.affine_select(out=bt, in_=ones[0:NS, 0:NS].rearrange("p (b t) -> p b t", t=NL),
                                         compare_op=ALU.is_ge, fill=0.0, base=0,
                                         pattern=[[-NL, NB], [0, NL]], channel_multiplier=1))
            step(nc.gpsimd.affine_select(out=btri, in_=btri, compare_op=ALU.is_ge, fill=0.0, base=0,
                                         pattern=[[1, NS]], channel_multiplier=-1))
            step(nc.gpsimd.memset(selh, 1.0))
            step(nc.gpsimd.affine_select(out=selh, in_=selh, compare_op=ALU.is_equal, fill=0.0, base=0,
                                         pattern=[[-1, H], [0, 128]], channel_multiplier=1))
            step(nc.gpsimd.memset(epsc, EPS))
            step(nc.gpsimd.memset(gst, 1.0))
            step(nc.gpsimd.memset(CT, 0.0))
            step(nc.gpsimd.memset(nT, 0.0))
            nc.gpsimd.memset(sm, 0.0).then_inc(consts, 1)
            pool.wait_ge(consts, 1)
            pool.dma_start(wsraw, gm_ws[0].rearrange("g t s -> t g s")).then_inc(misc_in, 16)
            pool.dma_start(gmB, gm_norm_g.rearrange("o g d -> o (g d)").partition_broadcast(128)).then_inc(misc_in, 16)
            pool.dma_start(bsB.rearrange("p g t -> p (g t)"),
                           gm_bs.rearrange("o g t -> o (g t)").partition_broadcast(128)).then_inc(misc_in, 16)
            pool.dma_start(gbias[:, 0:1], ml_b_i.rearrange("o h -> h o")).then_inc(misc_in, 16)
            pool.dma_start(gbias[:, 1:2], ml_b_f.rearrange("o h -> h o")).then_inc(misc_in, 16)
            pool.dma_start(m0s, state_m[0].rearrange("b h -> h b"), allow_slow_non_contiguous=True).then_inc(misc_in, 16)
            pool.dma_start(n0s, state_n[0].rearrange("b h d -> b (h d)")).then_inc(misc_in, 16)
            pool.dma_start(mlg, ml_norm_g[0].rearrange("h (v p) -> p h v", p=128),
                           allow_slow_non_contiguous=True).then_inc(misc_in, 16)
            def c_load(i):
                pool.dma_start(CIN[i % 3].rearrange("v (b d) -> v b d", b=4), cpiece(state_C, i)) \
                    .then_inc(c_in[i % 3], 16)

            def c_store(i):
                pool.dma_start(cpiece(C_s, i), CIN[i % 3].rearrange("v (b d) -> v b d", b=4)) \
                    .then_inc(c_st[i % 3], 16)

            def c_out_pieces():
                for h in range(H):
                    pool.dma_start(C_p[0, 0, h].rearrange("(v p) d -> p v d", p=128),
                                   E[:, h // 2, 256 * (h % 2):256 * (h % 2) + 256]
                                   .rearrange("p (v d) -> p v d", v=2)).then_inc(out_st, 16)
                pool.dma_start(n_p[0, 0], E[0:H, 2, 0:128]).then_inc(out_st, 16)

            for s in STEPS:
                over = SN[s] + 1
                kind, what, j = s
                if kind == "s_c":
                    k = what
                    pool.wait_ge(side_end, SN[s])
                    if k >= 2:
                        c_store(k - 2)
                    if 2 <= k < 15:
                        pool.wait_ge(c_st[(k - 2) % 3], 16 * ((k - 2) // 3 + 1))
                    if k < 15:
                        c_load(k + 1)
                    if k == 16:
                        pool.wait_ge(side_end, over)
                        c_store(15)
                        for i in range(3):
                            pool.wait_ge(c_st[i], 16 * (6 if i == 0 else 5))
                        nc.gpsimd.memset(sm[0:1, 60:61], 0.0).then_inc(c_free, 1)
                elif kind == "tr" and what == "gv" and j == 7:
                    pool.wait_ge(side_end, over)
                    pool.dma_start(v_s[0].rearrange("b t g d -> (b t) (g d)"), xtok[0:NS, NCH, :]).then_inc(out_st, 16)
                elif kind == "rows":
                    pool.wait_ge(side_end, over)
                    pool.dma_start(m_s[0].rearrange("b h -> h b"), rws[:, 3, NL - 1:NS:NL],
                                   allow_slow_non_contiguous=True).then_inc(out_st, 16)
                    pool.dma_start(m_p.rearrange("o b h -> h (o b)"), rws[:, 3, T - 1:T]).then_inc(out_st, 16)
                elif kind == "s_pre":
                    pool.wait_ge(side_end, over)
                    c_load(0)
                elif kind == "s_den":
                    pool.wait_ge(side_end, over)
                    pool.dma_start(n_s[0].rearrange("b h d -> b (h d)"), n0s).then_inc(out_st, 16)
                elif kind == "c_out" and what == 1:
                    pool.wait_ge(side_end, over)
                    c_out_pieces()
            pool.dma_start(xres[:, 0:NCH, :], x_prompt[0].rearrange("(t p) d -> p t d", p=128)).then_inc(xr_in, 16)
            pool.dma_start(xres[0:NS, NCH, :], x_sample.rearrange("b t d -> (b t) d")).then_inc(xr_in, 16)
            pool.wait_ge(out_st, 16 * 9)
            pool.wait_ge(side_end, len(STEPS))
            nc.gpsimd.memset(nst, 1.0).then_inc(n_set, 1)
            pool.dma_start(rw[:, :, 0:NG], rc_w[0].rearrange("(c p) n -> p c n", p=128),
                           allow_slow_non_contiguous=True).then_inc(moe_consts, 16)
            for g in range(NG):
                pool.dma_start(rw[:, :, NG + NPG * g:NG + NPG * g + NPG],
                               rf_w[0, g].rearrange("(c p) n -> p c n", p=128)).then_inc(moe_consts, 16)
            pool.dma_start(rb[:, 0:NG], rc_b.partition_broadcast(128)).then_inc(moe_consts, 16)
            pool.dma_start(rb[:, NG:NG + NE], rf_b.rearrange("o g n -> o (g n)").partition_broadcast(128)) \
                .then_inc(moe_consts, 16)
            nc.gpsimd.iota(io64, pattern=[[1, CAP]], base=0, channel_multiplier=0, allow_small_or_imprecise_dtypes=True)
            nc.gpsimd.iota(caps, pattern=[[CAP, MAXK]], base=CAP, channel_multiplier=0,
                           allow_small_or_imprecise_dtypes=True)
            nc.gpsimd.iota(w8, pattern=[[-1, NPG]], base=NPG, channel_multiplier=0, allow_small_or_imprecise_dtypes=True)
            nc.gpsimd.iota(tok1, pattern=[[128, NTILE]], base=1, channel_multiplier=1,
                           allow_small_or_imprecise_dtypes=True)
            pool.wait_ge(z_done, AT[("pa", 7)] + 1)
            pool.wait_ge(ev_act, EA[WO0])
            pool.wait_ge(ev_dve, ED[WO0])
            pool.dma_start(gffn, norm_ffn_g.partition_broadcast(128)).then_inc(moe_consts, 16)
            nc.gpsimd.affine_select(out=triS, in_=ones, compare_op=ALU.is_gt, fill=0.0, base=0,
                                    pattern=[[1, 128]], channel_multiplier=-1).then_inc(moe_made, 1)
            pool.wait_ge(z_done, NBK)
            for k in range(2):
                nc.gpsimd.memset(xg[k], 0.0).then_inc(xg_made, 1)
            for h in (hTh, hTl):
                nc.gpsimd.memset(h.bitcast(F32), 0.0).then_inc(xg_made, 1)
            pool.wait_ge(xg_made, 4)
            pool.dma_start(slot_dram[NE * CAP:NBLK * CAP, :].rearrange("(b q) d -> q b d", q=CAP),
                           xg[0].unsqueeze(1).broadcast_to([CAP, NOV, D])).then_inc(zeroed, 16)
            pool.dma_start(gfin, final_norm_g.rearrange("(o d) -> o d", o=1).partition_broadcast(128)).then_inc(gfin_in, 16)
            for t in range(NTILE):
                pool.wait_ge(n_xn, t + 1)
                pool.dma_start(xn_dram[128 * t:128 * t + rows(t), :], xn[0:rows(t), t, :]).then_inc(xn_st, 16)
            pool.wait_ge(xn_st, 16 * NTILE)
            pool.wait_ge(zeroed, 16)
            pool.wait_ge(routed, 1)

            def gather(b, k):
                if not (isinstance(b, int) and b < 2):
                    pool.wait_ge(xt_done, b - 1)
                step_r(nc.gpsimd.tensor_copy(idx1[k], idx[:, bass.ds(b, 1)]), b + 1)
                nc.gpsimd.indirect_dma_start(xg[k], None, xn_dram, bass.IndirectOffsetOnAxis(idx1[k], 0),
                                             bounds_check=T - 1, oob_is_err=False).then_inc(rows_in[k], 16)

            def step_r(ins, count):
                ins.then_inc(idx_step, 1)
                pool.wait_ge(idx_step, count)
                nc.gpsimd.tensor_tensor(stat[0:1, 23:24], ones[0:1, 0:1], ones[0:1, 0:1], ALU.mult)

            each_block(pool, gather)
            n_ov = pool.value_load(ctl[0:1, NOV:NOV + 1], min_val=0, max_val=NOV)
            pool.wait_ge(xt_done, NE)
            with pool.If(n_ov > 0):
                with pool.Fori(0, n_ov) as o:
                    pool.wait_ge(xt_done, o + NE)
                    step_r(nc.gpsimd.tensor_copy(idx1[2], idx[:, bass.ds(o + NE, 1)]), o + (NE + 1))
                    nc.gpsimd.indirect_dma_start(xg[0], None, xn_dram, bass.IndirectOffsetOnAxis(idx1[2], 0),
                                                 bounds_check=T - 1, oob_is_err=False).then_inc(o_rows, 16)
            pool.wait_ge(moe_over, 1)
            for t in range(NTILE):
                for j in range(2):
                    g = NTILE * j + t
                    nc.gpsimd.indirect_dma_start(yg[0:rows(t), g, :], None, slot_dram,
                                                 bass.IndirectOffsetOnAxis(slots[0:rows(t), g:g + 1], 0)) \
                        .then_inc(yg_in[t], 16)
            pool.wait_ge(moe_consts, 16 * N_MOE)

        def transpose(out, in_, k):
            return nc.tensor.transpose(out, in_, ident[0:k, 0:k])

        @block.tensor
        def _(pe):
            pe.wait_ge(consts, 1)
            pe.wait_ge(x_sc, NTILE // 2 + 1)
            pe.wait_ge(x_sc2, NTILE // 2)
            for c in X_ORDER:
                if c == KC:
                    pe.wait_ge(x_lo, 1)
                    for m in range(KC):
                        last = transpose(bank(0)[:, NS * m:NS * m + NS], xtok[0:NS, NCH, 128 * m:128 * m + 128], NS)
                    last.then_inc(x_tr, 1)
                    continue
                for t in range(NCH):
                    last = transpose(bank(c)[:, 128 * t:128 * t + 128], xtok[:, t, 128 * c:128 * c + 128], 128)
                last.then_inc(x_tr, 1)

            def position_weights(i):
                if i == 0:
                    pe.wait_ge(misc_in, 16 * N_MISC)
                    pe.wait_ge(x_lo, KC + 1)
                    for g in range(NG):
                        last = transpose(M[:, 3, 128 * g:128 * g + 128], wsraw[:, g, :], 128)
                    last.then_inc(ws_tr, 1)
                elif i == 1:
                    pe.wait_ge(ws_made, 1)
                    nc.tensor.matmul(M[0:NS, 0, 0:NG * NL], rep4, ws4, start=True, stop=True).then_inc(ws_tr, 1)

            def multiply(i):
                kind = BLOCKS[i][0]
                ah, al = (Hh, Hl) if kind in ("pa", "pb") else (Xh, Xl)
                if kind == "pb":
                    pe.wait_ge(ev_dve, ED[AT[("u", 7)] + 1])
                if kind == "pa":
                    pe.wait_ge(ev_dve, ED[AT[("og", 7)] + 1])
                hi = wh[:, i % 2, :].rearrange("p (c n) -> p c n", c=KC)
                lo = wl[:, i % 2, :].rearrange("p (c n) -> p c n", c=KC)
                steps = SIDE[i]
                at_piece = {piece_of(st, m, len(steps)): st for m, st in enumerate(steps)}
                assert len(at_piece) == len(steps)
                for c in range(KC):
                    if i == 0:
                        pe.wait_ge(x_lo, max(5, c + 2))
                    if c in at_piece:
                        side(at_piece[c])
                    for f in range(2):
                        cols = slice(HALF * f, HALF * f + HALF)
                        z = zz(i)[:, f, :]
                        nc.tensor.matmul(z, hi[:, c, :], ah[:, c, cols], start=c == 0, stop=False)
                        nc.tensor.matmul(z, hi[:, c, :], al[:, c, cols], start=False, stop=False)
                    for f in range(2):
                        cols = slice(HALF * f, HALF * f + HALF)
                        last = nc.tensor.matmul(zz(i)[:, f, :], lo[:, c, :], ah[:, c, cols], start=False,
                                                stop=c == KC - 1)
                last.then_inc(z_done, 1)

            def multiply_out(i):
                half, q = BLOCKS[i][1] // 8, BLOCKS[i][1] % 8
                if half == 0:
                    pe.wait_ge(ev_dve, ED[WO0] - (3 if q < 7 else 0))
                n = BLOCKS[i][1] - 9
                if i < NBK - 4:
                    for t in range(NTILE):
                        last = out_tile(half, t, (i,))
                    last.then_inc(z_done, 1)
                    if 0 < n <= NTILE:
                        router_logits(0, n - 1)
                    if 0 <= n < NTILE:
                        router_tokens(0, n)
                elif i < NBK - 1:
                    if n <= NTILE:
                        router_logits(0, n - 1)
                    if n < NTILE:
                        router_tokens(0, n)
                else:
                    for t in range(NTILE + 3):
                        if t < NTILE:
                            last = out_tile(half, t, range(NBK - 4, NBK))
                            if t:
                                last.then_inc(z_done, 1)
                        if 2 <= t < NTILE + 2:
                            router_tokens(1, t - 2)
                        if 3 <= t:
                            router_logits(1, t - 3)

            def out_tile(half, t, pieces):
                g = NTILE * half + t
                out = bank((g + 2) % 8)
                cols = slice(tok_cols(t), tok_cols(t) + 128)
                for i in pieces:
                    q = BLOCKS[i][1] % 8
                    if q == 0 and g >= 8:
                        pe.wait_ge(ev_dve, ED[WO0 + 7] + 2 * (g - 8) + 1)
                    nc.tensor.matmul(out, Xh[:, q, cols], split_to(wh, i), start=q == 0, stop=False)
                    nc.tensor.matmul(out, Xl[:, q, cols], split_to(wh, i), start=False, stop=False)
                    last = nc.tensor.matmul(out, Xh[:, q, cols], split_to(wl, i), start=False, stop=q == 7)
                return last

            def router_tokens(half, t):
                r, n = rows(t), NTILE * half + t
                pe.wait_ge(ev_dve, ED[WO0 + 7 + 8 * half] + 2 * t + 2)
                if n >= 2:
                    pe.wait_ge(n_ev, n - 1)
                else:
                    pe.wait_ge(ev_dve, ED[WO0 + 7] + 2 * (n + 2) + 1)
                for c in range(4):
                    last = transpose(M[:, n % 2, 128 * c:128 * c + r],
                                     xn[0:r, t, 512 * half + 128 * c:512 * half + 128 * c + 128], r)
                last.then_inc(n_tr, 1)

            def router_logits(half, t):
                r, n, w = rows(t), NTILE * half + t, NG + NE
                pe.wait_ge(n_ev, n + 1)
                if n == 0:
                    pe.wait_ge(ev_dve, ED[WO0 + 7] + 2 * (NTILE - 1) + 1)
                for c in range(4):
                    last = nc.tensor.matmul(M[0:r, 2 + half, w * t:w * t + w], xnT[n % 2][:, c, 0:r], rw[:, 4 * half + c, :],
                                            start=c == 0, stop=c == 3)
                last.then_inc(n_log, 1)

            def rows_of(bank, lhs, rhs, n):
                for h in range(H):
                    nc.tensor.matmul(bank[:, n * h:n * h + n], lhs(h), rhs(h), start=True, stop=True)

            def side(step):
                kind, what, j = step
                n = SN[step]
                before = STEPS[n - 1] if n else None
                if before and before[0] == "rows":
                    pe.wait_ge(side_act, HA[before] + 1)
                elif before and before[0] == "tr" and hands(before)[0]:
                    pe.wait_ge(side_dve, HD[before] + 1)
                elif before and before[0] == "ml3":
                    pe.wait_ge(root_in, RN[before] + 1)
                elif before:
                    pe.wait_ge(side_end, n)
                if kind == "tr":
                    pe.wait_ge(ev_act, EA[AT[(what, j)]] + 1)
                    src = kT[:, j, :] if what == "k" else ev[:, AT[(what, j)] % 2, :]
                    for t in range(NCH):
                        transpose(M[:, 0, 128 * t:128 * t + 128], src[:, NS + 128 * t:NS + 128 * t + 128], 128)
                    last = transpose(M[0:NS, 1, 0:128], src[:, 0:NS], 128)
                elif kind == "rows":
                    pe.wait_ge(ev_act, EA[AT[("gates", 0)]] + 1)
                    for f in range(2):
                        last = nc.tensor.matmul(M[0:H, f, 0:HALF], ident[0:2 * H, H:2 * H],
                                                ev[0:2 * H, AT[("gates", 0)] % 2, HALF * f:HALF * f + HALF],
                                                start=True, stop=True)
                elif kind == "mix":
                    g = what // 2
                    for c in range(NCH):
                        nc.tensor.matmul(M[:, 0, 128 * c:128 * c + 128], xtok[:, c, 128 * what:128 * what + 128],
                                         wsT[:, g, :], start=True, stop=True)
                    last = nc.tensor.matmul(M[:, 1, 0:NS], xtok[0:NS, NCH, 128 * what:128 * what + 128],
                                            wsS[:, g, :], start=True, stop=True)
                elif kind == "s_pre":
                    rows_of(M[:, 0, :], lambda h: selh[:, h, :], lambda h: rws[:, 2, 0:NS], NS)
                    rows_of(M[:, 0, 4 * NS:], lambda h: selh[:, h, :], lambda h: m0s, NB)
                    rows_of(M[:, 1, :], lambda h: selh[:, h, :], lambda h: rws[:, 3, 0:NS], NS)
                    rows_of(M[0:NS, 2, :], lambda h: kT[:, h, 0:NS], lambda h: qT[:, h, 0:NS], NS)
                    transpose(M[0:NS, 3, 0:H], rws[:, 0, 0:NS], H)
                    transpose(M[0:NS, 3, H:2 * H], rws[:, 4, 0:NS], H)
                    transpose(M[0:NB, 3, 64:64 + H], rws[:, 4, NS:NS + NB], H)
                    for h in range(H):
                        last = transpose(M[:, 3, 16 + NB * h:16 + NB * h + NB], n0s[:, 128 * h:128 * h + 128], NB)
                elif kind == "s_c":
                    if what < 16:
                        pe.wait_ge(c_in[what % 3], 16 * (what // 3 + 1))
                        for b in range(4):
                            last = transpose(M[:, 0, 128 * b:128 * b + 128],
                                             CIN[what % 3][:, 128 * b:128 * b + 128], 128)
                    if what > 0:
                        i = what - 1
                        h, vh, bh = i // 4, i // 2 % 2, i % 2
                        v = vtok[0:NS, NCH, 256 * h + 128 * vh:256 * h + 128 * vh + 128]
                        num = M[:, 2, NS * (H * vh + h):NS * (H * vh + h) + NS]
                        if bh == 0:
                            nc.tensor.matmul(num, v, E[0:NS, 0, NS * h:NS * h + NS], start=True, stop=False)
                        for b in range(4):
                            c0 = 16 * bh + NL * b
                            nc.tensor.matmul(num[:, c0:c0 + NL], CTS[i % 2][:, 128 * b:128 * b + 128],
                                             E[:, 0, 128 + NS * h + c0:128 + NS * h + c0 + NL], start=False,
                                             stop=bh == 1 and b == 3)
                        last = nc.tensor.matmul(M[:, 1, :], v, KWM, start=True, stop=True)
                elif kind == "s_den":
                    nc.tensor.matmul(M[:, 3, 0:128], ones[0:NS, :], E[0:NS, 0, 0:128], start=True, stop=False)
                    nc.tensor.matmul(M[:, 3, 0:128], ones, E[:, 0, 256:384], start=False, stop=True)
                    for h in range(H):
                        last = nc.tensor.matmul(M[0:NB, 1, 128 * h:128 * h + 128], selb, KWS[:, 128 * h:128 * h + 128],
                                                start=True, stop=True)
                elif kind == "s_ss":
                    nc.tensor.matmul(M[:, 3, 0:128], ones, E[:, 6, 256:384], start=True, stop=False)
                    last = nc.tensor.matmul(M[:, 3, 0:128], ones, E[:, 6, 384:512], start=False, stop=True)
                elif kind == "ml1":
                    seg = slice(NS + 128 * what, NS + 128 * what + 128)
                    rows_of(M[:, 0, :], lambda h: selh[:, h, :], lambda h: rws[:, 2, seg], 128)
                    rows_of(M[:, 1, :], lambda h: selh[:, h, :], lambda h: rws[:, 3, seg], 128)
                    rows_of(M[:, 2, :], lambda h: kT[:, h, seg], lambda h: qT[:, h, seg], 128)
                    last = transpose(M[:, 3, 0:H], rws[:, 0, seg], H)
                elif kind == "ml2":
                    for vh in range(2):
                        for h in range(H):
                            o = M[:, vh, 128 * h:128 * h + 128]
                            nc.tensor.matmul(o, vtok[:, what, 256 * h + 128 * vh:256 * h + 128 * vh + 128],
                                             E[:, 0, 128 * h:128 * h + 128], start=True, stop=False)
                            nc.tensor.matmul(o, CT[:, h, 128 * vh:128 * vh + 128],
                                             E[:, 1, 128 * h:128 * h + 128], start=False, stop=True)
                    nc.tensor.matmul(M[:, 2, :], ones, E[:, 0, :], start=True, stop=False)
                    last = nc.tensor.matmul(M[:, 2, :], ones, E[:, 2, :], start=False, stop=True)
                elif kind == "ml3":
                    nc.tensor.matmul(M[:, 3, :], ones, E[:, 0, :], start=True, stop=False)
                    nc.tensor.matmul(M[:, 3, :], ones, E[:, 1, :], start=False, stop=True)
                    for h in range(H):
                        kw = E[:, 5, 128 * h:128 * h + 128]
                        nc.tensor.matmul(M[:, h // 2, 256 * (h % 2):256 * (h % 2) + 256], kw,
                                         vtok[:, what, 256 * h:256 * h + 256], start=True, stop=True)
                        last = nc.tensor.matmul(M[:, 2, h:h + 1], kw, ones[:, 0:1], start=True, stop=True)
                else:
                    for q in range(4):
                        h, vh = 2 * what + q // 2, q % 2
                        last = transpose(M[:, 0, 128 * q:128 * q + 128], CT[:, h, 128 * vh:128 * vh + 128], 128)
                    if what == 1:
                        last = transpose(M[0:H, 1, 0:128], nT, 128)
                last.then_inc(side_mm, 1)

            for i in range(NBK):
                if 2 <= i < WO0:
                    if BLOCKS[i - 2][0] in ("pa", "pb"):
                        pe.wait_ge(ev_dve, ED[i - 2] + 1)
                    else:
                        pe.wait_ge(ev_act, EA[i - 2] + 1)
                pe.wait_ge(w_lo, i + 1)
                if i >= WO0:
                    multiply_out(i)
                else:
                    multiply(i)
                    position_weights(i)

            pe.wait_ge(r_oh, 1)
            RB = M[:, 1, :]
            c2 = CW.rearrange("p t e -> p (t e)")
            w2 = W1.rearrange("p t e -> p (t e)")
            n4 = NE * NCH
            nc.tensor.matmul(RB[:, 0:n4], triS, w2[:, 0:n4], start=True, stop=False)
            nc.tensor.matmul(RB[:, NE:n4], ones, c2[:, 0:n4 - NE], start=False, stop=True)
            nc.tensor.matmul(RB[:, n4:n4 + NE], triS[0:NS, :], w2[0:NS, n4:n4 + NE], start=True, stop=False)
            nc.tensor.matmul(RB[:, n4:n4 + NE], ones, c2[:, n4 - NE:n4], start=False, stop=True)
            nc.tensor.matmul(RB[:, n4 + NE:n4 + 2 * NE], ones[0:NS, :], w2[0:NS, n4:n4 + NE], start=True, stop=False)
            nc.tensor.matmul(RB[:, n4 + NE:n4 + 2 * NE], ones, c2[:, n4 - NE:n4], start=False, stop=True) \
                .then_inc(r_rank, 1)
            pe.wait_ge(r_ab, 1)
            for g in range(2 * NTILE):
                r = rows(g % NTILE)
                last = nc.tensor.matmul(M[0:CAP, 2, 0:NBLK], Aoh[0:r, g, :], Boh[0:r, g, :], start=g == 0,
                                        stop=g == 2 * NTILE - 1)
            last.then_inc(r_idx, 1)

            def tokens_by_feature(src):
                s = src.rearrange("q (p c) -> q p c", c=KC)
                for c in range(KC):
                    out = bank_xt()[:, CAP * c:CAP * c + CAP]
                    last = nc.tensor.matmul(out, s[:, :, c], ident[0:CAP, 0:CAP], start=True, stop=True) if c == 0 \
                        else transpose(out, s[:, :, c], CAP)
                return last

            def up(k, x, w, halfway=None):
                for c in range(KC):
                    if c == KC // 2 and halfway is not None:
                        halfway()
                    last = nc.tensor.matmul(bank_up(k).rearrange("q (g n) -> q g n", g=2), x[:, c, :], w[:, :, c, :],
                                            start=c == 0, stop=c == KC - 1)
                return last

            def hidden_by_feature(h):
                out = bank_h()
                nc.tensor.matmul(out[:, 0:CAP], h[:, 0:128], ident[0:CAP, 0:CAP], start=True, stop=True)
                return transpose(out[:, CAP:2 * CAP], h[:, 128:2 * 128], CAP)

            def down(k):
                for f in range(2):
                    out, cols = bank_out(k)[:, f, :], slice(512 * f, 512 * f + 512)
                    for j in range(2):
                        nc.tensor.matmul(out, hTh[:, j, :], dnh[:, j, cols], start=j == 0, stop=False)
                        nc.tensor.matmul(out, hTh[:, j, :], dnl[:, j, cols], start=False, stop=False)
                        last = nc.tensor.matmul(out, hTl[:, j, :], dnh[:, j, cols], start=False, stop=j == 1)
                return last

            def tokens_of(b, k, landed):
                pe.wait_ge(rows_in[k], landed)
                if not (isinstance(b, int) and b < 1):
                    pe.wait_ge(xt_ready, b)
                tokens_by_feature(xg[k]).then_inc(xt_done, 1)

            def hidden_of(b, r):
                pe.wait_ge(hid_ready, b + 1)
                hidden_by_feature(hid[r % 2]).then_inc(ht_done, 1)

            def up_of(b, r, landed, with_hidden=True):
                pe.wait_ge(xt_ready, b + 1)
                pe.wait_ge(eup_in[r], landed)
                halfway = (lambda: hidden_of(b - 1, (r - 1) % RING)) if with_hidden else None
                up(r % 2, xT[r % 2], eup[r], halfway).then_inc(up_done, 1)

            def down_of(b, r):
                pe.wait_ge(h_ready, b + 1)
                pe.wait_ge(dnl_ready, b + 1)
                if not (isinstance(b, int) and b < 2):
                    pe.wait_ge(y_copied, b - 1)
                down(r % 2).then_inc(down_done, 1)

            pe.wait_ge(routed, 1)
            tokens_of(0, 0, 16)
            up_of(0, 0, 32, with_hidden=False)
            tokens_of(1, 1, 16)
            for b in range(1, RING):
                up_of(b, b, 32)
                tokens_of(b + 1, (b + 1) % 2, 16 * ((b + 1) // 2 + 1))
                down_of(b - 1, b - 1)
            with pe.Fori(1, NE // RING - 1) as i:
                for r in range(RING):
                    b = i * RING + r
                    up_of(b, r, i * 32 + 32)
                    tokens_of(b + 1, (r + 1) % 2, i * 32 + 16 * ((r + 1) // 2 + 1))
                    down_of(b - 1, (r - 1) % RING)
            rounds = NE // RING
            for b in range(NE - RING, NE):
                up_of(b, b % RING, 32 * rounds)
                if b + 1 < NE:
                    tokens_of(b + 1, (b + 1) % 2, 16 * ((b + 1) // 2 + 1))
                down_of(b - 1, (b - 1) % RING)
            hidden_of(NE - 1, RING - 1)
            down_of(NE - 1, RING - 1)
            n_ov = pe.value_load(ctl[0:1, NOV:NOV + 1], min_val=0, max_val=NOV)
            with pe.If(n_ov > 0):
                with pe.Fori(0, n_ov) as o:
                    pe.wait_ge(o_rows, o * 16 + 16)
                    tokens_by_feature(xg[0]).then_inc(xt_done, 1)
                    pe.wait_ge(xt_ready, o + (NE + 1))
                    pe.wait_ge(o_w, o * 48 + 48)
                    up(0, xT[0], eup[0]).then_inc(up_done, 1)
                    pe.wait_ge(hid_ready, o + (NE + 1))
                    hidden_by_feature(hid[0]).then_inc(ht_done, 1)
                    pe.wait_ge(h_ready, o + (NE + 1))
                    pe.wait_ge(dnl_ready, o + (NE + 1))
                    pe.wait_ge(y_copied, o + NE)
                    down(0).then_inc(down_done, 1)

        @block.scalar
        def _(act):
            n = [0]

            def step(ins):
                ins.then_inc(a_step, 1)
                n[0] += 1
                act.wait_ge(a_step, n[0])

            A = nc.scalar.activation

            def split(i):
                act.wait_ge(raw_in[i % 3], 16 * (i // 3 + 1))
                if i >= WO0 + 2:
                    act.wait_ge(z_done, max(i - 3, WO0))
                elif i >= 2:
                    act.wait_ge(z_done, i - 1)
                A(split_to(wh, i), wraw[:, i % 3, 0:wsize(i)], ACT.Copy).then_inc(w_hi, 1)

            def root(x, k):
                act.wait_ge(root_in, k + 1)
                step(A(x, x, ACT.Ln, bias=epsc[0:x.shape[0], :]))
                A(x, x, ACT.Exp, scale=-0.5).then_inc(root_out, 1)

            act.wait_ge(stat_made, 1)
            for t in range(NTILE):
                r = rows(t)
                act.wait_ge(x_in[t], 16)
                A(junk[0:r, :], xtok[0:r, t, :], ACT.Square, accum_out=stat[0:r, 8 + t:9 + t]).then_inc(x_ss, 1)
                act.wait_ge(x_ss, t + 1)
            split(0)
            act.wait_ge(x_root, 1)
            for t in range(1, NTILE, 2):
                act.wait_ge(x_g, t + 1)
                A(xtok[:, t, :], xtok[:, t, :], ACT.Copy, scale=stat[:, 8 + t:9 + t]).then_inc(x_sc2, 1)
            for m, c in enumerate(X_ORDER):
                act.wait_ge(x_tr, m + 1)
                if c == KC:
                    A(Xh[:, :, 0:NS], bank(0)[:, 0:KC * NS].rearrange("p (c n) -> p c n", c=KC), ACT.Copy).then_inc(x_hi, 1)
                else:
                    A(Xh[:, c, NS:T], bank(c), ACT.Copy).then_inc(x_hi, 1)

            def squares(half, t):
                r = rows(t)
                if half == 0 and t == 0:
                    act.wait_ge(n_set, 1)
                act.wait_ge(ev_dve, ED[WO0 + 7 + 8 * half] + 2 * t + 1)
                x = xres[0:r, t, 512 * half:512 * half + 512]
                A(sq[0:r, :], x, ACT.Square, accum_out=nst[0:r, half, t:t + 1]).then_inc(n_ss, 1)
                act.wait_ge(n_ss, NTILE * half + t + 1)

            def router_copy(half, t):
                r, n = rows(t), NTILE * half + t
                act.wait_ge(n_tr, n + 1)
                if n >= 2:
                    act.wait_ge(n_log, n - 1)
                A(xnT[n % 2][:, :, 0:r], M[:, n % 2, :].rearrange("p (c n) -> p c n", n=128)[:, :, 0:r],
                  ACT.Copy).then_inc(n_ev, 1)

            def evacuate(i):
                kind, j = BLOCKS[i]
                if kind == "wo":
                    if 9 <= j < 9 + NTILE:
                        router_copy(0, j - 9)
                        squares(0, j - 9)
                    return
                e = ev[:, i % 2, :]
                if kind == "pa" and j == 7:
                    for c in range(KC):
                        act.wait_ge(ev_dve, ED[i] if c < 7 else ED[i] + 9)
                        if c == 0:
                            act.wait_ge(z_done, AT[("ga", 7)] + 1)
                        A(Xh[:, c, :], sumT[:, c, :], ACT.Copy).then_inc(ev_act, 1)
                    return
                if kind in ("pa", "pb"):
                    return
                act.wait_ge(z_done, i + 1)
                if kind == "q":
                    A(two(qT[:, j, :]), zz(i), ACT.Copy, scale=float(DQK) ** -0.5).then_inc(ev_act, 1)
                elif kind == "k":
                    A(two(kT[:, j, :]), zz(i), ACT.Copy).then_inc(ev_act, 1)
                else:
                    if i >= 2:
                        act.wait_ge(ev_dve, ED[i] if BLOCKS[i - 1][0] in ("pa", "pb") else ED[i - 1])
                    if kind in ("v", "gv", "gates"):
                        before = BLOCKS[i - 2]
                        tr = ("rows", 0, 0) if before[0] == "gates" else ("tr",) + before
                        if tr in SN:
                            act.wait_ge(side_mm, SN[tr] + 1)
                        func = ACT.Gelu_apprx_tanh if kind == "gv" else ACT.Copy
                        r = 2 * H if kind == "gates" else 128
                        A(two(e[0:r]), zz(i)[0:r], func).then_inc(ev_act, 1)
                    elif kind == "u":
                        if j < 2:
                            act.wait_ge(side_mm, SN[("tr", "gv", 6 + j)] + 1)
                        A(two(e), zz(i), ACT.Gelu_apprx_tanh).then_inc(ev_act, 1)
                        act.wait_ge(ev_dve, ED[i] + 1)
                        A(Hh[:, j, :], e, ACT.Copy).then_inc(ev_act, 1)
                    elif kind in ("gb", "ga"):
                        A(two(e), zz(i), ACT.Tanh, scale=0.5).then_inc(ev_act, 1)
                    elif kind == "og":
                        A(two(e), zz(i), ACT.Tanh, scale=0.5).then_inc(ev_act, 1)
                        act.wait_ge(ev_dve, ED[i] + 1)
                        act.wait_ge(z_done, AT[("pb", 7)] + 1)
                        A(Hh[:, j, :], e, ACT.Copy).then_inc(ev_act, 1)

            def side(st):
                kind, what, j = st
                a, d = HA[st], HD[st]
                if hands(st)[0] == 0 and st not in RN:
                    return
                act.wait_ge(side_mm, SN[st] + 1)
                if kind == "tr":
                    act.wait_ge(side_dve, d + 1)
                    g = j // 2
                    for t in range(NTILE):
                        r = rows(t)
                        last = A(gjunk[0:r, :], xtok[0:r, t, 256 * g:256 * g + 256], ACT.Square,
                                 accum_out=gst[0:r, t:t + 1])
                        if t < NTILE - 1:
                            step(last)
                    last.then_inc(side_act, 1)
                elif kind == "s_ss":
                    root(E[:, 1, 0:128], RN[st])
                elif kind == "ml3":
                    root(E[:, 0, :], RN[st])
                elif kind == "rows":
                    step(A(two(rws[:, 1, :]), M[0:H, 0:2, 0:HALF], ACT.Identity, bias=gbias[:, 1:2]))
                    A(rws[:, 0, :], ev[0:H, AT[("gates", 0)] % 2, :], ACT.Identity, bias=gbias[:, 0:1]) \
                        .then_inc(side_act, 1)
                    step(A(rws[:, 4, :], rws[:, 1, :], ACT.Abs))
                    step(A(rws[:, 4, :], rws[:, 4, :], ACT.Exp, scale=-1.0))
                    A(rws[:, 4, :], rws[:, 4, :], ACT.Ln, bias=1.0).then_inc(side_act, 1)
                elif kind == "s_pre":
                    A(E[:, 0, 384:512], M[:, 1, 0:128], ACT.Exp, scale=-1.0)
                    act.wait_ge(side_dve, d + 1)
                    A(E[0:NS, 0, 0:128], E[0:NS, 0, 0:128], ACT.Exp, scale=-1.0)
                    A(E[:, 0, 128:256], E[:, 0, 128:256], ACT.Exp).then_inc(side_act, 1)
                    A(sm[0:NS, 4:8], sm[0:NS, 4:8], ACT.Exp)
                    A(sm[0:NB, 48:52], sm[0:NB, 48:52], ACT.Exp)
                    A(sm[:, 96:128], sm[:, 96:128], ACT.Exp).then_inc(side_act, 1)
                elif kind == "s_c":
                    if what < 16:
                        A(CTS[what % 2], M[:, 0, :], ACT.Copy).then_inc(side_act, 1)
                    else:
                        A(CTS[0][:, 0:1], sm[:, 0:1], ACT.Copy).then_inc(side_act, 1)
                elif kind == "s_den":
                    act.wait_ge(c_free, 1)
                    A(E[:, 6, 0:256], M[:, 2, 0:256], ACT.Copy)
                    A(E[:, 6, 256:512], M[:, 2, 0:256], ACT.Square).then_inc(side_act, 1)
                elif kind == "ml1":
                    act.wait_ge(side_end, SN[st])
                    A(E[:, 4, :], M[:, 1, :], ACT.Exp, scale=-1.0)
                    act.wait_ge(side_dve, d + 1)
                    A(E[:, 0, :], E[:, 0, :], ACT.Exp, scale=-1.0)
                    A(sm[:, 4:12], sm[:, 4:12], ACT.Exp).then_inc(side_act, 1)
                    for h in range(H):
                        last = A(E[:, 1, 128 * h:128 * h + 128], M[:, 0, 128 * h:128 * h + 128], ACT.Exp,
                                 scale=-1.0, bias=sm[:, 12 + h:13 + h])
                    last.then_inc(side_act, 1)
                elif kind == "ml2":
                    A(E[:, 2:4, :], M[:, 0:2, :], ACT.Copy)
                    A(E[:, 0:2, :], M[:, 0:2, :], ACT.Square).then_inc(side_act, 1)

            for i in range(NBK):
                for m in splits_before(i):
                    split(m)
                for s in SIDE[i]:
                    side(s)
                evacuate(i)

            for t in range(NTILE):
                squares(1, t)
                router_copy(1, t)
            act.wait_ge(n_rstd, 1)
            for t in range(NTILE):
                r = rows(t)
                if t == NTILE - 1:
                    act.wait_ge(r_exp_in, 1)
                    A(rt[:, 0:25], rt[:, 0:25], ACT.Exp).then_inc(r_exp_out, 1)
                A(xn[0:r, t, :], xn[0:r, t, :], ACT.Copy, scale=nst[0:r, 0, t:t + 1]).then_inc(n_xn, 1)

            def silu_of(b, k):
                act.wait_ge(up_done, b + 1)
                if not (isinstance(b, int) and b < 2):
                    act.wait_ge(hid_ready, b - 1)
                A(sil[k], bank_up(k)[:, 0:EH], ACT.Silu).then_inc(sil_ready, 1)

            def out_of(b, k, stored=None):
                act.wait_ge(down_done, b + 1)
                if stored is not None:
                    act.wait_ge(y_st[k], stored)
                A(yout[k].rearrange("q (f n) -> q f n", f=2), bank_out(k)[0:CAP], ACT.Copy).then_inc(y_copied, 1)
                act.wait_ge(y_copied, b + 1)
                act.dma_start(slot_rows(b), yout[k]).then_inc(y_st[k], 16)

            def split_down(b, w):
                if not (isinstance(b, int) and b < 1):
                    act.wait_ge(down_done, b)
                for j in range(2):
                    A(dnh[:, j, :], w[:, j, :], ACT.Copy).then_inc(dnh_ready, 1)

            def high_of(b):
                act.wait_ge(ht_done, b + 1)
                if not (isinstance(b, int) and b < 1):
                    act.wait_ge(down_done, b)
                A(hTh[:, :, 0:CAP], bank_h().rearrange("p (j n) -> p j n", j=2), ACT.Copy).then_inc(hth_ready, 1)

            def block_of(b, r, landed, stored):
                silu_of(b, r % 2)
                act.wait_ge(edn_in[r], landed)
                split_down(b, edn[r])
                if not (isinstance(b, int) and b < 1):
                    out_of(b - 1, (r - 1) % 2, stored)
                high_of(b)

            act.wait_ge(routed, 1)
            act.wait_ge(xn_st, 16 * NTILE)
            for b in range(RING):
                block_of(b, b, 16, (None, None, None, 16)[b])
            with act.Fori(1, NE // RING) as i:
                for r in range(RING):
                    block_of(i * RING + r, r, i * 16 + 16, i * 32 + (-16, 0, 0, 16)[r])
            out_of(NE - 1, 1, 8 * NE - 16)
            n_ov = act.value_load(ctl[0:1, NOV:NOV + 1], min_val=0, max_val=NOV)
            for k in range(2):
                act.wait_ge(y_st[k], 8 * NE)
            with act.If(n_ov > 0):
                with act.Fori(0, n_ov) as o:
                    act.wait_ge(up_done, o + (NE + 1))
                    A(sil[0], bank_up(0)[:, 0:EH], ACT.Silu).then_inc(sil_ready, 1)
                    act.wait_ge(o_w, o * 48 + 48)
                    split_down(o + NE, edn[0])
                    high_of(o + NE)
                    act.wait_ge(down_done, o + (NE + 1))
                    A(yout[0].rearrange("q (f n) -> q f n", f=2), bank_out(0)[0:CAP], ACT.Copy).then_inc(y_copied, 1)
                    act.wait_ge(y_copied, o + (NE + 1))
                    act.dma_start(slot_rows(o + NE), yout[0]).then_inc(o_st, 16)
                    act.wait_ge(o_st, o * 16 + 16)
            A(nst[:, 1, 0:1], nst[:, 1, 0:1], ACT.Copy).then_inc(moe_over, 1)

            for t in range(NTILE):
                r = rows(t)
                act.wait_ge(f_sum, t + 1)
                A(sqf[0:r, :], xres[0:r, t, :], ACT.Square, accum_out=nst[0:r, 1, t:t + 1]).then_inc(f_ss, 1)
                act.wait_ge(f_ss, t + 1)

        @block.vector
        def _(dve):
            n = [0]
            V = nc.vector

            def step(ins):
                ins.then_inc(v_step, 1)
                n[0] += 1
                dve.wait_ge(v_step, n[0])

            def split(i):
                dve.wait_ge(w_hi, i + 1)
                V.tensor_tensor(split_to(wl, i), wraw[:, i % 3, 0:wsize(i)], split_to(wh, i).bitcast(F32),
                                ALU.subtract).then_inc(w_lo, 1)

            def root_of(x, inv, done=None):
                y, u = newt[0:x.shape[0], 0, 0:x.shape[1]], newt[0:x.shape[0], 1, 0:x.shape[1]]
                step(V.tensor_scalar(x, x, inv, EPS, ALU.mult, ALU.add))
                step(V.tensor_scalar(y.bitcast(I32), x.bitcast(I32), -0.5, float(0x5f3759df), ALU.mult, ALU.add))
                for k in range(3):
                    step(V.tensor_tensor(u, y, y, ALU.mult))
                    step(V.scalar_tensor_tensor(u, u, -0.5, x, ALU.mult, ALU.mult))
                    out = x if k == 2 else y
                    step(V.scalar_tensor_tensor(out, u, 1.5, y, ALU.add, ALU.mult))
                if done is not None:
                    V.tensor_copy(newt[0:1, 0, 0:1], newt[0:1, 1, 0:1]).then_inc(done, 1)

            V.memset(stat, 1.0).then_inc(stat_made, 1)
            dve.wait_ge(g_in, 16)
            for t in range(NTILE):
                r = rows(t)
                dve.wait_ge(x_ss, t + 1)
                V.tensor_tensor(xtok[0:r, t, :], xtok[0:r, t, :], gB[0:r, :], ALU.mult).then_inc(x_g, 1)
            root_of(stat[:, 8:8 + NTILE], 1.0 / D, x_root)
            for t in range(0, NTILE, 2):
                x = xtok[0:rows(t), t, :]
                V.tensor_scalar(x, x, stat[0:rows(t), 8 + t:9 + t], None, ALU.mult).then_inc(x_sc, 1)
            split(0)
            for m, c in enumerate(X_ORDER):
                dve.wait_ge(x_hi, m + 1)
                if c == KC:
                    V.tensor_tensor(Xl[:, :, 0:NS], bank(0)[:, 0:KC * NS].rearrange("p (c n) -> p c n", c=KC),
                                    Xh[:, :, 0:NS].bitcast(F32), ALU.subtract).then_inc(x_lo, 1)
                else:
                    V.tensor_tensor(Xl[:, c, NS:T], bank(c), Xh[:, c, NS:T].bitcast(F32), ALU.subtract).then_inc(x_lo, 1)

            def position_weights(i):
                dve.wait_ge(ws_tr, i + 1)
                if i == 0:
                    dve.wait_ge(consts, 1)
                    V.tensor_tensor(wsT, M[:, 3, :].rearrange("p (g t) -> p g t", g=NG),
                                    tri.unsqueeze(1).broadcast_to([128, NG, 128]), ALU.mult)
                    step(V.tensor_copy(rep4.rearrange("p (b t) -> p b t", t=NL),
                                       ident[0:NL, 0:NL].unsqueeze(1).broadcast_to([NL, NB, NL])))
                    V.tensor_copy(ws4.rearrange("p (g t) -> p g t", g=NG), wsT[0:NL, :, 0:NL]).then_inc(ws_made, 1)
                else:
                    for g in range(NG):
                        V.tensor_tensor(wsS[:, g, :].rearrange("p (b t) -> p b t", t=NL),
                                        M[0:NS, 0, NL * g:NL * g + NL].unsqueeze(1).broadcast_to([NS, NB, NL]),
                                        btri.rearrange("p (b t) -> p b t", t=NL), ALU.mult)

            def hm(c, h, vh):
                if c == NCH:
                    return vtok[:, NCH, NS * (H * vh + h):NS * (H * vh + h) + NS]
                return vtok[:, c, 128 * (H * vh + h):128 * (H * vh + h) + 128]

            def evacuate(i):
                kind, j = BLOCKS[i]
                e = ev[:, i % 2, :]
                if kind == "u":
                    dve.wait_ge(ev_act, EA[i] + 1)
                    V.tensor_tensor(e, e, mixT[:, j, :], ALU.mult).then_inc(ev_dve, 1)
                    dve.wait_ge(ev_act, EA[i] + 2)
                    V.tensor_tensor(Hl[:, j, :], e, Hh[:, j, :].bitcast(F32), ALU.subtract).then_inc(ev_dve, 1)
                elif kind in ("gb", "ga"):
                    dve.wait_ge(ev_act, EA[i] + 1)
                    V.tensor_scalar(e, e, 0.5, 0.5, ALU.mult, ALU.add).then_inc(ev_dve, 1)
                elif kind == "pb":
                    dve.wait_ge(z_done, i + 1)
                    dve.wait_ge(ev_dve, ED[i])
                    if j == 0:
                        dve.wait_ge(out_st, 16 * 3)
                    V.tensor_tensor(two(sumT[:, j, :]), zz(i), two(ev[:, (i - 1) % 2, :]), ALU.mult) \
                        .then_inc(ev_dve, 1)
                elif kind == "pa":
                    g = ev[:, (i - 1) % 2, :]
                    d0 = ED[i]

                    def rest(c):
                        dve.wait_ge(ev_act, EA[i] + c + 1)
                        V.tensor_tensor(Xl[:, c, :], sumT[:, c, :], Xh[:, c, :].bitcast(F32), ALU.subtract) \
                            .then_inc(ev_dve, 1)

                    if j == 7:
                        for c in range(KC - 1):
                            rest(c)
                        d0 += KC - 1
                    dve.wait_ge(z_done, i + 1)
                    dve.wait_ge(ev_dve, d0)
                    V.tensor_tensor(two(g), zz(i), two(g), ALU.mult).then_inc(ev_dve, 1)
                    dve.wait_ge(ev_dve, d0 + 1)
                    V.tensor_tensor(sumT[:, j, :], sumT[:, j, :], g, ALU.add).then_inc(ev_dve, 1)
                    if j == 7:
                        rest(KC - 1)
                elif kind == "og":
                    h, vh = j // 2, j % 2
                    dve.wait_ge(ev_act, EA[i] + 1)
                    step(V.tensor_scalar(e, e, 0.5, 0.5, ALU.mult, ALU.add))
                    V.scalar_tensor_tensor(e[:, NS:T].rearrange("p (c n) -> p c n", c=NCH),
                                           e[:, NS:T].rearrange("p (c n) -> p c n", c=NCH), mlg[:, h, vh:vh + 1],
                                           vtok[:, 0:NCH, 128 * (H * vh + h):128 * (H * vh + h) + 128],
                                           ALU.mult, ALU.mult)
                    V.scalar_tensor_tensor(e[:, 0:NS], e[:, 0:NS], mlg[:, h, vh:vh + 1], hm(NCH, h, vh),
                                           ALU.mult, ALU.mult).then_inc(ev_dve, 1)
                    dve.wait_ge(ev_act, EA[i] + 2)
                    V.tensor_tensor(Hl[:, j, :], e, Hh[:, j, :].bitcast(F32), ALU.subtract).then_inc(ev_dve, 1)
                elif kind == "wo":
                    half, q = j // 8, j % 8
                    if q < 7:
                        return
                    if half == 0:
                        dve.wait_ge(z_done, i + 1)
                    dve.wait_ge(xr_in, 32)
                    dve.wait_ge(moe_consts, 16 * N_MOE)
                    for t in range(NTILE):
                        g = NTILE * half + t
                        out = bank((g + 2) % 8)
                        r = rows(t)
                        cols = slice(512 * half, 512 * half + 512)
                        xs = xres[0:r, t, cols]
                        if half:
                            dve.wait_ge(z_done, NBK - 4 + max(t, 1))
                        V.tensor_tensor(xs, xs, out[0:r, :], ALU.add).then_inc(ev_dve, 1)
                        dve.wait_ge(ev_dve, ED[i] + 2 * t + 1)
                        V.tensor_tensor(xn[0:r, t, cols], xs, gffn[0:r, cols], ALU.mult).then_inc(ev_dve, 1)

            def normalise(st, R, NUM, S, out, w):
                step(V.scalar_tensor_tensor(S, M[:, 3, 0:w], 1.0 / DV, R, ALU.mult, ALU.mult))
                V.tensor_tensor(S, S, R, ALU.mult).then_inc(root_in, 1)
                dve.wait_ge(root_out, RN[st] + 1)
                step(V.tensor_tensor(S, S, R, ALU.mult))
                return V.tensor_tensor(out, NUM, S.unsqueeze(1).broadcast_to([128, 2, w]), ALU.mult)

            def side(st):
                kind, what, j = st
                a, d = HA[st], HD[st]
                dve.wait_ge(side_mm, SN[st] + 1)
                if kind == "tr":
                    dst, w = (ktok, 512) if what == "k" else (vtok, D) if what == "v" else (xtok, D)
                    V.tensor_copy(dst[:, 0:NCH, 128 * j:128 * j + 128], M[:, 0, :].rearrange("p (t n) -> p t n", t=NCH))
                    last = V.tensor_copy(dst[0:NS, NCH, 128 * j:128 * j + 128], M[0:NS, 1, 0:128])
                    if hands(st)[0]:
                        last.then_inc(side_dve, 1)
                        dve.wait_ge(side_act, a + 1)
                        g = j // 2
                        root_of(gst, 1.0 / 256)
                        for t in range(NTILE):
                            r = rows(t)
                            s = xtok[0:r, t, 256 * g:256 * g + 256]
                            last = V.scalar_tensor_tensor(s, s, gst[0:r, t:t + 1], gmB[0:r, 256 * g:256 * g + 256],
                                                          ALU.mult, ALU.mult)
                elif kind == "rows":
                    LI, LF, MM, mm, tmp = (rws[:, r, :] for r in range(5))
                    dve.wait_ge(side_act, a + 2)
                    step(V.scalar_tensor_tensor(LF, LF, 0.0, tmp, ALU.min, ALU.subtract))
                    zero = CT[0:H, 0, 0:128]
                    for c in range(NCH):
                        seg = slice(NS + 128 * c, NS + 128 * c + 128)
                        V.tensor_tensor_scan(LF[:, seg], LF[:, seg], zero, 0.0, ALU.add, ALU.add)
                    ls = LF[:, 0:NS].rearrange("p (b t) -> p b t", t=NL)
                    for t in range(1, NL):
                        step(V.tensor_tensor(ls[:, :, t], ls[:, :, t], ls[:, :, t - 1], ALU.add))
                    step(V.tensor_tensor(LI, LI, LF, ALU.subtract))
                    for c in range(NCH):
                        seg = slice(NS + 128 * c, NS + 128 * c + 128)
                        m0 = 0.0 if c == 0 else mm[:, NS + 128 * c - 1:NS + 128 * c]
                        step(V.tensor_tensor_scan(MM[:, seg], LI[:, seg], LI[:, seg], m0, ALU.max, ALU.max))
                        step(V.tensor_tensor(mm[:, seg], MM[:, seg], LF[:, seg], ALU.add))
                    Ms, As = (r[:, 0:NS].rearrange("p (b t) -> p b t", t=NL) for r in (MM, LI))
                    step(V.tensor_tensor(Ms[:, :, 0], As[:, :, 0], m0s, ALU.max))
                    for t in range(1, NL):
                        step(V.tensor_tensor(Ms[:, :, t], As[:, :, t], Ms[:, :, t - 1], ALU.max))
                    V.tensor_tensor(mm[:, 0:NS], MM[:, 0:NS], LF[:, 0:NS], ALU.add)
                    last_m = Ms[:, :, NL - 1:NL].broadcast_to([H, NB, NL])
                    V.tensor_tensor(tmp[:, 0:NS].rearrange("p (b t) -> p b t", t=NL), As, last_m, ALU.subtract)
                    last = V.tensor_tensor(tmp[:, NS:NS + NB], m0s, Ms[:, :, NL - 1], ALU.subtract)
                elif kind == "mix":
                    g = what // 2
                    V.tensor_tensor(mixT[:, what, NS:T].rearrange("p (c n) -> p c n", c=NCH),
                                    M[:, 0, :].rearrange("p (c n) -> p c n", c=NCH),
                                    bsB[:, g, :].unsqueeze(1).broadcast_to([128, NCH, 128]), ALU.add)
                    last = V.tensor_tensor(mixT[:, what, 0:NS].rearrange("p (b t) -> p b t", b=NB),
                                           M[:, 1, 0:NS].rearrange("p (b t) -> p b t", b=NB),
                                           bsB[:, g, 0:NL].unsqueeze(1).broadcast_to([128, NB, NL]), ALU.add)
                elif kind == "s_pre":
                    V.tensor_copy(sm[0:NS, 0:8], M[0:NS, 3, 0:8])
                    V.tensor_copy(sm[:, 16:48], M[:, 3, 16:48])
                    V.tensor_copy(sm[0:NB, 48:52], M[0:NB, 3, 64:68])
                    step(V.tensor_copy(sm[:, 128:160], M[:, 0, 128:160]))
                    for h in range(H):
                        V.tensor_scalar(E[0:NS, 0, NS * h:NS * h + NS], M[0:NS, 0, NS * h:NS * h + NS],
                                        sm[0:NS, h:h + 1], 0.0, ALU.subtract, ALU.max)
                    Mb = M[:, 0, 0:128].rearrange("p (x t) -> p x t", t=NL)
                    V.tensor_tensor(E[:, 0, 128:256].rearrange("p (x t) -> p x t", t=NL),
                                    sm[:, 128:160].unsqueeze(2).broadcast_to([128, H * NB, NL]), Mb, ALU.subtract)
                    V.tensor_tensor(sm[:, 96:128], sm[:, 128:160], Mb[:, :, NL - 1], ALU.subtract) \
                        .then_inc(side_dve, 1)
                    dve.wait_ge(side_act, a + 2)
                    P = E[0:NS, 0, 0:128].rearrange("p (h t) -> p h t", h=H)
                    step(V.tensor_tensor(P, P, btri.unsqueeze(1).broadcast_to([NS, H, NS]), ALU.mult))
                    V.tensor_tensor(E[0:NS, 0, 0:128], E[0:NS, 0, 0:128], M[0:NS, 2, 0:128], ALU.mult)
                    q = E[:, 0, 128:256].rearrange("p (h t) -> p h t", h=H)
                    step(V.tensor_tensor(q, q, qT[:, :, 0:NS], ALU.mult))
                    V.tensor_tensor(E[:, 0, 256:384].rearrange("p (x t) -> p x t", t=NL),
                                    E[:, 0, 128:256].rearrange("p (x t) -> p x t", t=NL),
                                    sm[:, 16:48].unsqueeze(2).broadcast_to([128, H * NB, NL]), ALU.mult)
                    for h in range(H):
                        last = V.tensor_scalar(KWS[:, 128 * h:128 * h + 128], ktok[0:NS, NCH, 128 * h:128 * h + 128],
                                               sm[0:NS, 4 + h:5 + h], None, ALU.mult)
                elif kind == "s_c":
                    dve.wait_ge(side_act, a + 1)
                    if what > 0:
                        i = what - 1
                        h, bh = i // 4, i % 2
                        for b in range(4):
                            s = CIN[i % 3][:, 128 * b:128 * b + 128]
                            x = 96 + NB * h + 4 * bh + b
                            last = V.scalar_tensor_tensor(s, s, sm[:, x:x + 1], M[:, 1, 128 * b:128 * b + 128],
                                                          ALU.mult, ALU.add)
                    if what < 16:
                        h, bh = what // 4, what % 2
                        last = V.tensor_tensor(KWM.rearrange("p (b d) -> p b d", b=4),
                                               KWS[:, 128 * h:128 * h + 128].unsqueeze(1).broadcast_to([NS, 4, 128]),
                                               selb[:, 4 * bh:4 * bh + 4].unsqueeze(2).broadcast_to([NS, 4, 128]),
                                               ALU.mult)
                elif kind == "s_den":
                    R = E[:, 0, 384:512]
                    step(V.tensor_tensor(R, M[:, 3, 0:128], R, ALU.max))
                    step(V.scalar_tensor_tensor(R, M[:, 3, 0:128], -1.0, R, ALU.mult, ALU.max))
                    V.reciprocal(R, R)
                    dve.wait_ge(side_act, a + 1)
                    for h in range(H):
                        x = n0s[:, 128 * h:128 * h + 128]
                        last = V.scalar_tensor_tensor(x, x, sm[0:NB, 48 + h:49 + h], M[0:NB, 1, 128 * h:128 * h + 128],
                                                      ALU.mult, ALU.add)
                elif kind == "s_ss":
                    last = normalise(st, E[:, 0, 384:512], E[:, 6, 0:256].rearrange("p (v x) -> p v x", v=2),
                                     E[:, 1, 0:128], vtok[:, NCH, 0:256].rearrange("p (v x) -> p v x", v=2), 128)
                elif kind == "ml1":
                    step(V.tensor_copy(sm[:, 0:4], M[:, 3, 0:4]))
                    for h in range(H):
                        V.tensor_scalar(E[:, 0, 128 * h:128 * h + 128], M[:, 0, 128 * h:128 * h + 128],
                                        sm[:, h:h + 1], 0.0, ALU.subtract, ALU.max)
                    ML = M[:, 0, 127:512:128]
                    if what == 0:
                        V.memset(sm[:, 12:16], 0.0)
                    else:
                        V.tensor_copy(sm[:, 12:16], sm[:, 52:56])
                    V.tensor_tensor(sm[:, 4:8], sm[:, 0:4], ML, ALU.subtract)
                    m0 = sm[:, 56:60] if what == 0 else sm[:, 52:56]
                    V.tensor_tensor(sm[:, 8:12], m0, ML, ALU.subtract).then_inc(side_dve, 1)
                    dve.wait_ge(side_act, a + 1)
                    P = E[:, 0, :].rearrange("p (h t) -> p h t", h=H)
                    step(V.tensor_tensor(P, P, tri.unsqueeze(1).broadcast_to([128, H, 128]), ALU.mult))
                    V.tensor_tensor(E[:, 0, :], E[:, 0, :], M[:, 2, :], ALU.mult)
                    for h in range(H):
                        V.tensor_scalar(E[:, 5, 128 * h:128 * h + 128], ktok[:, what, 128 * h:128 * h + 128],
                                        sm[:, 4 + h:5 + h], None, ALU.mult)
                    dve.wait_ge(side_act, a + 2)
                    seg = slice(NS + 128 * what, NS + 128 * what + 128)
                    V.tensor_copy(sm[:, 52:56], M[:, 1, 127:512:128])
                    q = E[:, 1, :].rearrange("p (h t) -> p h t", h=H)
                    step(V.tensor_tensor(q, q, qT[:, :, seg], ALU.mult))
                    for h in range(H):
                        last = V.tensor_scalar(E[:, 2, 128 * h:128 * h + 128], E[:, 1, 128 * h:128 * h + 128],
                                               nT[:, h:h + 1], None, ALU.mult)
                elif kind == "ml2":
                    R = E[:, 4, :]
                    step(V.tensor_tensor(R, M[:, 2, :], R, ALU.max))
                    step(V.scalar_tensor_tensor(R, M[:, 2, :], -1.0, R, ALU.mult, ALU.max))
                    dve.wait_ge(side_act, a + 1)
                    last = V.reciprocal(R, R)
                elif kind == "ml3":
                    for h in range(H):
                        V.scalar_tensor_tensor(CT[:, h, :], CT[:, h, :], sm[:, 8 + h:9 + h],
                                               M[:, h // 2, 256 * (h % 2):256 * (h % 2) + 256], ALU.mult, ALU.add)
                    step(V.tensor_tensor(nT, nT, sm[:, 8:12], ALU.mult))
                    V.tensor_tensor(nT, nT, M[:, 2, 0:H], ALU.add)
                    last = normalise(st, E[:, 4, :], E[:, 2:4, :], E[:, 0, :],
                                     vtok[:, what, :].rearrange("p (v x) -> p v x", v=2), 512)
                else:
                    last = V.tensor_copy(E[:, what, :], M[:, 0, :])
                    if what == 1:
                        last = V.tensor_copy(E[0:H, 2, 0:128], M[0:H, 1, 0:128])
                last.then_inc(side_end, 1)
                dve.wait_ge(side_end, SN[st] + 1)

            for i in range(NBK):
                for m in splits_before(i):
                    split(m)
                if i in (1, 2):
                    position_weights(i - 1)
                for s in SIDE[i]:
                    side(s)
                evacuate(i)

            dve.wait_ge(moe_consts, 16 * N_MOE)
            dve.wait_ge(moe_made, 1)
            step(V.memset(Lg, 0.0))
            dve.wait_ge(n_ss, 2 * NTILE)
            step(V.tensor_tensor(nst[:, 0, :], nst[:, 0, :], nst[:, 1, :], ALU.add))
            root_of(nst[:, 0, :], 1.0 / D, n_rstd)
            nw = NG + NE
            for half in range(2):
                for t in range(NTILE):
                    r = rows(t)
                    dve.wait_ge(n_log, NTILE * (half + 1))
                    L = Lg[0:r, t, :]
                    last = V.scalar_tensor_tensor(L, M[0:r, 2 + half, nw * t:nw * t + nw], nst[0:r, 0, t:t + 1],
                                                  L if half else rb[0:r, :], ALU.mult, ALU.add)
                step(last)
            G = Lg[:, :, 0:NG]
            fine = Lg[:, :, NG:nw].rearrange("p t (g e) -> p t g e", g=NG)

            cur_rt = [32]

            def tmp(*shape):
                m = int(np.prod(shape))
                o = cur_rt[0]
                cur_rt[0] += m
                assert cur_rt[0] <= 512
                ap = rt[:, o:o + m]
                if len(shape) == 2:
                    ap = ap.rearrange("p (a b) -> p a b", a=shape[0])
                return ap

            def spread(x, m):
                return x.unsqueeze(2).broadcast_to([128, x.shape[1], m])

            def first_max(x, m, mx, hot, work):
                step(V.tensor_reduce(mx, x, AX, ALU.max))
                step(V.tensor_tensor(work, x, spread(mx, m), ALU.is_ge))
                step(V.tensor_tensor(work, work, w8[:, NPG - m:NPG].unsqueeze(1).broadcast_to([128, NTILE, m]), ALU.mult))
                best = tmp(NTILE)
                step(V.tensor_reduce(best, work, AX, ALU.max))
                step(V.tensor_tensor(hot, work, spread(best, m), ALU.is_equal))

            gm, m1, m2 = tmp(NTILE), tmp(NTILE), tmp(NTILE)
            ohg, gwork = tmp(NTILE, NG), tmp(NTILE, NG)
            first_max(G, NG, gm, ohg, gwork)
            V.tensor_tensor(rt[:, 0:20].rearrange("p (t g) -> p t g", g=NG), G, spread(gm, NG), ALU.subtract)
            step(V.tensor_tensor(F4, fine, ohg.unsqueeze(3).broadcast_to([128, NTILE, NG, NPG]), ALU.mult))
            fs, oh1, oh2, fwork = tmp(NTILE, NPG), tmp(NTILE, NPG), tmp(NTILE, NPG), tmp(NTILE, NPG)
            step(V.tensor_tensor(fs, F4[:, :, 0, :], F4[:, :, 1, :], ALU.add))
            for g in range(2, NG):
                step(V.tensor_tensor(fs, fs, F4[:, :, g, :], ALU.add))
            first_max(fs, NPG, m1, oh1, fwork)
            step(V.scalar_tensor_tensor(fs, oh1, -BIG, fs, ALU.mult, ALU.add))
            first_max(fs, NPG, m2, oh2, fwork)
            V.tensor_tensor(rt[:, 20:25], m2, m1, ALU.subtract).then_inc(r_exp_in, 1)
            for j, hot in enumerate((oh1, oh2)):
                last = V.tensor_tensor(OH[:, j].rearrange("p t (g e) -> p t g e", g=NG),
                                       ohg.unsqueeze(3).broadcast_to([128, NTILE, NG, NPG]),
                                       hot.unsqueeze(2).broadcast_to([128, NTILE, NG, NPG]), ALU.mult)
            step(last)
            step(V.tensor_tensor(W1, OH[:, 0], OH[:, 1], ALU.add))
            step(V.tensor_copy(CW[:, 0, :], W1[:, 0, :]))
            for t in range(1, NCH):
                last = V.tensor_tensor(CW[:, t, :], CW[:, t - 1, :], W1[:, t, :], ALU.add)
                if t < NCH - 1:
                    step(last)
            last.then_inc(r_oh, 1)
            n10 = 2 * NTILE
            full = [128, 2, NTILE, NE]
            rank, base, ex, kb, hit = tmp(n10), tmp(n10), tmp(n10), tmp(n10), tmp(n10)

            def pick(out, x):
                step(V.tensor_tensor(OT, OH, x, ALU.mult))
                step(V.tensor_reduce(out.rearrange("p (j t) -> p j t", j=2), OT, AX, ALU.add))

            pick(ex, io64[:, 0:NE].unsqueeze(1).unsqueeze(1).broadcast_to(full))
            dve.wait_ge(r_exp_out, 1)
            se = tmp(NTILE)
            step(V.tensor_reduce(se, rt[:, 0:20].rearrange("p (t g) -> p t g", g=NG), AX, ALU.add))
            step(V.scalar_tensor_tensor(GT[:, 0, :], rt[:, 20:25], 1.0, se, ALU.add, ALU.mult))
            step(V.reciprocal(GT[:, 0, :], GT[:, 0, :]))
            V.tensor_tensor(GT[:, 1, :], GT[:, 0, :], rt[:, 20:25], ALU.mult)
            dve.wait_ge(r_rank, 1)
            RK = M[:, 1, 0:(NTILE + 1) * NE].rearrange("p (t e) -> p t e", e=NE)
            cn = RK[:, NTILE, :]
            nb, S, zero = tmp(NE), tmp(NE), tmp(NE)
            V.memset(zero, 0.0)
            step(V.tensor_tensor(HT, cn.unsqueeze(2).broadcast_to([128, NE, MAXK]),
                                 caps.unsqueeze(1).broadcast_to([128, NE, MAXK]), ALU.is_gt))
            step(V.tensor_reduce(nb, HT, AX, ALU.add))
            step(V.tensor_tensor_scan(S, nb, zero, 0.0, ALU.add, ALU.add))
            step(V.tensor_tensor(nb, S, nb, ALU.subtract))

            pick(rank, RK[:, 0:NTILE, :].unsqueeze(1).broadcast_to(full))
            pick(base, nb.unsqueeze(1).unsqueeze(1).broadcast_to(full))
            step(V.tensor_tensor(HT[:, 0:n10, :], spread(rank, MAXK), caps.unsqueeze(1).broadcast_to([128, n10, MAXK]),
                                 ALU.is_ge))
            V.tensor_copy(hit, HT[:, 0:n10, 0])
            step(V.tensor_reduce(kb, HT[:, 0:n10, :], AX, ALU.add))
            step(V.tensor_tensor(base, base, kb, ALU.add))
            step(V.tensor_tensor(base, base, ex, ALU.subtract))
            step(V.scalar_tensor_tensor(base, base, float(NE - 1), hit, ALU.add, ALU.mult))
            step(V.tensor_tensor(base, base, ex, ALU.add))
            step(V.scalar_tensor_tensor(rank, kb, float(-CAP), rank, ALU.mult, ALU.add))
            step(V.scalar_tensor_tensor(ex, base, float(CAP), rank, ALU.mult, ALU.add))
            V.tensor_copy(slots, ex)
            V.tensor_tensor(Aoh, io64.unsqueeze(1).broadcast_to([128, n10, CAP]), spread(rank, CAP), ALU.is_equal)
            step(V.tensor_tensor(Boh, io64[:, 0:NBLK].unsqueeze(1).broadcast_to([128, n10, NBLK]), spread(base, NBLK),
                                 ALU.is_equal))
            for j in range(2):
                last = V.tensor_tensor(Boh[:, NTILE * j:NTILE * j + NTILE, :], Boh[:, NTILE * j:NTILE * j + NTILE, :],
                                       spread(tok1, NBLK), ALU.mult)
            last.then_inc(r_ab, 1)
            step(V.tensor_tensor(CO, S[0:1].unsqueeze(1).broadcast_to([1, NOV, NE]),
                                 io64[0:1, 0:NOV].unsqueeze(2).broadcast_to([1, NOV, NE]), ALU.is_le))
            own = tmp(NOV)
            step(V.tensor_reduce(own[0:1], CO, AX, ALU.add))
            V.tensor_scalar(ctl[:, 0:NOV], own[0:1], float(NE - 1), None, ALU.min)
            V.tensor_copy(ctl[:, NOV:NOV + 1], S[0:1, NE - 1:NE])
            dve.wait_ge(r_idx, 1)
            step(V.tensor_scalar(VI, M[0:CAP, 2, 0:NBLK], 0.0, float(4 * T), ALU.is_equal, ALU.mult))
            step(V.scalar_tensor_tensor(VI, M[0:CAP, 2, 0:NBLK], -1.0, VI, ALU.add, ALU.add))
            step(V.tensor_copy(idx, VI))
            V.tensor_copy(rt[0:1, 0:1], rt[0:1, 0:1]).then_inc(routed, 1)

            def tokens(k):
                return V.tensor_copy(xT[k], bank_xt().rearrange("p (c n) -> p c n", c=KC))

            def gated(k):
                return V.tensor_tensor(hid[k], sil[k], bank_up(k)[:, EH:2 * EH], ALU.mult)

            def rests_of(b, w):
                for j in range(2):
                    dve.wait_ge(dnh_ready, b * 2 + (j + 1))
                    last = V.tensor_tensor(dnl[:, j, :], w[:, j, :], dnh[:, j, :].bitcast(F32), ALU.subtract)
                last.then_inc(dnl_ready, 1)
                dve.wait_ge(hth_ready, b + 1)
                V.tensor_tensor(hTl[:, :, 0:CAP], bank_h().rearrange("p (j n) -> p j n", j=2),
                                hTh[:, :, 0:CAP].bitcast(F32), ALU.subtract).then_inc(h_ready, 1)

            def tokens_of(b, k):
                dve.wait_ge(xt_done, b + 1)
                if not (isinstance(b, int) and b < 2):
                    dve.wait_ge(up_done, b - 1)
                tokens(k).then_inc(xt_ready, 1)

            def hidden_of(b, r):
                dve.wait_ge(sil_ready, b + 1)
                gated(r % 2).then_inc(hid_ready, 1)
                rests_of(b, edn[r])

            tokens_of(0, 0)
            for b in range(RING):
                tokens_of(b + 1, (b + 1) % 2)
                hidden_of(b, b)
            with dve.Fori(1, NE // RING - 1) as i:
                for r in range(RING):
                    tokens_of(i * RING + (r + 1), (r + 1) % 2)
                    hidden_of(i * RING + r, r)
            for b in range(NE - RING, NE):
                if b + 1 < NE:
                    tokens_of(b + 1, (b + 1) % 2)
                hidden_of(b, b % RING)
            n_ov = dve.value_load(ctl[0:1, NOV:NOV + 1], min_val=0, max_val=NOV)
            with dve.If(n_ov > 0):
                with dve.Fori(0, n_ov) as o:
                    dve.wait_ge(xt_done, o + (NE + 1))
                    dve.wait_ge(up_done, o + NE)
                    tokens(0).then_inc(xt_ready, 1)
                    dve.wait_ge(sil_ready, o + (NE + 1))
                    gated(0).then_inc(hid_ready, 1)
                    rests_of(o + NE, edn[0])

            dve.wait_ge(gfin_in, 16)
            for tiles in (range(0, 3), range(3, NTILE)):
                for t in tiles:
                    r = rows(t)
                    x = xres[0:r, t, :]
                    dve.wait_ge(yg_in[t], 32)
                    step(V.scalar_tensor_tensor(x, yg[0:r, t, :], GT[0:r, 0, t:t + 1], x, ALU.mult, ALU.add))
                    V.scalar_tensor_tensor(x, yg[0:r, NTILE + t, :], GT[0:r, 1, t:t + 1], x, ALU.mult, ALU.add) \
                        .then_inc(f_sum, 1)
                dve.wait_ge(f_ss, tiles[-1] + 1)
                root_of(nst[:, 1, tiles[0]:tiles[-1] + 1], 1.0 / D)
                for t in tiles:
                    r = rows(t)
                    V.scalar_tensor_tensor(yg[0:r, t, :], xres[0:r, t, :], nst[0:r, 1, t:t + 1], gfin[0:r, :],
                                           ALU.mult, ALU.mult).then_inc(f_out, 1)


_INS = ["x_prompt", "x_sample", "state_mlstm_C", "state_mlstm_n", "state_mlstm_m", "norm_mix_g", "w_in", "ml_b_i",
        "ml_b_f", "ml_norm_g", "gm_norm_g", "gm_ws", "gm_bs", "p_a", "p_b", "w_out", "norm_ffn_g", "rc_w", "rc_b",
        "rf_w", "rf_b", "e_wg", "e_wu", "e_wd", "final_norm_g"]
_OUTS = [(1, NP_TOK, D), (NB, NL, D), (1, 1, H, DV, DQK), (1, 1, H, DQK), (1, 1, H), (1, NB, H, DV, DQK),
         (1, NB, H, DQK), (1, NB, H), (1, NB, NL, 4, 256)]


def kernel(**inputs):
    import concourse.bacc as bacc
    from concourse.bass_utils import run_bass_kernel_spmd

    nc = bacc.Bacc("TRN2", target_bir_lowering=False, num_devices=1)
    arrays, args = {}, []
    for name in _INS:
        a = np.ascontiguousarray(inputs[name])
        arrays[f"in_{name}"] = a
        args.append(nc.dram_tensor(f"in_{name}", a.shape, mybir.dt.from_np(a.dtype), kind="ExternalInput").ap())
    for i, shape in enumerate(_OUTS):
        args.append(nc.dram_tensor(f"out_{i}", shape, F32, kind="ExternalOutput").ap())
    build(nc, *args)
    r = run_bass_kernel_spmd(nc, [arrays], core_ids=[0])
    return tuple(r.results[0][f"out_{i}"] for i in range(len(_OUTS)))
```
